# Optimizing a Trainium2 kernel written in Bass

```python
import math
import jax, jax.numpy as jnp
from jax import lax
import numpy as np
import jax
import jax.numpy as jnp

D_MODEL = 1024
BATCH = 1
SEQ = 256
DEPTH = 2

N_BRANCH = 4
BRANCH_W = 256
GM_GROUPS = 4
GM_CHUNK = 128
GM_GD = BRANCH_W // GM_GROUPS
POOL_WINDOWS = (2, 4, 8, 16)
POOL_GD = BRANCH_W // len(POOL_WINDOWS)
ATT_HEADS = 4
ATT_HD = BRANCH_W // ATT_HEADS
IDX_HEADS = 4
IDX_HD = 32
TOPK_MAX = 256
Q_BLOCK = 128
REL_BUCKETS = 32
REL_MAX_DIST = 128
CONV_K = 31
D_FF = 2816
EPS = 1e-6

IN_SIZES = (2 * BRANCH_W, BRANCH_W, BRANCH_W, BRANCH_W, BRANCH_W, IDX_HEADS * IDX_HD, IDX_HD, IDX_HEADS, 2 * BRANCH_W, N_BRANCH * D_MODEL)
IN_COLS = 2 * BRANCH_W + 4 * BRANCH_W + IDX_HEADS * IDX_HD + IDX_HD + IDX_HEADS + 2 * BRANCH_W + N_BRANCH * D_MODEL


def rmsnorm(x, g):
    xf = x.astype(jnp.float32)
    y = xf * lax.rsqrt(jnp.mean(xf * xf, axis=-1, keepdims=True) + EPS)
    return (y * g.astype(jnp.float32)).astype(x.dtype)

def layernorm(x, g, b):
    xf = x.astype(jnp.float32)
    mu = jnp.mean(xf, axis=-1, keepdims=True)
    xc = xf - mu
    y = xc * lax.rsqrt(jnp.mean(xc * xc, axis=-1, keepdims=True) + EPS)
    return (y * g.astype(jnp.float32) + b.astype(jnp.float32)).astype(x.dtype)

def swiglu_ffn(h, w_gu, w_down):
    a, b = jnp.split(h @ w_gu, 2, axis=-1)
    return (jax.nn.silu(a) * b) @ w_down

def gmlp_mixer(uv, v_g, ws, wb):
    B, S, _ = uv.shape
    u, v = jnp.split(jax.nn.gelu(uv), 2, axis=-1)
    v = rmsnorm(v, v_g)
    vc = v.reshape(B, S // GM_CHUNK, GM_CHUNK, GM_GROUPS, GM_GD)
    causal = jnp.tril(jnp.ones((GM_CHUNK, GM_CHUNK), dtype=bool))
    wsm = jnp.where(causal[None], ws, 0.0).astype(v.dtype)
    mixed = jnp.einsum('gts,bcsgd->bctgd', wsm, vc) + wb.T[None, None, :, :, None]
    return u * mixed.reshape(B, S, BRANCH_W)

def pool_mixer(p, pw, scale):
    B, S, _ = p.shape
    wmax = POOL_WINDOWS[-1]
    pf = p.astype(jnp.float32)
    csp = jnp.pad(jnp.cumsum(pf, axis=1), ((0, 0), (wmax, 0), (0, 0)))
    count = jnp.arange(1, S + 1, dtype=jnp.float32)[:, None]
    outs = []
    for g, w in enumerate(POOL_WINDOWS):
        sl = slice(g * POOL_GD, (g + 1) * POOL_GD)
        win = csp[:, wmax:, sl] - csp[:, wmax - w:wmax - w + S, sl]
        outs.append(win / jnp.minimum(count, float(w)) - pf[:, :, sl])
    d = jnp.stack(outs, axis=2).astype(p.dtype)
    y = jnp.einsum('bsgc,gcd->bsgd', d, pw).reshape(B, S, BRANCH_W)
    return y * scale

def conv_mixer(ab, dw, db, ln_g, ln_b):
    a, gt = jnp.split(ab, 2, axis=-1)
    h = a * jax.nn.sigmoid(gt)
    h = lax.conv_general_dilated(h, dw[:, None, :].astype(h.dtype), window_strides=(1,),
                                 padding=[(CONV_K - 1, 0)], dimension_numbers=('NWC', 'WIO', 'NWC'),
                                 feature_group_count=BRANCH_W) + db
    return jax.nn.silu(layernorm(h, ln_g, ln_b))

def t5_bucket(n):
    n = jnp.maximum(n, 0)
    max_exact = REL_BUCKETS // 2
    large = max_exact + (jnp.log(jnp.maximum(n, 1).astype(jnp.float32) / max_exact)
                         / math.log(REL_MAX_DIST / max_exact) * (REL_BUCKETS - max_exact)).astype(jnp.int32)
    return jnp.where(n < max_exact, n, jnp.minimum(large, REL_BUCKETS - 1))

def sparse_attention(q, k, v, q_idx, k_idx, w_idx, rel_bias):
    B, S, _ = q.shape
    topk = min(TOPK_MAX, S // 4)
    q = q.reshape(B, S, ATT_HEADS, ATT_HD)
    k = k.reshape(B, S, ATT_HEADS, ATT_HD)
    v = v.reshape(B, S, ATT_HEADS, ATT_HD)
    q_idx = q_idx.reshape(B, S, IDX_HEADS, IDX_HD)
    w_idx = w_idx.astype(jnp.float32) * (IDX_HEADS ** -0.5)
    s_pos = jnp.arange(S)
    gather = jax.vmap(lambda a, i: a[i])

    def block(i):
        t0 = i * Q_BLOCK
        t_pos = t0 + jnp.arange(Q_BLOCK)
        qb = lax.dynamic_slice_in_dim(q, t0, Q_BLOCK, axis=1)
        qib = lax.dynamic_slice_in_dim(q_idx, t0, Q_BLOCK, axis=1)
        wib = lax.dynamic_slice_in_dim(w_idx, t0, Q_BLOCK, axis=1)
        rel = jax.nn.relu(jnp.einsum('bqhd,bsd->bqhs', qib, k_idx).astype(jnp.float32) * (IDX_HD ** -0.5))
        score = jnp.einsum('bqh,bqhs->bqs', wib, rel)
        score = jnp.where(s_pos[None, None, :] <= t_pos[None, :, None], score, -jnp.inf)
        _, idx = lax.top_k(score, topk)
        valid = idx <= t_pos[None, :, None]
        ks = gather(k, idx)
        vs = gather(v, idx)
        bias = rel_bias[t5_bucket(t_pos[None, :, None] - idx)]
        logits = (jnp.einsum('bqhd,bqkhd->bqhk', qb, ks).astype(jnp.float32) * (ATT_HD ** -0.5)
                  + bias.astype(jnp.float32).transpose(0, 1, 3, 2))
        logits = jnp.where(valid[:, :, None, :], logits, -jnp.inf)
        p = jax.nn.softmax(logits, axis=-1).astype(v.dtype)
        o = jnp.einsum('bqhk,bqkhd->bqhd', p, vs)
        return o.reshape(B, Q_BLOCK, BRANCH_W)

    out = lax.map(block, jnp.arange(S // Q_BLOCK))
    return out.transpose(1, 0, 2, 3).reshape(B, S, BRANCH_W)

def mixing_sublayer(h, w_in, gm_v_g, gm_ws, gm_b, pool_w, pool_scale, conv_dw, conv_b,
                    conv_ln_g, conv_ln_b, w_branch, w_out, rel_bias):
    B, S, _ = h.shape
    z = h @ w_in
    uv, pz, qz, kz, vz, qi, ki, wi, cz, gz = jnp.split(z, list(np.cumsum(IN_SIZES)[:-1]), axis=-1)
    branches = (
        gmlp_mixer(uv, gm_v_g, gm_ws, gm_b),
        pool_mixer(pz, pool_w, pool_scale),
        sparse_attention(qz, kz, vz, qi, ki, wi, rel_bias),
        conv_mixer(cz, conv_dw, conv_b, conv_ln_g, conv_ln_b),
    )
    gates = jax.nn.sigmoid(gz.reshape(B, S, N_BRANCH, D_MODEL))
    y = gates[:, :, 0] * (branches[0] @ w_branch[0])
    for n in range(1, N_BRANCH):
        y = y + gates[:, :, n] * (branches[n] @ w_branch[n])
    return y @ w_out

def first_inputs(seed: int = 0) -> dict:
    key = jax.random.key(seed)
    ks = jax.random.split(key, 24)
    f32 = jnp.float32

    def nrm(k, shape, scale):
        return jax.random.normal(k, shape, f32) * scale

    def gain(k, shape):
        return 1.0 + 0.05 * jax.random.normal(k, shape, f32)

    L, D, C, F = DEPTH, D_MODEL, BRANCH_W, D_FF
    return {
        'x': nrm(ks[0], (BATCH, SEQ, D), 1.0),
        'ffn1_pre_g': gain(ks[1], (L, D)),
        'ffn1_post_g': gain(ks[2], (L, D)),
        'ffn1_w_gu': nrm(ks[3], (L, D, 2 * F), D ** -0.5),
        'ffn1_w_down': nrm(ks[4], (L, F, D), F ** -0.5),
        'mix_pre_g': gain(ks[5], (L, D)),
        'mix_post_g': gain(ks[6], (L, D)),
        'w_in': nrm(ks[7], (L, D, IN_COLS), D ** -0.5),
        'gm_v_g': gain(ks[8], (L, C)),
        'gm_ws': nrm(ks[9], (L, GM_GROUPS, GM_CHUNK, GM_CHUNK), GM_CHUNK ** -0.5),
        'gm_b': 1.0 + 0.1 * jax.random.normal(ks[10], (L, GM_GROUPS, GM_CHUNK), f32),
        'pool_w': nrm(ks[11], (L, len(POOL_WINDOWS), POOL_GD, POOL_GD), POOL_GD ** -0.5),
        'pool_scale': gain(ks[12], (L, C)),
        'conv_dw': nrm(ks[13], (L, CONV_K, C), CONV_K ** -0.5),
        'conv_b': nrm(ks[14], (L, C), 0.02),
        'conv_ln_g': gain(ks[15], (L, C)),
        'conv_ln_b': nrm(ks[16], (L, C), 0.02),
        'w_branch': nrm(ks[17], (L, N_BRANCH, C, D), C ** -0.5),
        'w_out': nrm(ks[18], (L, D, D), D ** -0.5),
        'ffn2_pre_g': gain(ks[19], (L, D)),
        'ffn2_post_g': gain(ks[20], (L, D)),
        'ffn2_w_gu': nrm(ks[21], (L, D, 2 * F), D ** -0.5),
        'ffn2_w_down': nrm(ks[22], (L, F, D), F ** -0.5),
        'rel_bias': nrm(ks[23], (REL_BUCKETS, ATT_HEADS), 0.5),
    }

def first_block(x, ffn1_pre_g, ffn1_post_g, ffn1_w_gu, ffn1_w_down, mix_pre_g, mix_post_g, w_in,
              gm_v_g, gm_ws, gm_b, pool_w, pool_scale, conv_dw, conv_b, conv_ln_g, conv_ln_b,
              w_branch, w_out, ffn2_pre_g, ffn2_post_g, ffn2_w_gu, ffn2_w_down, rel_bias):
    for l in range(DEPTH):
        h = swiglu_ffn(rmsnorm(x, ffn1_pre_g[l]), ffn1_w_gu[l], ffn1_w_down[l])
        x = x + 0.5 * rmsnorm(h, ffn1_post_g[l])
        h = mixing_sublayer(rmsnorm(x, mix_pre_g[l]), w_in[l], gm_v_g[l], gm_ws[l], gm_b[l],
                            pool_w[l], pool_scale[l], conv_dw[l], conv_b[l], conv_ln_g[l],
                            conv_ln_b[l], w_branch[l], w_out[l], rel_bias)
        x = x + rmsnorm(h, mix_post_g[l])
        h = swiglu_ffn(rmsnorm(x, ffn2_pre_g[l]), ffn2_w_gu[l], ffn2_w_down[l])
        x = x + 0.5 * rmsnorm(h, ffn2_post_g[l])
    return x


HEAD_DIM = 64
ROPE_DIM = HEAD_DIM // 4
ROPE_THETA = 500000.0
NEG_INF = -1e30
RMS_EPS = 1e-6

NSA_HEADS = 4
NSA_CMP_LEN = 32
NSA_CMP_STRIDE = 16
NSA_CMP_HIDDEN = 128
NSA_SEL_LEN = 64
NSA_SEL_TOPK = 16
NSA_WINDOW = 512
NSA_FORCE_SCORE = 1e4

DIL_PATTERNS = ((128, 1), (512, 4), (2048, 16))
DIL_HEADS_PER_GROUP = 2
DIL_HEADS = DIL_HEADS_PER_GROUP * len(DIL_PATTERNS)

FOX_HEADS = 6


NSA_Q_W = NSA_HEADS * HEAD_DIM
NSA_KV_W = 6 * HEAD_DIM
NSA_GATE_W = 3 * NSA_HEADS
DIL_W = DIL_HEADS * HEAD_DIM
DIL_OUT_W = DIL_HEADS_PER_GROUP * HEAD_DIM
FOX_W = FOX_HEADS * HEAD_DIM
IN_WIDTHS = (NSA_Q_W, NSA_KV_W, NSA_GATE_W, 3 * DIL_W, 3 * FOX_W, FOX_HEADS, 3 * D_MODEL)
IN_COLS_2 = sum(IN_WIDTHS)


def _split_cols(x, widths):
    offsets = [int(o) for o in np.cumsum(widths)[:-1]]
    return jnp.split(x, offsets, axis=-1)

def _rms_norm(x, g):
    xf = x.astype(jnp.float32)
    y = xf * lax.rsqrt(jnp.mean(xf * xf, axis=-1, keepdims=True) + RMS_EPS)
    return (y * g.astype(jnp.float32)).astype(x.dtype)

def _modulate(x, shift, scale):
    return x * (1.0 + scale) + shift

def _swiglu(x, w_in, w_out):
    gate, up = jnp.split(x @ w_in, 2, axis=-1)
    return (jax.nn.silu(gate) * up) @ w_out

def _rope_tables(seq_len):
    inv_freq = ROPE_THETA ** (-jnp.arange(0, ROPE_DIM, 2, dtype=jnp.float32) / ROPE_DIM)
    ang = jnp.arange(seq_len, dtype=jnp.float32)[:, None] * inv_freq[None, :]
    return jnp.cos(ang), jnp.sin(ang)

def _partial_rope(x, cos, sin):
    half = ROPE_DIM // 2
    c = cos[None, :, None, :]
    s = sin[None, :, None, :]
    x1 = x[..., :half].astype(jnp.float32)
    x2 = x[..., half:ROPE_DIM].astype(jnp.float32)
    rot = jnp.concatenate([x1 * c - x2 * s, x2 * c + x1 * s], axis=-1).astype(x.dtype)
    return jnp.concatenate([rot, x[..., ROPE_DIM:]], axis=-1)

def _masked_softmax(s, mask):
    s = jnp.where(mask, s, NEG_INF)
    m = jnp.max(s, axis=-1, keepdims=True)
    e = jnp.where(mask, jnp.exp(s - m), 0.0)
    den = jnp.sum(e, axis=-1, keepdims=True)
    den = jnp.where(den > 0, den, 1.0)
    return e / den, m + jnp.log(den)

def _nsa_attention(q, k_cmp, v_cmp, k_sel, v_sel, k_win, v_win, gate_logits,
                   cmp_pe, cmp_w1, cmp_w2):
    B, S = q.shape[0], q.shape[1]
    scale = HEAD_DIM ** -0.5
    n_cmp = (S - NSA_CMP_LEN) // NSA_CMP_STRIDE + 1
    cmp_start = np.arange(n_cmp) * NSA_CMP_STRIDE
    cmp_idx = cmp_start[:, None] + np.arange(NSA_CMP_LEN)[None, :]

    def compress(t, j):
        blk = t[:, cmp_idx] + cmp_pe[j]
        hid = jax.nn.silu(blk.reshape(B, n_cmp, NSA_CMP_LEN * HEAD_DIM) @ cmp_w1[j])
        return hid @ cmp_w2[j]

    kc = compress(k_cmp, 0)
    vc = compress(v_cmp, 1)
    cmp_end = jnp.asarray(cmp_start + NSA_CMP_LEN - 1)
    n_sel = S // NSA_SEL_LEN
    sel_start = np.arange(n_sel) * NSA_SEL_LEN
    ov = np.minimum(cmp_start[:, None] + NSA_CMP_LEN, sel_start[None, :] + NSA_SEL_LEN) \
        - np.maximum(cmp_start[:, None], sel_start[None, :])
    overlap = jnp.asarray(np.clip(ov, 0, None) / NSA_CMP_LEN, dtype=jnp.float32)
    top_k = min(NSA_SEL_TOPK, n_sel)
    sel_ids = jnp.arange(n_sel)
    kw_pad = jnp.pad(k_win, ((0, 0), (NSA_WINDOW, 0), (0, 0)))
    vw_pad = jnp.pad(v_win, ((0, 0), (NSA_WINDOW, 0), (0, 0)))
    win_len = NSA_WINDOW + Q_BLOCK
    gather = jax.vmap(lambda a, i: a[i])

    def block(qb):
        q0 = qb * Q_BLOCK
        t = q0 + jnp.arange(Q_BLOCK)
        qblk = lax.dynamic_slice_in_dim(q, q0, Q_BLOCK, axis=1)
        s = jnp.einsum('bqhd,bnd->bhqn', qblk, kc).astype(jnp.float32) * scale
        p_cmp, _ = _masked_softmax(s, cmp_end[None, :] <= t[:, None])
        o_cmp = jnp.einsum('bhqn,bnd->bqhd', p_cmp.astype(vc.dtype), vc)
        imp = jnp.einsum('bhqn,nj->bqj', p_cmp, overlap)
        valid = (sel_ids[None, :] * NSA_SEL_LEN) <= t[:, None]
        forced = (sel_ids[None, :] == (t // NSA_SEL_LEN)[:, None]) | (sel_ids[None, :] == 0)
        imp = jnp.where(forced, NSA_FORCE_SCORE, jnp.where(valid, imp, -1.0))
        _, blk_idx = lax.top_k(imp, top_k)
        tok = (blk_idx[..., None] * NSA_SEL_LEN + jnp.arange(NSA_SEL_LEN)).reshape(B, Q_BLOCK * top_k * NSA_SEL_LEN)
        ks = gather(k_sel, tok).reshape(B, Q_BLOCK, top_k * NSA_SEL_LEN, HEAD_DIM)
        vs = gather(v_sel, tok).reshape(B, Q_BLOCK, top_k * NSA_SEL_LEN, HEAD_DIM)
        s = jnp.einsum('bqhd,bqkd->bhqk', qblk, ks).astype(jnp.float32) * scale
        smask = (tok.reshape(B, Q_BLOCK, top_k * NSA_SEL_LEN) <= t[None, :, None])[:, None]
        p, _ = _masked_softmax(s, smask)
        o_sel = jnp.einsum('bhqk,bqkd->bqhd', p.astype(vs.dtype), vs)
        kw = lax.dynamic_slice_in_dim(kw_pad, q0, win_len, axis=1)
        vw = lax.dynamic_slice_in_dim(vw_pad, q0, win_len, axis=1)
        kpos = q0 - NSA_WINDOW + jnp.arange(win_len)
        wmask = (kpos[None, :] <= t[:, None]) & (kpos[None, :] > t[:, None] - NSA_WINDOW) & (kpos[None, :] >= 0)
        s = jnp.einsum('bqhd,bkd->bhqk', qblk, kw).astype(jnp.float32) * scale
        p, _ = _masked_softmax(s, wmask)
        o_win = jnp.einsum('bhqk,bkd->bqhd', p.astype(vw.dtype), vw)
        g = jax.nn.sigmoid(lax.dynamic_slice_in_dim(gate_logits, q0, Q_BLOCK, axis=1).astype(jnp.float32)).astype(q.dtype)
        return g[..., 0:1] * o_cmp + g[..., 1:2] * o_sel + g[..., 2:3] * o_win

    out = lax.map(block, jnp.arange(S // Q_BLOCK))
    return out.transpose(1, 0, 2, 3, 4).reshape(B, S, NSA_Q_W)

def _dilated_attention(q, k, v):
    B, S = q.shape[0], q.shape[1]
    scale = HEAD_DIM ** -0.5
    hpg = DIL_HEADS_PER_GROUP
    qg_all = [q[:, :, g * hpg:(g + 1) * hpg] for g in range(len(DIL_PATTERNS))]
    kg_all = [k[:, :, g * hpg:(g + 1) * hpg] for g in range(len(DIL_PATTERNS))]
    vg_all = [v[:, :, g * hpg:(g + 1) * hpg] for g in range(len(DIL_PATTERNS))]

    def block(qb):
        q0 = qb * Q_BLOCK
        t = q0 + jnp.arange(Q_BLOCK)
        outs, lses = [], []
        for g, (window, dil) in enumerate(DIL_PATTERNS):
            qg = lax.dynamic_slice_in_dim(qg_all[g], q0, Q_BLOCK, axis=1)
            pos = t[:, None] - dil * jnp.arange(window // dil + 1)[None, :]
            valid = pos >= 0
            idx = jnp.maximum(pos, 0)
            kk = kg_all[g][:, idx]
            vv = vg_all[g][:, idx]
            s = jnp.einsum('bqhd,bqkhd->bhqk', qg, kk).astype(jnp.float32) * scale
            p, lse = _masked_softmax(s, valid)
            outs.append(jnp.einsum('bhqk,bqkhd->bqhd', p.astype(vv.dtype), vv))
            lses.append(lse[..., 0])
        wts = jax.nn.softmax(jnp.stack(lses, axis=0), axis=0)
        wts = wts.transpose(0, 1, 3, 2)[..., None].astype(q.dtype)
        return jnp.sum(wts * jnp.stack(outs, axis=0), axis=0)

    out = lax.map(block, jnp.arange(S // Q_BLOCK))
    return out.transpose(1, 0, 2, 3, 4).reshape(B, S, DIL_OUT_W)

def _forgetting_attention(q, k, v, f_logit, f_bias):
    B, S = q.shape[0], q.shape[1]
    scale = HEAD_DIM ** -0.5
    log_f = jax.nn.log_sigmoid(f_logit.astype(jnp.float32) + f_bias.astype(jnp.float32))
    cum = jnp.cumsum(log_f, axis=1)
    cum_k = cum.transpose(0, 2, 1)[:, :, None, :]
    kpos = jnp.arange(S)

    def block(qb):
        q0 = qb * Q_BLOCK
        t = q0 + jnp.arange(Q_BLOCK)
        qblk = lax.dynamic_slice_in_dim(q, q0, Q_BLOCK, axis=1)
        cq = lax.dynamic_slice_in_dim(cum, q0, Q_BLOCK, axis=1).transpose(0, 2, 1)[..., None]
        s = jnp.einsum('bqhd,bkhd->bhqk', qblk, k).astype(jnp.float32) * scale + (cq - cum_k)
        p, _ = _masked_softmax(s, kpos[None, :] <= t[:, None])
        return jnp.einsum('bhqk,bkhd->bqhd', p.astype(v.dtype), v)

    out = lax.map(block, jnp.arange(S // Q_BLOCK))
    return out.transpose(1, 0, 2, 3, 4).reshape(B, S, FOX_W)

def _token_mixing(n, w_in, cmp_pe, cmp_w1, cmp_w2, fox_bias, br_nsa, br_dil, br_fox, w_out, cos, sin):
    B, S = n.shape[0], n.shape[1]
    proj = n @ w_in
    nsa_q, nsa_kv, nsa_g, dil_qkv, fox_qkv, fox_f, merge_g = _split_cols(proj, IN_WIDTHS)

    def heads(t, h):
        return t.reshape(B, S, h, HEAD_DIM)

    def rope_single(t):
        return _partial_rope(t[:, :, None, :], cos, sin)[:, :, 0, :]

    q_a = _partial_rope(heads(nsa_q, NSA_HEADS), cos, sin)
    kc, vc, ks, vs, kw, vw = jnp.split(nsa_kv, 6, axis=-1)
    y_a = _nsa_attention(q_a, rope_single(kc), vc, rope_single(ks), vs, rope_single(kw), vw,
                         nsa_g.reshape(B, S, NSA_HEADS, 3), cmp_pe, cmp_w1, cmp_w2)
    dq, dk, dv = jnp.split(dil_qkv, 3, axis=-1)
    y_b = _dilated_attention(_partial_rope(heads(dq, DIL_HEADS), cos, sin),
                             _partial_rope(heads(dk, DIL_HEADS), cos, sin),
                             heads(dv, DIL_HEADS))
    fq, fk, fv = jnp.split(fox_qkv, 3, axis=-1)
    y_c = _forgetting_attention(heads(fq, FOX_HEADS), heads(fk, FOX_HEADS), heads(fv, FOX_HEADS),
                                fox_f, fox_bias)
    g_a, g_b, g_c = jnp.split(jax.nn.sigmoid(merge_g), 3, axis=-1)
    merged = g_a * (y_a @ br_nsa) + g_b * (y_b @ br_dil) + g_c * (y_c @ br_fox)
    return merged @ w_out

def second_inputs(seed: int = 0) -> dict:
    key = jax.random.key(seed)
    ks = jax.random.split(key, 17)
    L, D = DEPTH, D_MODEL

    def nrm(k, shape, scale):
        return jax.random.normal(k, shape, jnp.float32) * scale

    return {
        'x': nrm(ks[0], (BATCH, SEQ, D), 1.0),
        'c': nrm(ks[1], (BATCH, D), 1.0),
        'ada_w': nrm(ks[2], (L, D, 9 * D), 0.5 * D ** -0.5),
        'ada_b': nrm(ks[3], (L, 9 * D), 0.02),
        'norm_g': 1.0 + nrm(ks[4], (L, 3, D), 0.05),
        'final_norm_g': 1.0 + nrm(ks[5], (D,), 0.05),
        'ffn_w_in': nrm(ks[6], (L, 2, D, 2 * D_FF), D ** -0.5),
        'ffn_w_out': nrm(ks[7], (L, 2, D_FF, D), D_FF ** -0.5),
        'mix_w_in': nrm(ks[8], (L, D, IN_COLS_2), D ** -0.5),
        'nsa_cmp_pe': nrm(ks[9], (L, 2, NSA_CMP_LEN, HEAD_DIM), 0.1),
        'nsa_cmp_w1': nrm(ks[10], (L, 2, NSA_CMP_LEN * HEAD_DIM, NSA_CMP_HIDDEN), (NSA_CMP_LEN * HEAD_DIM) ** -0.5),
        'nsa_cmp_w2': nrm(ks[11], (L, 2, NSA_CMP_HIDDEN, HEAD_DIM), NSA_CMP_HIDDEN ** -0.5),
        'fox_f_bias': jax.random.uniform(ks[12], (L, FOX_HEADS), jnp.float32, 1.0, 6.0),
        'br_w_nsa': nrm(ks[13], (L, NSA_Q_W, D), NSA_Q_W ** -0.5),
        'br_w_dil': nrm(ks[14], (L, DIL_OUT_W, D), DIL_OUT_W ** -0.5),
        'br_w_fox': nrm(ks[15], (L, FOX_W, D), FOX_W ** -0.5),
        'mix_w_out': nrm(ks[16], (L, D, D), D ** -0.5),
    }

def second_block(x, c, ada_w, ada_b, norm_g, final_norm_g, ffn_w_in, ffn_w_out, mix_w_in,
              nsa_cmp_pe, nsa_cmp_w1, nsa_cmp_w2, fox_f_bias, br_w_nsa, br_w_dil, br_w_fox,
              mix_w_out):
    S = x.shape[1]
    cos, sin = _rope_tables(S)
    cond = jax.nn.silu(c)
    h = x
    for l in range(DEPTH):
        mod = cond @ ada_w[l] + ada_b[l]
        sh1, sc1, ga1, sh2, sc2, ga2, sh3, sc3, ga3 = [m[:, None, :] for m in jnp.split(mod, 9, axis=-1)]
        n = _modulate(_rms_norm(h, norm_g[l, 0]), sh1, sc1)
        h = h + 0.5 * ga1 * _swiglu(n, ffn_w_in[l, 0], ffn_w_out[l, 0])
        n = _modulate(_rms_norm(h, norm_g[l, 1]), sh2, sc2)
        h = h + ga2 * _token_mixing(n, mix_w_in[l], nsa_cmp_pe[l], nsa_cmp_w1[l], nsa_cmp_w2[l],
                                    fox_f_bias[l], br_w_nsa[l], br_w_dil[l], br_w_fox[l],
                                    mix_w_out[l], cos, sin)
        n = _modulate(_rms_norm(h, norm_g[l, 2]), sh3, sc3)
        h = h + 0.5 * ga3 * _swiglu(n, ffn_w_in[l, 1], ffn_w_out[l, 1])
    return _rms_norm(h, final_norm_g)


def setup_inputs(seed=0):
    out = dict(first_inputs(seed))
    for name, value in second_inputs(seed + 1).items():
        if name != "x":
            out[name + "_2"] = value
    return out


def reference(
    x, ffn1_pre_g, ffn1_post_g, ffn1_w_gu, ffn1_w_down, mix_pre_g, mix_post_g, w_in, gm_v_g,
    gm_ws, gm_b, pool_w, pool_scale, conv_dw, conv_b, conv_ln_g, conv_ln_b, w_branch, w_out,
    ffn2_pre_g, ffn2_post_g, ffn2_w_gu, ffn2_w_down, rel_bias, c_2, ada_w_2, ada_b_2, norm_g_2,
    final_norm_g_2, ffn_w_in_2, ffn_w_out_2, mix_w_in_2, nsa_cmp_pe_2, nsa_cmp_w1_2,
    nsa_cmp_w2_2, fox_f_bias_2, br_w_nsa_2, br_w_dil_2, br_w_fox_2, mix_w_out_2,
):
    x = first_block(
        x, ffn1_pre_g, ffn1_post_g, ffn1_w_gu, ffn1_w_down, mix_pre_g, mix_post_g, w_in, gm_v_g,
        gm_ws, gm_b, pool_w, pool_scale, conv_dw, conv_b, conv_ln_g, conv_ln_b, w_branch, w_out,
        ffn2_pre_g, ffn2_post_g, ffn2_w_gu, ffn2_w_down, rel_bias,
    )
    return second_block(
        x, c_2, ada_w_2, ada_b_2, norm_g_2, final_norm_g_2, ffn_w_in_2, ffn_w_out_2, mix_w_in_2,
        nsa_cmp_pe_2, nsa_cmp_w1_2, nsa_cmp_w2_2, fox_f_bias_2, br_w_nsa_2, br_w_dil_2,
        br_w_fox_2, mix_w_out_2,
    )


_drawn_inputs = setup_inputs


def setup_inputs(seed=0):
    import zlib

    import numpy as np

    out = dict(_drawn_inputs(seed))
    spreads = {}
    factors = {'gm_v_g': 3.156,
     'conv_b': 2.726,
     'conv_ln_b': 4.887,
     'ada_b_2': 5.201,
     'norm_g_2': 6.042,
     'nsa_cmp_pe_2': 8.0,
     'nsa_cmp_w1_2': 2.702,
     'fox_f_bias_2': 3.029}
    for name, (base, spread) in spreads.items():
        noise = np.random.default_rng([zlib.crc32(name.encode()), seed]).standard_normal(out[name].shape)
        drawn = base * np.exp(spread * noise) if base else spread * noise
        out[name] = jnp.asarray(drawn.astype(out[name].dtype))
    for name, factor in factors.items():
        out[name] = (out[name] * factor).astype(out[name].dtype)
    return out
```

```python
from contextlib import ExitStack

import numpy as np
import concourse.bass as bass
from concourse import mybir

F32 = mybir.dt.float32
F32R = mybir.dt.float32r
ALU = mybir.AluOpType
ACT = mybir.ActivationFunctionType
AX = mybir.AxisListType

P = 128
D = 1024
C = D // P
T = 256
FF = 2816
NF = FF // P
DEPTH = 2
RING = 3
UNITS = 33
LAYER_UNITS = 3 * UNITS
SLOT = 2096
EPS = 1e-6
NEG = -1e30
TAKEN = -3e38
ADA_V = 336
CAUSAL = P + T
SPAN = ((0, P), (P, T))

U_GATE, V_GATE, POOL_U, Q_U, K_U, V_U, IDX_U, CONV_A, CONV_G, GATES1, BR1, OUT1 = 0, 1, 2, 3, 4, 5, 6, 7, 8, 9, 25, 29
COLS1 = [(0, 256), (256, 256), (512, 256), (768, 256), (1024, 256), (1280, 256), (1536, 164), (1700, 256), (1956, 256)]
COLS1 += [(2212 + 256 * i, 256) for i in range(16)]
NQ_U, KV_U, VG_U, DQK_U, FQK_U, DV_U, FV_U, DVF_U, W1_U, GATES2, BR2, OUT2 = 0, 1, 2, 3, 6, 9, 10, 11, 12, 14, 26, 29
COLS2 = [[(0, 256)], [(256, 192), (512, 64)], [(448, 64), (576, 76)]]
COLS2 += [[(652 + 256 * i, 256)] for i in range(3)] + [[(1804 + 256 * i, 256)] for i in range(3)]
COLS2 += [[(1420, 256)], [(2572, 256)], [(1420 + 256, 128), (2572 + 256, 134)], None, None]
COLS2 += [[(2962 + 256 * i, 256)] for i in range(12)]
V1_PRE1, V1_POST1, V1_PREM, V1_POSTM, V1_PRE2, V1_POST2, V1_PS, V1_CB, V1_LG, V1_LB, V1_DW, V1_N = 0, 8, 16, 24, 32, 40, 48, 50, 52, 54, 56, 118
V2_G, V2_B, V2_PE, V2_N = 0, 24, 96, 128
GROUPS2 = ["d0", "d1", "d2", "s0", "w0", "s1", "w1", "f0", "f1", "f2"]
SIDE2 = {1: ["rope0"], 2: ["rope1"], 3: ["dup"], 4: ["rope3"], 5: ["rope4"], 6: ["rope5"],
         7: ["qk d0"], 8: ["qk d1", "ke"], 9: ["qk d2"], 11: ["lf"], 12: ["fox", "tr d0"], 13: ["pv d0", "tr d1", "hid"],
         14: ["pv d1", "tr d2", "w2"], 15: ["pv d2", "cqk"], 16: ["ctr", "qk s0"], 17: ["tr s0", "qk w0"],
         18: ["cpv 0", "pv s0", "tr w0", "qk s1"], 19: ["pv w0", "tr s1", "qk w1"],
         20: ["cpv 1", "pv s1", "tr w1", "qk f0"], 21: ["pv w1", "tr f0", "qk f1"],
         22: ["pv f0", "tr f1", "qk f2"], 23: ["pv f1", "tr f2"], 24: ["pv f2"]}
ROPED = [0, 1, 3, 4, 5]
CHUNK2 = {"w0": 0, "w1": 1, "d2": 2, "f0": 3, "f1": 4, "f2": 5}
SIDE1 = {2: ["gm0"], 3: ["gm1"], 4: ["pool0"], 5: ["pool1"], 7: ["idx 0"], 8: ["idx 1"], 9: ["convh"],
         **{10 + j: [f"top {j}", f"tap {j}"] for j in range(8)},
         18: ["ln1", "qk 0"], 19: ["ln2", "qk 1"], 20: ["ln3", "tr 0"], 21: ["pv 0", "tr 1"], 22: ["pv 1"]}


class Counts:

    def __init__(self, known=None):
        self.known, self.order, self.section, self.layer, self.newest = known, {}, "setup", 0, {}

    def done(self, who, what):
        names = self.order.setdefault((who, self.section), {})
        assert what not in names, what
        names[what] = len(names) + 1
        self.newest[who] = what
        return 1

    def at(self, who, what, section=None):
        if self.known is None:
            return 1
        section = section or self.section
        value = self.known[(who, section)][what]
        for s, times in (("setup", 1), ("block1", DEPTH), ("block2", DEPTH), ("end", 1)):
            if s == section:
                break
            value += times * len(self.known.get((who, s), {}))
        if section == self.section and section.startswith("block"):
            return value + self.layer * len(self.known[(who, section)])
        return value + ((DEPTH - 1) * len(self.known[(who, section)]) if section.startswith("block") else 0)


def spread(ap, at, n):
    dims = [list(d) for d in ap.ap]
    dims.insert(at, [0, n])
    return bass.AP(ap.tensor, ap.offset, dims)


def window(ap, dims):
    return bass.AP(ap.tensor, ap.offset, [list(ap.ap[0])] + [list(d) for d in dims])


def program(nc, known, i, out):
    m = Counts(known)
    at, done = m.at, m.done
    with ExitStack() as ctx:
        def sb(name, shape, dt=F32):
            return ctx.enter_context(nc.sbuf_tensor(name, shape, dt))

        def sem(name):
            return ctx.enter_context(nc.semaphore(name))

        raw = sb("raw", [P, RING, SLOT])
        hi = sb("hi", [P, RING, SLOT], F32R)
        lo = sb("lo", [P, RING, SLOT], F32R)
        XT = sb("XT", [P, C, T])
        NH = sb("NH", [P, C, T], F32R)
        NL = sb("NL", [P, C, T], F32R)
        T8 = sb("T8", [P, C, T])
        BH = sb("BH", [P, 8, T], F32R)
        BL = sb("BL", [P, 8, T], F32R)
        arena = sb("arena", [P, 21700])
        used = {"shared": 0, "block1": 0, "block2": 0}

        def place(where, *shape):
            size = int(np.prod(shape))
            a = used[where] + (used["shared"] if where != "shared" else 0)
            used[where] += size
            assert used["shared"] + max(used["block1"], used["block2"]) <= 21700
            v = arena[:, a:a + size]
            if len(shape) == 2:
                v = v.rearrange("p (a b) -> p a b", b=shape[1])
            if len(shape) == 3:
                v = v.rearrange("p (a b c) -> p a b c", b=shape[1], c=shape[2])
            return v

        ident = place("shared", P)
        tri = place("shared", T)
        causal = place("shared", CAUSAL)
        mean_d = place("shared", P)
        mean_w = place("shared", P)
        eps = place("shared", 1)
        rms = place("shared", 3, T)
        vrow = place("shared", P)
        vec = place("shared", P)
        vec0 = place("shared", 16)
        cond = place("shared", C)
        mods = place("shared", DEPTH, 72)
        modl = place("shared", 72)
        gains = place("shared", 48)
        acc_ada = place("shared", 2 * T)
        PT = place("shared", 2, CAUSAL)
        NM = place("shared", 10, 4)
        DEN = place("shared", 10, 4)
        FAC = place("shared", 10, 4)
        G = place("block1", 32, T)
        SA, HF = G[:, 0:2, :], G[:, 2:4, :]
        P1 = place("block1", 4, CAUSAL)
        CA = P1[:, 0:2, 0:T]
        SG = P1[:, 2:4, 0:T]
        TB = place("block1", 4, CAUSAL)
        UT = place("block1", 2, T)
        PZ = place("block1", 2, 16 + T)
        SC = place("block1", 2, 16 + T)
        WK = place("block1", 2, 16 + T)
        PD = place("block1", 2, T)
        WI = place("block1", 2, 4)
        M8 = place("block1", 2, 8)
        REL = UT
        CH = place("block1", 2, 30 + T)
        ACC = PD
        SM = place("block1", CAUSAL)
        WS = place("block1", 4, P)
        QKI = WS.rearrange("p g t -> p (g t)").rearrange("p (a t) -> p a t", a=2)
        WST = place("block1", 4, P)
        PW = place("block1", 2, 64)
        RC = place("block1", 2, T)
        GB = place("block1", 2, P)
        BG = place("block1", T)
        ms = place("block1", 8)
        BT = place("block1", 2, T)
        SCf, WKf = (v.rearrange("p a b -> p (a b)") for v in (SC, WK))
        QT, KT, VT, VG = (T8[:, 2 * k:2 * k + 2, :] for k in range(4))
        ADA = ((0, ADA_V), (ADA_V, 2 * T - ADA_V))
        ADW = [G[:, 8:24, :].rearrange("p c t -> p (c t)")[:, C * o:C * (o + w)].rearrange("p (c n) -> p c n", n=w) for o, w in ADA]
        onehot = G[:, 0:2, :]
        brev = G[:, 2:10, :]
        flip = G[:, 10, 0:P]
        bias_rows = G[:, 12:14, :]
        G2 = place("block2", 24, T)
        P2 = place("block2", 6, CAUSAL)
        DM = place("block2", 3, CAUSAL)
        NQ = place("block2", 2, T)
        KVC = place("block2", 16 + T)
        KSW = G2[:, 8, :]
        KSD = place("block2", 2, T)
        VSW = place("block2", 2, 140)
        DQK = place("block2", 6, T)
        FQK = place("block2", 6, T)
        DV = place("block2", 2, 3 * P)
        FV = place("block2", 2, 3 * P)
        FL = place("block2", 2, 8)
        LF = place("block2", 2, 8)
        LE = place("block2", 2, 8)
        CT = place("block2", 2, 8)
        CS = DQK
        PTC = T8[:, 0:4, :]
        FM = T8[:, 4:7, :].rearrange("p a t -> p (a t)").rearrange("p (e k) -> p e k", e=2)
        LFB = G2[:, 0:6, :].rearrange("p h (t k) -> p h t k", t=2)
        ROPE = place("block2", 2, T)
        SWAP = place("block2", P)
        DUP = place("block2", 2, P)
        KE = G2[:, 6:8, :]
        W2 = place("block2", 192)
        HID = place("block2", 2, 16)
        KC2 = place("block2", 16)
        VC2 = place("block2", 64)
        PC = place("block2", 8, 16)
        CMK = place("block2", 2, 16)
        CMB = place("block2", 2, 16)
        CN = place("block2", 3, 8)
        GT = place("block2", 2, 12)
        FB = place("block2", 8)
        DE = place("block2", 3, 12)
        D4 = place("block2", 3, 4)
        Z = T8[:, 0:4, :].rearrange("p (r a) t -> p r a t", r=2)
        RT = T8[:, 4:8, :].rearrange("p (r a) t -> p r a t", r=2)

        zero = sb("zero", [P, 640], mybir.dt.bfloat16)
        tick = sb("tick", [P, 4])
        pool_tick = sb("pool_tick", [P, 2])

        ps = ctx.enter_context(nc.psum_tensor("ps", [P, 8, 512], F32))
        g_dram = nc.dram_tensor("bias_by_distance", [4, 512], F32, kind="Internal").ap()

        raw_ready = [sem(f"raw_ready{k}") for k in range(RING)]
        hi_ready = sem("hi_ready")
        lo_ready = sem("lo_ready")
        unit_used = sem("unit_used")
        silu_ready = sem("silu_ready")
        hidden_ready = sem("hidden_ready")
        hidden_hi = sem("hidden_hi")
        hidden_lo = sem("hidden_lo")
        const_in = sem("const_in")
        ada_in = [sem(f"ada_in{k}") for k in range(2)]
        ada_sum = [sem(f"ada_sum{k}") for k in range(2)]
        ada_out = sem("ada_out")
        ada_step = sem("ada_step")
        ada_fold = sem("ada_fold")
        ada_kept = sem("ada_kept")
        small_in = sem("small_in")
        rows_in = sem("rows_in")
        stored = sem("stored")
        pe_done, act_done, dve_done, pool_done = sem("pe_done"), sem("act_done"), sem("dve_done"), sem("pool_done")
        sems = {"pe": pe_done, "act": act_done, "dve": dve_done, "pool": pool_done}

        SMALL1, SMALL2, CONSTS2 = 6, 4, 6
        ROWS1, ROWS2 = 11, 3

        def small_target(block, l):
            return 16 * SMALL1 * (l + 1) if block == 1 else 16 * (SMALL1 * DEPTH + CONSTS2 + SMALL2 * (l + 1))

        def rows_target(block, l):
            return 16 * ROWS1 * (l + 1) if block == 1 else 16 * (ROWS1 * (DEPTH + 1) + ROWS2 * (l + 1))

        def unit_number(block, l, pos):
            return (block - 1) * DEPTH * LAYER_UNITS + l * LAYER_UNITS + pos

        block_ = ctx.enter_context(nc.Block())

        @block_.sync
        def _(sp):
            def load(block, l, q, s, pieces):
                sp.wait_ge(lo_ready, unit_number(block, l, 3 * q + s) + 1)
                assert len(pieces) == 2
                for dst, src in pieces:
                    sp.dma_start(dst(s), src).then_inc(raw_ready[s], 16)

            def cols(slot, a, b, n):
                return raw[:, slot, 0:8 * n].rearrange("p (c n) -> p c n", n=n)[:, :, a:b]

            def gate_up(w, f):
                view = w.rearrange("(c p) n -> p c n", p=P)
                return [(lambda s: cols(s, 0, P, T), view[:, :, bass.ds(P * f, P)]),
                        (lambda s: cols(s, P, T, T), view[:, :, bass.ds(P * f + FF, P)])]

            def down(w, i):
                view = w.rearrange("(k p) n -> p k n", p=P)
                return [(lambda s: raw[:, s, 0:1024], view[:, 2 * i, :]),
                        (lambda s: raw[:, s, 1024:2048], view[:, 2 * i + 1, :])]

            def halves(w, a, n):
                view = w.rearrange("(c p) n -> p c n", p=P)
                return [(lambda s, h=h: raw[:, s, 0:8 * n].rearrange("p (c n) -> p c n", n=n)[:, 4 * h:4 * h + 4, :],
                         view[:, 4 * h:4 * h + 4, a:a + n]) for h in range(2)]

            def rows(w, k):
                view = w.rearrange("(k p) n -> p k n", p=P)
                return [(lambda s, j=j: raw[:, s, 1024 * j:1024 * j + 1024], view[:, k + j, :]) for j in range(2)]

            def ffn(block, l, b, gu, dn):
                load(block, l, b, 0, gate_up(gu, 0))
                load(block, l, b, 1, gate_up(gu, 1))
                with sp.Fori(1, NF // 2) as i:
                    load(block, l, b + i - 1, 2, gate_up(gu, 2 * i))
                    load(block, l, b + i, 0, gate_up(gu, 2 * i + 1))
                    load(block, l, b + i, 1, down(dn, i - 1))
                load(block, l, b + 10, 2, down(dn, NF // 2 - 1))

            sp.dma_start(T8[:, :, :].rearrange("p (a b) t -> p a (b t)", a=2),
                         i["x"][0].rearrange("(a p) d -> p a d", p=P)).then_inc(const_in, 16)
            for n, (dst, src) in enumerate([
                (ident, i["ident"]), (tri, i["tri"]), (causal, i["causal"]), (RC.rearrange("p a b -> p (a b)"), i["rcount"]),
                (onehot.rearrange("p a b -> p (a b)")[0:32], i["onehot"]), (flip, i["flip"]),
                (WI.rearrange("p a b -> p (a b)")[0:32, 0:4], i["rel_bias"]),
                (vrow[0:8], i["c_2"].rearrange("a (c p) -> (a c) p", p=P)),
                (vrow[8:16], i["final_norm_g_2"].rearrange("(c p) -> c p", p=P)),
            ]):
                sp.dma_start(dst, src).then_inc(const_in, 16)
            sp.wait_ge(act_done, at("act", "bias rows", "setup"))
            sp.dma_start(g_dram, bias_rows.rearrange("p a b -> p (a b)")[0:4]).then_inc(const_in, 16)
            sp.wait_ge(const_in, 16 * 11)
            for t in range(2):
                sp.dma_start(brev.rearrange("p (h t) w -> p h t w", t=2)[:, :, t, :],
                             bass.AP(g_dram.tensor, P * (1 - t), [[1, P], [512, 4], [1, T]])).then_inc(const_in, 16)
            for block in (1, 2):
                m.section = f"block{block}"
                with sp.Fori(0, DEPTH) as l:
                    m.layer = l
                    if block == 1:
                        gu1, dn1, gu2, dn2 = i["ffn1_w_gu"][l], i["ffn1_w_down"][l], i["ffn2_w_gu"][l], i["ffn2_w_down"][l]
                    else:
                        gu1, dn1 = i["ffn_w_in_2"][l, 0], i["ffn_w_out_2"][l, 0]
                        gu2, dn2 = i["ffn_w_in_2"][l, 1], i["ffn_w_out_2"][l, 1]
                    ffn(block, l, 0, gu1, dn1)
                    for u in range(UNITS):
                        if block == 1:
                            if u < BR1:
                                pieces = halves(i["w_in"][l], *COLS1[u])
                            elif u < OUT1:
                                pieces = rows(i["w_branch"][l, u - BR1], 0)
                            else:
                                pieces = halves(i["w_out"][l], 256 * (u - OUT1), 256)
                        else:
                            if u in (W1_U, W1_U + 1):
                                pieces = [(lambda s, kv=kv: raw[64 * kv:64 * kv + 64, s, 0:2048].rearrange("p (j n) -> p j n", n=P),
                                           i["nsa_cmp_w1_2"][l, kv, 1024 * (u - W1_U):1024 * (u - W1_U) + 1024, :]
                                           .rearrange("(j d) n -> d j n", d=64)) for kv in range(2)]
                            elif u < BR2:
                                parts = COLS2[u]
                                if len(parts) == 1:
                                    pieces = halves(i["mix_w_in_2"][l], *parts[0])
                                else:
                                    n = parts[0][1] + parts[1][1]
                                    view = i["mix_w_in_2"][l].rearrange("(c p) n -> p c n", p=P)
                                    pieces = []
                                    for k, (a, w) in enumerate(parts):
                                        o = 0 if k == 0 else parts[0][1]
                                        pieces.append((lambda s, o=o, w=w, n=n: cols(s, o, o + w, n), view[:, :, a:a + w]))
                            elif u == BR2:
                                pieces = rows(i["br_w_nsa_2"][l], 0)
                            elif u == BR2 + 1:
                                pieces = rows(i["br_w_fox_2"][l], 0)
                            elif u == BR2 + 2:
                                pieces = [(lambda s: raw[:, s, 0:1024], i["br_w_fox_2"][l, 256:384, :]),
                                          (lambda s: raw[:, s, 1024:2048], i["br_w_dil_2"][l])]
                            else:
                                pieces = halves(i["mix_w_out_2"][l], 256 * (u - OUT2), 256)
                        load(block, l, 11 + u // 3, u % 3, pieces)
                    ffn(block, l, 22, gu2, dn2)
            sp.wait_ge(act_done, at("act", "out", "end"))
            sp.dma_start(out[0].rearrange("(a p) d -> p a d", p=P),
                         XT[:, :, :].rearrange("p (a b) t -> p a (b t)", a=2)).then_inc(stored, 16)
            sp.wait_ge(stored, 16)


        @block_.gpsimd
        def _(pool):
            m.section = "setup"
            nc.gpsimd.memset(eps, EPS).then_inc(pool_done, done("pool", "eps"))
            nc.gpsimd.memset(mean_d, 1.0 / D).then_inc(pool_done, done("pool", "mean_d"))
            nc.gpsimd.memset(mean_w, 1.0 / 256).then_inc(pool_done, done("pool", "mean_w"))

            def small(dst, src):
                pool.dma_start(dst, src).then_inc(small_in, 16)

            def take_wait(k):
                nc.gpsimd.tensor_tensor(pool_tick[:, k:k + 1], eps, eps, ALU.mult)

            def load_rows(block, l):
                def rows(dst, src):
                    pool.dma_start(dst, src).then_inc(rows_in, 16)

                if block == 1:
                    for name, row, n in (("ffn1_pre_g", V1_PRE1, 8), ("ffn1_post_g", V1_POST1, 8), ("mix_pre_g", V1_PREM, 8),
                                         ("mix_post_g", V1_POSTM, 8), ("ffn2_pre_g", V1_PRE2, 8), ("ffn2_post_g", V1_POST2, 8),
                                         ("pool_scale", V1_PS, 2), ("conv_b", V1_CB, 2), ("conv_ln_g", V1_LG, 2), ("conv_ln_b", V1_LB, 2)):
                        rows(vrow[row:row + n], i[name][l].rearrange("(c p) -> c p", p=P))
                    rows(vrow[V1_DW:V1_N], i["conv_dw"][l].rearrange("j (c p) -> (j c) p", p=P))
                else:
                    rows(vrow[V2_G:V2_B], i["norm_g_2"][l].rearrange("k (c p) -> (k c) p", p=P))
                    rows(vrow[V2_B:V2_PE], i["ada_b_2"][l].rearrange("(k p) -> k p", p=P))
                    rows(vrow[V2_PE:V2_N].rearrange("p (v d) -> p v d", v=2), i["nsa_cmp_pe_2"][l].rearrange("v j d -> j v d"))

            def ada(l, s):
                w = i["ada_w_2"][l].rearrange("(c p) n -> p c n", p=P)
                with pool.Fori(0, 9) as k:
                    a = 18 * l + 9 * s + k
                    for h, (o, n) in reversed(list(enumerate(ADA))):
                        pool.wait_ge(ada_sum[h], a + 1)
                        pool.dma_start(ADW[h], w[:, :, bass.ds(512 * (9 * s + k) + o, n)]).then_inc(ada_in[h], 16)
                    pool.wait_ge(ada_in[1], 16 * (a + 1))
                    nc.gpsimd.tensor_tensor(ADW[1], ADW[1], spread(cond, 2, ADA[1][1]), ALU.mult).then_inc(ada_fold, 1)
                    for n, half in enumerate((4, 2)):
                        pool.wait_ge(ada_fold, 3 * a + n + 1)
                        nc.gpsimd.tensor_tensor(ADW[1][:, 0:half], ADW[1][:, 0:half], ADW[1][:, half:2 * half], ALU.add).then_inc(ada_fold, 1)
                    pool.wait_ge(ada_fold, 3 * a + 3)
                    pool.wait_ge(ada_out, a + 1)
                    nc.gpsimd.tensor_tensor(acc_ada[:, ADA_V:], ADW[1][:, 0], ADW[1][:, 1], ALU.add).then_inc(ada_sum[1], 1)

            def scale_group(p_tile, g, slot):
                pool.wait_ge(dve_done, at("dve", f"factor {g}"))
                for e in range(2):
                    for t, (o, w) in enumerate(SPAN):
                        v = p_tile[:, 2 * slot + e, o:o + w]
                        last = nc.gpsimd.tensor_tensor(v, v, window(FAC[:, g, 2 * e + t:2 * e + t + 1], [[0, w]]), ALU.mult)
                last.then_inc(pool_done, done("pool", f"p {g}"))

            pool.wait_ge(pe_done, at("pe", "vec0"))
            load_rows(1, 0)
            pool.wait_ge(act_done, at("act", "TB"))
            for block in (1, 2):
                if block == 2:
                    m.section = "between"
                    pool.wait_ge(rows_in, 16 * ROWS1 * (DEPTH + 1))
                    load_rows(2, 0)
                    pool.wait_ge(dve_done, at("dve", "x2 3", "block1"))
                    for dst, src in ((DM.rearrange("p a b -> p (a b)"), i["dilated"]), (ROPE.rearrange("p a b -> p (a b)"), i["rope"]),
                                     (SWAP, i["swap"]), (DUP.rearrange("p a b -> p (a b)"), i["dup"]),
                                     (CMK.rearrange("p a b -> p (a b)"), i["cmp_add"]), (CMB.rearrange("p a b -> p (a b)"), i["cmp_keep"])):
                        small(dst, src)
                m.section = f"block{block}"
                with pool.Fori(0, DEPTH) as l:
                    m.layer = l
                    pool.wait_ge(dve_done, at("dve", "gains"))
                    take_wait(0)
                    load_rows(block, DEPTH - 1)
                    if block == 1:
                        small(WS, i["gm_ws"][l].rearrange("g t s -> t g s"))
                        for k in range(2):
                            small(GB[64 * k:64 * k + 64], i["gm_b"][l].rearrange("(h k) t -> k h t", k=2)[k].partition_broadcast(64))
                            small(PW[64 * k:64 * k + 64], i["pool_w"][l].rearrange("(h k) c d -> k c h d", k=2)[k])
                        small(BG, i["gm_v_g"][l].partition_broadcast(P))
                        nc.gpsimd.memset(PZ[:, :, 0:16], 0.0)
                        nc.gpsimd.memset(CH[:, :, 0:30], 0.0).then_inc(pool_done, done("pool", "pads"))
                    else:
                        for k in range(2):
                            small(W2[:, 64 * k:64 * k + 64], i["nsa_cmp_w2_2"][l, 0])
                        small(W2[:, 128:192], i["nsa_cmp_w2_2"][l, 1])
                        small(FB[:, 0:6], i["fox_f_bias_2"][l].partition_broadcast(P))
                        nc.gpsimd.memset(KVC[:, T:T + 16], 0.0).then_inc(pool_done, done("pool", "pads"))
                    if block == 1:
                        ada(l, 0)
                    for u in range(UNITS):
                        for work in (SIDE1 if block == 1 else SIDE2).get(u, ()):
                            if block == 1 and work[:2] == "qk":
                                scale_group(P1, int(work[3:]), int(work[3:]))
                            elif work == "qk d2":
                                for g in range(3):
                                    scale_group(P2, g, g)
                            elif work[:2] == "qk" and work[3] != "d":
                                g = GROUPS2.index(work[3:])
                                scale_group(P2, g, g % 3)
                        if block == 1 and u in (BR1 + 1, BR1 + 2):
                            k = u - BR1
                            pool.wait_ge(dve_done, at("dve", f"gated {k}"))
                            if k == 2:
                                pool.wait_ge(pool_done, at("pool", "sum 1"))
                            nc.gpsimd.tensor_tensor(T8[:, :, :], G[:, 0:8, :] if k == 1 else T8[:, :, :], G[:, 8 * k:8 * k + 8, :],
                                                    ALU.add).then_inc(pool_done, done("pool", f"sum {k}"))
                        if block == 2 and u == BR2 + 2:
                            pool.wait_ge(dve_done, at("dve", "gated 1"))
                            nc.gpsimd.tensor_tensor(T8[:, :, :], G2[:, 0:8, :], G2[:, 16:24, :],
                                                    ALU.add).then_inc(pool_done, done("pool", "sum 1"))
                    if block == 1:
                        pool.wait_ge(dve_done, at("dve", "xm 3"))
                        take_wait(1)
                        ada(l, 1)

        def split_pieces(block, pos, s, dst):
            u = pos - UNITS
            if block == 1 and u == IDX_U:
                a, b = dst[:, s, 0:8 * 260].rearrange("p (c n) -> p c n", n=260), raw[:, s, 0:8 * 164].rearrange("p (c n) -> p c n", n=164)
                return [(a[:, :, 0:128], b[:, :, 0:128]),
                        (a[:, :, 128:256].rearrange("p c (k n) -> p c k n", k=4), spread(b[:, :, 128:160], 2, 4)),
                        (a[:, :, 256:260], b[:, :, 160:164])]
            n = 2048
            if block == 2 and u == VG_U:
                n = 8 * 140
            if block == 2 and u == DVF_U:
                n = 8 * 262
            return [(dst[:, s, 0:n], raw[:, s, 0:n])]

        @block_.scalar
        def _(act):
            def split_hi(block, l, q, s, pos=0):
                n = unit_number(block, l, 3 * q + s)
                act.wait_ge(raw_ready[s], 32 * ((block - 1) * DEPTH * UNITS + l * UNITS + q + 1))
                act.wait_ge(unit_used, n + 1)
                for dst, src in split_pieces(block, pos, s, hi):
                    last = nc.scalar.activation(dst, src, ACT.Copy)
                last.then_inc(hi_ready, 1)

            def settle():
                act.wait_ge(act_done, at("act", m.newest["act"]))

            def unit_out(block, l, q, s):
                act.wait_ge(unit_used, unit_number(block, l, 3 * q + s) + 4)

            def root(name, bank):
                act.wait_ge(pe_done, at("pe", name + " stat"))
                nc.scalar.activation(rms[:, 0, :], ps[:, bank, 0:T], ACT.Sqrt, bias=eps).then_inc(act_done, done("act", name + " root"))

            def squares(name, x):
                for b in range(4):
                    if x:
                        act.wait_ge(dve_done, at("dve", f"{x} {b}"))
                    nc.scalar.activation(T8[:, 2 * b:2 * b + 2, :], XT[:, 2 * b:2 * b + 2, :], ACT.Square)\
                        .then_inc(act_done, done("act", f"{name} sq{b}"))
                root(name, 3)

            def pre(name, shift):
                for c in range(C):
                    act.wait_ge(dve_done, at("dve", f"{name} n{c}"))
                    if shift is None:
                        ins = nc.scalar.activation(NH[:, c, :], T8[:, c, :], ACT.Copy)
                    else:
                        ins = nc.scalar.activation(NH[:, c, :], T8[:, c, :], ACT.Identity, bias=modl[:, shift + c:shift + c + 1])
                    ins.then_inc(act_done, done("act", f"{name} h{c}"))

            def post(name):
                for b in range(4):
                    nc.scalar.activation(T8[:, 2 * b:2 * b + 2, :].rearrange("p a t -> p (a t)"), ps[:, 4 + b, :],
                                         ACT.Square).then_inc(act_done, done("act", f"{name} sq{b}"))
                root(name, 3)

            def silu(block, l, F, f, q, s, bank, par):
                unit_out(block, l, q, s)
                nc.scalar.activation(SA[:, par, :], ps[:, bank, 0:T], ACT.Silu).then_inc(silu_ready, 1)

            def hidden_parts(F, f):
                for k in range(2):
                    act.wait_ge(hidden_ready, NF * F + f + k + 1)
                    nc.scalar.activation(BH[:, k, :], HF[:, k, :], ACT.Copy).then_inc(hidden_hi, 1)

            def ffn(block, l, b, F, last_of_layer):
                split_hi(block, l, b, 2)
                silu(block, l, F, 0, b, 0, 0, 0)
                split_hi(block, l, b + 1, 0)
                silu(block, l, F, 1, b, 1, 1, 1)
                hidden_parts(F, 0)

                def body(i, more):
                    split_hi(block, l, b + i, 1)
                    silu(block, l, F, 2 * i, b + i - 1, 2, 2, 0)
                    if more is not None:
                        split_hi(block, l, b + i, 2, more)
                    silu(block, l, F, 2 * i + 1, b + i, 0, 0, 1)
                    if more is not None and not (last_of_layer and more == -1):
                        split_hi(block, l, b + i + 1, 0, 0 if more != -1 else b * 3 + UNITS)
                    unit_out(block, l, b + i, 1)
                    hidden_parts(F, 2 * i)

                with act.Fori(1, NF // 2 - 1) as i:
                    body(i, 0)
                body(NF // 2 - 1, -1)
                if not last_of_layer:
                    split_hi(block, l, b + 11, 1, b * 3 + UNITS + 1)
                unit_out(block, l, b + 10, 2)

            def softmax_exp(p_tile, g, slot):
                act.wait_ge(dve_done, at("dve", f"nm {g}"))
                for e in range(2):
                    for t, (o, w) in enumerate(SPAN):
                        v = p_tile[:, 2 * slot + e, o:o + w]
                        k = 2 * e + t
                        last = nc.scalar.activation(v, v, ACT.Exp, bias=NM[:, g, k:k + 1], scale=-1.0, accum_out=DEN[:, g, k:k + 1])
                last.then_inc(act_done, done("act", f"exp {g}"))

            def turned_out(g):
                act.wait_ge(pe_done, at("pe", f"tr {g}"))
                for e in range(2):
                    last = nc.scalar.activation(PT[:, e, :], ps[:, 5 + e, 0:CAUSAL], ACT.Copy)
                last.then_inc(act_done, done("act", f"pt {g}"))

            def heads_out(name, chunk):
                act.wait_ge(pe_done, at("pe", f"pv {name}"))
                nc.scalar.activation(BH[:, chunk, :], ps[:, 7, 0:T], ACT.Copy).then_inc(act_done, done("act", f"bh {chunk}"))

            def evac1(l, u):
                if u < BR1:
                    unit_out(1, l, 11 + u // 3, u % 3)
                bank = ps[:, u % 3, :]
                if u in (U_GATE, V_GATE):
                    ins = nc.scalar.activation((UT if u == U_GATE else VG)[:, :, :], bank.rearrange("p (a t) -> p a t", a=2), ACT.Gelu_apprx_tanh)
                elif u == POOL_U:
                    act.wait_ge(pool_done, at("pool", "pads"))
                    ins = nc.scalar.activation(PZ[:, :, 16:16 + T], bank.rearrange("p (a t) -> p a t", a=2), ACT.Copy)
                elif u in (Q_U, K_U, V_U, IDX_U, CONV_A):
                    dst = {Q_U: QT, K_U: KT, V_U: VT, IDX_U: QKI, CONV_A: CA}[u]
                    ins = nc.scalar.activation(dst, bank.rearrange("p (a t) -> p a t", a=2), ACT.Copy)
                    if u == IDX_U:
                        ins = nc.scalar.activation(WI.rearrange("p a b -> p (a b)"), ps[:, 7, 0:8], ACT.Copy, scale=0.5)
                elif u == CONV_G:
                    ins = nc.scalar.activation(SG, bank.rearrange("p (a t) -> p a t", a=2), ACT.Sigmoid)
                elif u < BR1:
                    k = 2 * (u - GATES1)
                    ins = nc.scalar.activation(G[:, k:k + 2, :], bank.rearrange("p (a t) -> p a t", a=2), ACT.Sigmoid)
                else:
                    return
                ins.then_inc(act_done, done("act", f"ev {u}"))

            def side1(l, work):
                if work == "gm1":
                    act.wait_ge(dve_done, at("dve", "b0"))
                    nc.scalar.activation(BH[:, 0:2, :], BT, ACT.Copy).then_inc(act_done, done("act", "bh b0"))
                elif work == "pool1":
                    act.wait_ge(pe_done, at("pe", "pw"))
                    act.wait_ge(dve_done, at("dve", "bl b0"))
                    for c in range(2):
                        ins = nc.scalar.activation(BT[:, c, :], ps[:, 3, T * c:T * c + T], ACT.Copy, scale=vec[:, V1_PS + c:V1_PS + c + 1])
                    ins.then_inc(act_done, done("act", "b1"))
                    act.wait_ge(act_done, at("act", "b1"))
                    nc.scalar.activation(BH[:, 2:4, :], BT, ACT.Copy).then_inc(act_done, done("act", "bh b1"))
                elif work[:3] == "idx":
                    t = int(work[4:])
                    o, w = SPAN[t]
                    act.wait_ge(pe_done, at("pe", work))
                    for h in range(4):
                        if h >= 2 or t:
                            act.wait_ge(dve_done, at("dve", f"score {t} {h - 2}" if h >= 2 else f"score 0 {h + 2}"))
                        nc.scalar.activation(REL[:, h % 2, 0:w], ps[:, 3 + h, 0:w], ACT.Relu, scale=32 ** -0.5)\
                            .then_inc(act_done, done("act", f"rel {t} {h}"))
                elif work == "ln1":
                    act.wait_ge(dve_done, at("dve", "xc"))
                    act.wait_ge(dve_done, at("dve", "bl b1"))
                    nc.scalar.activation(BT, ACC, ACT.Square).then_inc(act_done, done("act", "xcsq"))
                elif work == "gm0":
                    act.wait_ge(dve_done, at("dve", "gm ms"))
                    nc.scalar.activation(ms[:, 2:4], ms[:, 0:2], ACT.Sqrt).then_inc(act_done, done("act", "gm root"))
                elif work == "ln2":
                    root("ln", 6)
                elif work == "ln3":
                    act.wait_ge(dve_done, at("dve", "lnx"))
                    for c in range(2):
                        ins = nc.scalar.activation(BT[:, c, :], ACC[:, c, :], ACT.Silu, bias=vec[:, V1_LB + c:V1_LB + c + 1],
                                                   scale=vec[:, V1_LG + c:V1_LG + c + 1])
                    ins.then_inc(act_done, done("act", "b3"))
                    act.wait_ge(act_done, at("act", "b3"))
                    nc.scalar.activation(BH[:, 6:8, :], BT, ACT.Copy).then_inc(act_done, done("act", "bh b3"))
                elif work[:2] == "qk":
                    softmax_exp(P1, int(work[3:]), int(work[3:]))
                elif work[:2] == "tr":
                    turned_out(int(work[3:]))
                elif work[:2] == "pv":
                    heads_out(work[3:], 4 + int(work[3:]))

            def evac2(l, u):
                if u < BR2 and u not in (W1_U, W1_U + 1):
                    unit_out(2, l, 11 + u // 3, u % 3)
                bank = ps[:, u % 3, :]
                pair = bank.rearrange("p (a t) -> p a t", a=2)
                if u in ROPED:
                    if u in ROPED[2:]:
                        act.wait_ge(dve_done, at("dve", f"rope {({3: 1, 4: 0, 5: 3})[u]}"))
                    ins = nc.scalar.activation(Z[:, u % 2], pair, ACT.Copy)
                elif u == VG_U:
                    v = bank[:, 0:280].rearrange("p (a t) -> p a t", a=2)
                    nc.scalar.activation(VSW, v, ACT.Copy)
                    ins = nc.scalar.activation(GT, v[:, :, 128:140], ACT.Sigmoid)
                elif u in (FQK_U, FQK_U + 1, FQK_U + 2):
                    ins = nc.scalar.activation(FQK[:, 2 * (u - FQK_U):2 * (u - FQK_U) + 2, :], pair, ACT.Copy)
                elif u == DV_U or u == FV_U:
                    ins = nc.scalar.activation((DV if u == DV_U else FV)[:, :, 0:T], pair, ACT.Copy)
                elif u == DVF_U:
                    for t in range(2):
                        src = (bank, ps[:, 6, :])[t]
                        nc.scalar.activation(DV[:, t, T:T + P], src[:, 0:P], ACT.Copy)
                        nc.scalar.activation(FV[:, t, T:T + P], src[:, P:T], ACT.Copy)
                        ins = nc.scalar.activation(FL[:, t, 0:6], src[:, T:T + 6], ACT.Copy)
                elif GATES2 <= u < BR2:
                    k = 2 * (u - GATES2)
                    ins = nc.scalar.activation(G2[:, k:k + 2, :], pair, ACT.Sigmoid)
                else:
                    return
                ins.then_inc(act_done, done("act", f"ev {u}"))

            def side2(l, work):
                what, _, g = work.partition(" ")
                if work == "dup":
                    act.wait_ge(pe_done, at("pe", "dup"))
                    nc.scalar.activation(KSD, ps[:, 3, :].rearrange("p (a t) -> p a t", a=2), ACT.Copy).then_inc(act_done, done("act", "ksd"))
                elif work == "ke":
                    act.wait_ge(dve_done, at("dve", "ke"))
                    nc.scalar.activation(BH[:, 6:8, :], KE, ACT.Copy).then_inc(act_done, done("act", "keh"))
                elif work == "lf":
                    act.wait_ge(dve_done, at("dve", "fx"))
                    nc.scalar.activation(LE[:, :, 0:6], LF[:, :, 0:6], ACT.Abs).then_inc(act_done, done("act", "fabs"))
                    act.wait_ge(act_done, at("act", "fabs"))
                    nc.scalar.activation(LE[:, :, 0:6], LE[:, :, 0:6], ACT.Exp, scale=-1.0).then_inc(act_done, done("act", "fexp"))
                    act.wait_ge(dve_done, at("dve", "fexp1"))
                    nc.scalar.activation(LE[:, :, 0:6], LE[:, :, 0:6], ACT.Ln).then_inc(act_done, done("act", "fln"))
                elif work == "fox":
                    act.wait_ge(pe_done, at("pe", "fox"))
                    nc.scalar.activation(CT, ps[:, 7, 0:16].rearrange("p (a b) -> p a b", a=2), ACT.Copy)
                    for k, b in enumerate((3, 4)):
                        nc.scalar.activation(CS[:, 2 * k:2 * k + 2, :], ps[:, b, :].rearrange("p (a t) -> p a t", a=2), ACT.Copy)
                    for k in range(2):
                        ins = nc.scalar.activation(CS[:, 4 + k, :], ps[:, 5 + k, 0:T], ACT.Copy)
                    ins.then_inc(act_done, done("act", "cs"))
                elif work == "hid":
                    unit_out(2, l, 11 + (W1_U + 1) // 3, (W1_U + 1) % 3)
                    for kv in range(2):
                        ins = nc.scalar.activation(HID[:, kv, :], ps[:, kv, 0:16], ACT.Silu)
                    ins.then_inc(act_done, done("act", "hid"))
                elif work == "w2":
                    act.wait_ge(pe_done, at("pe", "w2"))
                    nc.scalar.activation(KC2, ps[:, 3, 384:400], ACT.Copy)
                    nc.scalar.activation(VC2[0:16], ps[0:16, 4, 384:448], ACT.Copy).then_inc(act_done, done("act", "w2"))
                elif work == "cqk":
                    act.wait_ge(dve_done, at("dve", "cnm"))
                    nc.scalar.activation(PC, PC, ACT.Exp, scale=0.125).then_inc(act_done, done("act", "cexp"))
                elif work == "ctr":
                    act.wait_ge(pe_done, at("pe", "ctr"))
                    for e in range(2):
                        ins = nc.scalar.activation(PTC[0:16, 2 * e:2 * e + 2, :], ps[0:16, 5 + e, :].rearrange("p (a t) -> p a t", a=2), ACT.Copy)
                    ins.then_inc(act_done, done("act", "ptc"))
                elif what == "qk":
                    k = GROUPS2.index(g)
                    softmax_exp(P2, k, k % 3)
                    if g == "d2":
                        act.wait_ge(dve_done, at("dve", "dmax"))
                        nc.scalar.activation(DE[:, 0, :], DE[:, 0, :], ACT.Exp).then_inc(act_done, done("act", "dexp"))
                elif what == "tr":
                    turned_out(GROUPS2.index(g))
                elif what == "pv" and g in CHUNK2:
                    heads_out(GROUPS2.index(g), CHUNK2[g])

            def gated_parts():
                for b in range(4):
                    act.wait_ge(dve_done, at("dve", f"y {b}"))
                    nc.scalar.activation(NH[:, 2 * b:2 * b + 2, :], T8[:, 2 * b:2 * b + 2, :], ACT.Copy).then_inc(act_done, done("act", f"yh {b}"))

            m.section = "setup"
            act.wait_ge(pe_done, at("pe", "vec0"))
            nc.scalar.activation(vec0, ps[:, 0, 0:16], ACT.Copy).then_inc(act_done, done("act", "vec0"))
            act.wait_ge(act_done, at("act", "vec0"))
            nc.scalar.activation(cond, vec0[:, 0:8], ACT.Silu)
            act.wait_ge(pe_done, at("pe", "bias rows"))
            nc.scalar.activation(bias_rows.rearrange("p a b -> p (a b)")[0:4], ps[0:4, 1, :], ACT.Copy).then_inc(act_done, done("act", "bias rows"))
            act.wait_ge(pe_done, at("pe", "xT"))
            for b in range(4):
                ins = nc.scalar.activation(XT[:, 2 * b:2 * b + 2, :].rearrange("p a t -> p (a t)"), ps[:, 4 + b, :], ACT.Copy)
            ins.then_inc(act_done, done("act", "XT"))
            act.wait_ge(act_done, at("act", "XT"))
            act.wait_ge(pool_done, at("pool", "eps"))
            squares("next", None)
            act.wait_ge(pe_done, at("pe", "TB"))
            for h in range(4):
                ins = nc.scalar.activation(TB[:, h, :], ps[:, h, 0:CAUSAL], ACT.Copy, scale=8.0)
            ins.then_inc(act_done, done("act", "TB"))

            for block in (1, 2):
                m.section = f"block{block}"
                with act.Fori(0, DEPTH) as l:
                    m.layer = l
                    act.wait_ge(pe_done, at("pe", "vec"))
                    n = V1_N if block == 1 else V2_N
                    nc.scalar.activation(vec[:, 0:n], ps[:, 1, 0:n], ACT.Copy).then_inc(act_done, done("act", "vec"))
                    split_hi(block, l, 0, 0)
                    if block == 2:
                        act.wait_ge(dve_done, at("dve", "gains"))
                    F = ((block - 1) * DEPTH + l) * 2
                    shifts = (None, None, None) if block == 1 else (0, 24, 48)
                    pre("pre1", shifts[0])
                    split_hi(block, l, 0, 1)
                    ffn(block, l, 0, F, False)
                    if block == 1:
                        post("post1")
                    squares("prem", "x1")
                    pre("prem", shifts[1])
                    for u in range(UNITS):
                        p = u + 2
                        split_hi(block, l, 11 + p // 3, p % 3, UNITS + p)
                        (evac1 if block == 1 else evac2)(l, u)
                        for work in (SIDE1 if block == 1 else SIDE2).get(u, ()):
                            settle()
                            (side1 if block == 1 else side2)(l, work)
                        if u == (BR1 + 3 if block == 1 else BR2 + 2):
                            gated_parts()
                    unit_out(block, l, 21, 2)
                    if block == 1:
                        post("postm")
                    squares("pre2", "xm")
                    pre("pre2", shifts[2])
                    ffn(block, l, 22, F + 1, True)
                    if block == 1:
                        post("post2")
                    squares("next", "x2")
            m.section = "end"
            act.wait_ge(pe_done, at("pe", "out"))
            for b in range(8):
                ins = nc.scalar.activation(XT[:, b, :], ps[:, b, 0:T], ACT.Copy)
            ins.then_inc(act_done, done("act", "out"))

        @block_.vector
        def _(dve):
            def mine(what):
                dve.wait_ge(dve_done, at("dve", what))

            def settle():
                mine(m.newest["dve"])

            def take_wait():
                nc.vector.memset(tick[:, 0:1], 0.0)

            def split_lo(block, l, q, s, pos=0):
                dve.wait_ge(hi_ready, unit_number(block, l, 3 * q + s) + 1)
                for (dst, src), (part, _) in zip(split_pieces(block, pos, s, lo), split_pieces(block, pos, s, hi)):
                    last = nc.vector.tensor_tensor(dst, src, part.bitcast(F32), ALU.subtract)
                last.then_inc(lo_ready, 1)

            def inverse_root(name, v, plus, r, root, step):
                dve.wait_ge(act_done, at("act", name + " root"))
                nc.vector.reciprocal(r, root).then_inc(dve_done, done("dve", name + " recip"))
                mine(name + " recip")
                nc.vector.scalar_tensor_tensor(out=step, in0=v, scalar=plus, in1=r, op0=ALU.add, op1=ALU.mult).then_inc(dve_done, done("dve", name + " vr"))
                mine(name + " vr")
                nc.vector.scalar_tensor_tensor(out=step, in0=step, scalar=-0.5, in1=r, op0=ALU.mult, op1=ALU.mult)\
                    .then_inc(dve_done, done("dve", name + " vrr"))
                mine(name + " vrr")
                nc.vector.scalar_tensor_tensor(out=r, in0=step, scalar=1.5, in1=r, op0=ALU.add, op1=ALU.mult)\
                    .then_inc(dve_done, done("dve", name + " rstd"))
                mine(name + " rstd")

            def mean_square(name, bank=3):
                inverse_root(name, ps[:, bank, 0:T], EPS, rms[:, 1, :], rms[:, 0, :], rms[:, 2, :])

            def pre(name, gain, shift):

                def scaled(c):
                    nc.vector.scalar_tensor_tensor(out=T8[:, c, :], in0=XT[:, c, :], scalar=gain[:, c:c + 1], in1=rms[:, 1, :],
                                                   op0=ALU.mult, op1=ALU.mult).then_inc(dve_done, done("dve", f"{name} n{c}"))

                scaled(0)
                for c in range(C):
                    if c + 1 < C:
                        scaled(c + 1)
                    dve.wait_ge(act_done, at("act", f"{name} h{c}"))
                    part = NH[:, c, :].bitcast(F32)
                    if shift is None:
                        ins = nc.vector.tensor_tensor(NL[:, c, :], T8[:, c, :], part, ALU.subtract)
                    else:
                        ins = nc.vector.scalar_tensor_tensor(out=NL[:, c, :], in0=T8[:, c, :], scalar=modl[:, shift + c:shift + c + 1],
                                                             in1=part, op0=ALU.add, op1=ALU.subtract)
                    ins.then_inc(dve_done, done("dve", f"{name} l{c}"))

            def post(name, gain, x):
                mean_square(name)

                def scaled(b):
                    for c in (2 * b, 2 * b + 1):
                        ins = nc.vector.scalar_tensor_tensor(out=T8[:, c, :], in0=ps[:, 4 + b, T * (c % 2):T * (c % 2) + T],
                                                             scalar=gain[:, c:c + 1], in1=rms[:, 1, :], op0=ALU.mult, op1=ALU.mult)
                    ins.then_inc(dve_done, done("dve", f"{name} n{b}"))

                scaled(0)
                for b in range(4):
                    if b < 3:
                        scaled(b + 1)
                    mine(f"{name} n{b}")
                    pair = XT[:, 2 * b:2 * b + 2, :]
                    nc.vector.tensor_tensor(pair, pair, T8[:, 2 * b:2 * b + 2, :], ALU.add).then_inc(dve_done, done("dve", f"{x} {b}"))
                mine(x + " 3")

            def gated_add(gate, x):
                for c in range(C):
                    ins = nc.vector.scalar_tensor_tensor(out=XT[:, c, :], in0=ps[:, 4 + c // 2, T * (c % 2):T * (c % 2) + T],
                                                         scalar=gate[:, c:c + 1], in1=XT[:, c, :], op0=ALU.mult, op1=ALU.add)
                    if c % 2:
                        ins.then_inc(dve_done, done("dve", f"{x} {c // 2}"))
                mine(x + " 3")

            def gate_times_up(F, f, bank, par):
                dve.wait_ge(silu_ready, NF * F + f + 1)
                if not isinstance(f, int) or f >= 2:
                    dve.wait_ge(hidden_lo, NF * F + f - 1)
                nc.vector.tensor_tensor(HF[:, par, :], SA[:, par, :], ps[:, bank, T:2 * T], ALU.mult).then_inc(hidden_ready, 1)

            def hidden_parts(F, f):
                for k in range(2):
                    dve.wait_ge(hidden_hi, NF * F + f + k + 1)
                    nc.vector.tensor_tensor(BL[:, k, :], HF[:, k, :], BH[:, k, :].bitcast(F32), ALU.subtract).then_inc(hidden_lo, 1)

            def ada_column(a):
                dve.wait_ge(ada_in[0], 16 * (a + 1))
                for c in range(C):
                    if c == 0:
                        ins = nc.vector.tensor_scalar(acc_ada[:, 0:ADA_V], ADW[0][:, c, :], cond[:, 0:1], None, ALU.mult)
                    else:
                        dve.wait_ge(ada_step, 7 * a + c)
                        ins = nc.vector.scalar_tensor_tensor(out=acc_ada[:, 0:ADA_V], in0=ADW[0][:, c, :], scalar=cond[:, c:c + 1],
                                                             in1=acc_ada[:, 0:ADA_V], op0=ALU.mult, op1=ALU.add)
                    ins.then_inc(ada_step if c < C - 1 else ada_sum[0], 1)

            def ffn(block, l, b, F, last_of_layer, half):
                split_lo(block, l, b, 2)
                gate_times_up(F, 0, 0, 0)
                split_lo(block, l, b + 1, 0)
                gate_times_up(F, 1, 1, 1)
                hidden_parts(F, 0)

                def body(i, more):
                    a = 18 * l + 9 * half + i - 1
                    split_lo(block, l, b + i, 1)
                    gate_times_up(F, 2 * i, 2, 0)
                    if block == 1 and not (isinstance(i, int) and i == 1):
                        dve.wait_ge(ada_out, a + 1)
                        nc.vector.tensor_copy(mods.rearrange("p a b -> p (a b)")[:, bass.ds(4 * a - 4, 4)], ps[:, 1, 0:4]).then_inc(ada_kept, 1)
                    if more != -1 and block == 1:
                        ada_column(a)
                    split_lo(block, l, b + i, 2)
                    gate_times_up(F, 2 * i + 1, 0, 1)
                    if not (last_of_layer and more == -1):
                        split_lo(block, l, b + i + 1, 0)
                    hidden_parts(F, 2 * i)

                body(1, 0)
                with dve.Fori(2, NF // 2 - 1) as i:
                    body(i, 0)
                body(NF // 2 - 1, -1)
                if not last_of_layer:
                    split_lo(block, l, b + 11, 1, b * 3 + UNITS + 1)
                if block == 2:
                    dve.wait_ge(unit_used, unit_number(block, l, 3 * (b + 10) + 2) + 4)

            def negated_logits(p_tile, g, slot, masks, by_head=None):
                dve.wait_ge(pe_done, at("pe", f"qk {g}"))
                if by_head is None:
                    take_wait()
                else:
                    for e in range(2):
                        last = nc.vector.tensor_tensor(p_tile[:, 2 * slot + e, :], ps[:, 3 + e, 0:CAUSAL], by_head(e), ALU.add)
                    last.then_inc(dve_done, done("dve", f"biased {g}"))
                    mine(f"biased {g}")
                    take_wait()
                for e in range(2):
                    for t, (o, w) in enumerate(SPAN):
                        v = p_tile[:, 2 * slot + e, o:o + w]
                        scores = ps[:, 3 + e, o:o + w] if by_head is None else v
                        k = 2 * e + t
                        last = nc.vector.tensor_tensor_reduce(v, scores, masks(e)[:, o:o + w], -0.125, 3e38, ALU.add, ALU.min, NM[:, g, k:k + 1])
                last.then_inc(dve_done, done("dve", f"nm {g}"))

            def factor(g, gate=None):
                dve.wait_ge(act_done, at("act", f"exp {g}"))
                if gate is None:
                    nc.vector.reciprocal(FAC[:, g, :], DEN[:, g, :]).then_inc(dve_done, done("dve", f"factor {g}"))
                else:
                    nc.vector.reciprocal(FAC[:, g, :], DEN[:, g, :]).then_inc(dve_done, done("dve", f"recip {g}"))
                    mine(f"recip {g}")
                    nc.vector.tensor_tensor(window(FAC[:, g, :], [[2, 2], [1, 2]]), window(FAC[:, g, :], [[2, 2], [1, 2]]), gate, ALU.mult)\
                        .then_inc(dve_done, done("dve", f"factor {g}"))

            def heads_rest(chunk):
                dve.wait_ge(act_done, at("act", f"bh {chunk}"))
                nc.vector.tensor_tensor(BL[:, chunk, :], ps[:, 7, 0:T], BH[:, chunk, :].bitcast(F32), ALU.subtract)\
                    .then_inc(dve_done, done("dve", f"bl {chunk}"))

            def branch_rest(k):
                dve.wait_ge(act_done, at("act", f"bh b{k}"))
                nc.vector.tensor_tensor(BL[:, 2 * k:2 * k + 2, :], BT, BH[:, 2 * k:2 * k + 2, :].bitcast(F32), ALU.subtract)\
                    .then_inc(dve_done, done("dve", f"bl b{k}"))

            def side1(l, work):
                what, _, g = work.partition(" ")
                if work == "gm0":
                    dve.wait_ge(act_done, at("act", f"ev {V_GATE}"))
                    take_wait()
                    for t in range(2):
                        last = nc.vector.tensor_tensor_reduce(PD[:, t, :], VG[:, t, :], VG[:, t, :], 1.0, 0.0, ALU.mult, ALU.add, ms[:, t:t + 1])
                    last.then_inc(dve_done, done("dve", "gm sum"))
                    mine("gm sum")
                    nc.vector.tensor_scalar(ms[:, 0:2], ms[:, 0:2], 1.0 / 256, EPS, ALU.mult, ALU.add).then_inc(dve_done, done("dve", "gm ms"))
                    dve.wait_ge(pe_done, at("pe", "wsT"))
                    nc.vector.tensor_tensor(WST, ps[:, 3, :].rearrange("p (g t) -> p g t", g=4), spread(tri[:, 0:P], 1, 4), ALU.mult)\
                        .then_inc(dve_done, done("dve", "WST"))
                    inverse_root("gm", ms[:, 0:2], 0.0, ms[:, 4:6], ms[:, 2:4], ms[:, 6:8])
                    for t in range(2):
                        last = nc.vector.scalar_tensor_tensor(out=VG[:, t, :], in0=VG[:, t, :], scalar=ms[:, 4 + t:5 + t], in1=BG,
                                                              op0=ALU.mult, op1=ALU.mult)
                    last.then_inc(dve_done, done("dve", "VN"))
                elif work == "gm1":
                    dve.wait_ge(pe_done, at("pe", "mixed"))
                    for c in range(2):
                        last = nc.vector.tensor_tensor(BT[:, c, :].rearrange("p (a t) -> p a t", a=2), ps[:, 3, T * c:T * c + T].rearrange("p (a t) -> p a t", a=2),
                                                       spread(GB[:, c, :], 1, 2), ALU.add)
                    last.then_inc(dve_done, done("dve", "mixed"))
                    mine("mixed")
                    nc.vector.tensor_tensor(BT, BT, UT, ALU.mult).then_inc(dve_done, done("dve", "b0"))
                    branch_rest(0)
                elif work == "pool0":
                    dve.wait_ge(act_done, at("act", f"ev {POOL_U}"))
                    A, B, n = SC, WK, 16 + T
                    for k, (dst, src, w, c) in enumerate(((A, PZ, 1, 0), (B, A, 2, 0), (A, B, 4, 1), (B, A, 8, 1))):
                        lo_x = 2 * w - 1
                        nc.vector.tensor_tensor(dst[:, c:2, lo_x:n], src[:, c:2, lo_x:n], src[:, c:2, lo_x - w:n - w], ALU.add)\
                            .then_inc(dve_done, done("dve", f"window {k}"))
                        mine(f"window {k}")
                    for k, W in enumerate((A, B)):
                        rows = slice(64 * k, 64 * k + 64)
                        last = nc.vector.tensor_tensor(PD[rows], W[rows, :, 16:n], RC[rows], ALU.mult)
                    last.then_inc(dve_done, done("dve", "means"))
                    mine("means")
                    nc.vector.tensor_tensor(PD, PD, PZ[:, :, 16:n], ALU.subtract).then_inc(dve_done, done("dve", "pd"))
                elif work == "pool1":
                    branch_rest(1)
                elif what == "idx":
                    t = int(g)
                    o, w = SPAN[t]
                    for h in range(4):
                        dve.wait_ge(act_done, at("act", f"rel {t} {h}"))
                        if h == 0:
                            if t == 0:
                                mine("pd")
                            ins = nc.vector.tensor_scalar(SCf[:, o:o + w], REL[:, 0, 0:w], WI[:, t, 0:1], None, ALU.mult)
                        else:
                            mine(f"score {t} {h - 1}")
                            ins = nc.vector.scalar_tensor_tensor(out=SCf[:, o:o + w], in0=REL[:, h % 2, 0:w], scalar=WI[:, t, h:h + 1],
                                                                 in1=SCf[:, o:o + w], op0=ALU.mult, op1=ALU.add)
                        ins.then_inc(dve_done, done("dve", f"score {t} {h}"))
                    mine(f"score {t} 3")
                    nc.vector.tensor_tensor(WKf[:, o:o + w], SCf[:, o:o + w], causal[:, o:o + w], ALU.add).then_inc(dve_done, done("dve", f"scores {t}"))
                elif work == "convh":
                    dve.wait_ge(act_done, at("act", f"ev {CONV_G}"))
                    dve.wait_ge(pool_done, at("pool", "pads"))
                    nc.vector.tensor_tensor(CH[:, :, 30:30 + T], CA, SG, ALU.mult).then_inc(dve_done, done("dve", "convh"))
                elif what == "top":
                    j = int(g)
                    mine(f"taken {j - 1}" if j else "scores 1")
                    take_wait()
                    for t, (o, w) in enumerate(SPAN):
                        last = nc.vector.max(M8[:, t, :], WKf[:, o:o + w])
                    last.then_inc(dve_done, done("dve", f"best {j}"))
                    mine(f"best {j}")
                    take_wait()
                    for t, (o, w) in enumerate(SPAN):
                        last = nc.vector.match_replace(WKf[:, o:o + w], M8[:, t, :], WKf[:, o:o + w], TAKEN)
                    last.then_inc(dve_done, done("dve", f"taken {j}"))
                    if j == 7:
                        mine("taken 7")
                        nc.vector.tensor_scalar(SM, WKf[:, 0:CAUSAL], -2e38, NEG, ALU.is_ge, ALU.mult).then_inc(dve_done, done("dve", "not taken"))
                        mine("not taken")
                        nc.vector.tensor_tensor(SM, SM, causal, ALU.add).then_inc(dve_done, done("dve", "SM"))
                        mine("SM")
                elif what == "tap":
                    j = int(g)
                    for tap in range(4 * j, min(4 * j + 4, 31)):
                        mine(f"tap {tap - 1}" if tap else "convh")
                        for c in range(2):
                            w = vec[:, V1_DW + 2 * tap + c:V1_DW + 2 * tap + c + 1]
                            if tap == 0:
                                last = nc.vector.tensor_scalar(ACC[:, c, :], CH[:, c, 0:T], w, vec[:, V1_CB + c:V1_CB + c + 1], ALU.mult, ALU.add)
                            else:
                                last = nc.vector.scalar_tensor_tensor(out=ACC[:, c, :], in0=CH[:, c, tap:tap + T], scalar=w,
                                                                      in1=ACC[:, c, :], op0=ALU.mult, op1=ALU.add)
                        last.then_inc(dve_done, done("dve", f"tap {tap}"))
                elif work == "ln1":
                    dve.wait_ge(pe_done, at("pe", "lnmean"))
                    nc.vector.tensor_tensor(ACC, ACC, spread(ps[:, 5, 0:T], 1, 2), ALU.subtract).then_inc(dve_done, done("dve", "xc"))
                elif work == "ln2":
                    mean_square("ln", 6)
                    nc.vector.tensor_tensor(ACC, ACC, spread(rms[:, 1, :], 1, 2), ALU.mult).then_inc(dve_done, done("dve", "lnx"))
                elif work == "ln3":
                    branch_rest(3)
                elif what == "qk":
                    k = int(g)
                    negated_logits(P1, k, k, lambda e: SM, lambda e: TB[:, 2 * k + e, :])
                    factor(k)
                elif what == "pv":
                    heads_rest(4 + int(g))

            def side2(l, work):
                what, _, g = work.partition(" ")
                if work[:4] == "rope":
                    u = int(work[4:])
                    dve.wait_ge(pe_done, at("pe", f"swap {u}"))
                    nc.vector.tensor_tensor(RT[:, 0], Z[:, u % 2], spread(ROPE[:, 0, :], 1, 2), ALU.mult)
                    nc.vector.tensor_tensor(RT[:, 1], ps[:, 4, :].rearrange("p (a t) -> p a t", a=2), spread(ROPE[:, 1, :], 1, 2), ALU.mult)\
                        .then_inc(dve_done, done("dve", f"parts {u}"))
                    mine(f"parts {u}")
                    if u == KV_U:
                        nc.vector.tensor_tensor(KVC[0:64, 0:T], RT[0:64, 0, 0, :], RT[0:64, 1, 0, :], ALU.add)
                        nc.vector.tensor_copy(KVC[64:128, 0:T], Z[64:128, u % 2, 0, :])
                        ins = nc.vector.tensor_tensor(KSW, RT[:, 0, 1, :], RT[:, 1, 1, :], ALU.add)
                    else:
                        dst = NQ if u == NQ_U else DQK[:, 2 * (u - DQK_U):2 * (u - DQK_U) + 2, :]
                        ins = nc.vector.tensor_tensor(dst, RT[:, 0], RT[:, 1], ALU.add)
                    ins.then_inc(dve_done, done("dve", f"rope {u}"))
                    mine(f"rope {u}")
                elif work == "ke":
                    dve.wait_ge(pool_done, at("pool", "pads"))
                    nc.vector.tensor_tensor(window(KE, [[16, 32], [1, 16]]), window(KVC, [[1, 32], [16, 16]]), window(vec[:, V2_PE:V2_N], [[1, 32], [0, 16]]), ALU.add)\
                        .then_inc(dve_done, done("dve", "ke"))
                    dve.wait_ge(act_done, at("act", "keh"))
                    nc.vector.tensor_tensor(BL[:, 6:8, :], KE, BH[:, 6:8, :].bitcast(F32), ALU.subtract).then_inc(dve_done, done("dve", "kel"))
                elif work == "lf":
                    dve.wait_ge(act_done, at("act", f"ev {DVF_U}"))
                    nc.vector.tensor_tensor(LF[:, :, 0:6], FL[:, :, 0:6], spread(FB[:, 0:6], 1, 2), ALU.add).then_inc(dve_done, done("dve", "fx"))
                    dve.wait_ge(act_done, at("act", "fexp"))
                    nc.vector.tensor_scalar(LE[:, :, 0:6], LE[:, :, 0:6], 1.0, None, ALU.add).then_inc(dve_done, done("dve", "fexp1"))
                    nc.vector.tensor_scalar(FL[:, :, 0:6], LF[:, :, 0:6], 0.0, -8.0, ALU.min, ALU.mult).then_inc(dve_done, done("dve", "fmin"))
                    mine("fmin")
                    dve.wait_ge(act_done, at("act", "fln"))
                    nc.vector.scalar_tensor_tensor(out=LF[:, :, 0:6], in0=LE[:, :, 0:6], scalar=8.0, in1=FL[:, :, 0:6], op0=ALU.mult, op1=ALU.add)\
                        .then_inc(dve_done, done("dve", "lf"))
                    mine("lf")
                    for h in range(6):
                        last = nc.vector.tensor_copy(LFB[:, h], spread(LF[:, :, h], 2, P))
                    last.then_inc(dve_done, done("dve", "lfb"))
                elif work == "cqk":
                    dve.wait_ge(pe_done, at("pe", "cqk"))
                    for e in range(2):
                        last = nc.vector.tensor_tensor(window(PC[:, 4 * e, :], [[32, 2], [16, 2], [1, 16]]), window(ps[:, 3 + e, 384:448], [[32, 2], [16, 2], [1, 16]]),
                                                       window(CMK[:, 0, :], [[0, 2], [16, 2], [1, 16]]), ALU.add)
                    last.then_inc(dve_done, done("dve", "cadd"))
                    mine("cadd")
                    nc.vector.tensor_reduce(CN[:, 0, :], PC, AX.X, ALU.max).then_inc(dve_done, done("dve", "cmax"))
                    mine("cmax")
                    nc.vector.tensor_tensor(PC, PC, spread(CN[:, 0, :], 2, 16), ALU.subtract).then_inc(dve_done, done("dve", "cnm"))
                    dve.wait_ge(act_done, at("act", "cexp"))
                    for e in range(2):
                        last = nc.vector.tensor_tensor(window(PC[:, 4 * e, :], [[32, 2], [16, 2], [1, 16]]), window(PC[:, 4 * e, :], [[32, 2], [16, 2], [1, 16]]),
                                                       window(CMB[:, 0, :], [[0, 2], [16, 2], [1, 16]]), ALU.mult)
                    last.then_inc(dve_done, done("dve", "ckeep"))
                    mine("ckeep")
                    nc.vector.tensor_reduce(CN[:, 1, :], PC, AX.X, ALU.add).then_inc(dve_done, done("dve", "csum"))
                    mine("csum")
                    nc.vector.tensor_scalar(CN[:, 1, :], CN[:, 1, :], 1.0, None, ALU.max).then_inc(dve_done, done("dve", "cden"))
                    mine("cden")
                    nc.vector.reciprocal(CN[:, 2, :], CN[:, 1, :]).then_inc(dve_done, done("dve", "crec"))
                    mine("crec")
                    nc.vector.tensor_tensor(window(CN[:, 2, :], [[4, 2], [2, 2], [1, 2]]), window(CN[:, 2, :], [[4, 2], [2, 2], [1, 2]]),
                                            window(GT[:, 0, :], [[3, 2], [6, 2], [12, 2]]), ALU.mult).then_inc(dve_done, done("dve", "cfac"))
                    mine("cfac")
                    nc.vector.tensor_tensor(PC, PC, spread(CN[:, 2, :], 2, 16), ALU.mult).then_inc(dve_done, done("dve", "pc"))
                elif what == "qk":
                    k = GROUPS2.index(g)
                    j = int(g[1])
                    if g[0] == "f":
                        if j == 0:
                            dve.wait_ge(act_done, at("act", "cs"))
                        for e in range(2):
                            for t, (o, w) in enumerate(SPAN):
                                h = 2 * j + e
                                last = nc.vector.scalar_tensor_tensor(out=FM[:, e, o:o + w], in0=CS[:, h, 0:w], scalar=CT[:, t, h:h + 1],
                                                                      in1=causal[:, o:o + w], op0=ALU.subtract, op1=ALU.add)
                        last.then_inc(dve_done, done("dve", f"decay {g}"))
                        mine(f"decay {g}")
                    masks = {"d": lambda e: DM[:, j, :], "s": lambda e: causal, "w": lambda e: causal, "f": lambda e: FM[:, e, :]}[g[0]]
                    negated_logits(P2, k, k % 3, masks)
                    if g[0] in "sw":
                        factor(k, window(GT[:, 0, 6 * j + "sw".index(g[0]) + 1:], [[3, 2], [12, 2]]))
                    elif g[0] == "f":
                        factor(k)
                    elif g == "d2":
                        nm, den = NM[:, 0:3, :], DEN[:, 0:3, :]
                        mine("nm 2")
                        nc.vector.tensor_tensor(D4[:, 0, :], NM[:, 0, :], NM[:, 1, :], ALU.min).then_inc(dve_done, done("dve", "dmin0"))
                        mine("dmin0")
                        nc.vector.tensor_tensor(D4[:, 0, :], D4[:, 0, :], NM[:, 2, :], ALU.min).then_inc(dve_done, done("dve", "dmin"))
                        mine("dmin")
                        de = window(DE[:, 0, :], [[4, 3], [1, 4]])
                        nc.vector.tensor_tensor(de, spread(D4[:, 0, :], 1, 3), nm, ALU.subtract).then_inc(dve_done, done("dve", "dmax"))
                        dve.wait_ge(act_done, at("act", "dexp"))
                        nc.vector.tensor_tensor(window(DE[:, 1, :], [[4, 3], [1, 4]]), de, den, ALU.mult).then_inc(dve_done, done("dve", "dprod"))
                        mine("dprod")
                        nc.vector.tensor_tensor(D4[:, 1, :], DE[:, 1, 0:4], DE[:, 1, 4:8], ALU.add).then_inc(dve_done, done("dve", "dsum0"))
                        mine("dsum0")
                        nc.vector.tensor_tensor(D4[:, 1, :], D4[:, 1, :], DE[:, 1, 8:12], ALU.add).then_inc(dve_done, done("dve", "dsum"))
                        mine("dsum")
                        nc.vector.reciprocal(D4[:, 2, :], D4[:, 1, :]).then_inc(dve_done, done("dve", "drec"))
                        mine("drec")
                        for n in range(3):
                            nc.vector.tensor_tensor(FAC[:, n, :], DE[:, 0, 4 * n:4 * n + 4], D4[:, 2, :], ALU.mult)\
                                .then_inc(dve_done, done("dve", f"factor {n}"))
                elif what == "pv" and g in CHUNK2:
                    heads_rest(CHUNK2[g])

            def gated(gates, n, last, sum_before):
                for b in range(4):
                    dve.wait_ge(pe_done, at("pe", f"br {n} {b}"))
                    v = gates[:, 2 * b:2 * b + 2, :].rearrange("p a t -> p (a t)")
                    nc.vector.tensor_tensor(v, v, ps[:, 4 + b, :], ALU.mult).then_inc(dve_done, done("dve", f"gated {n}" if b == 3 else f"gated {n} {b}"))
                    if last:
                        mine(f"gated {n}" if b == 3 else f"gated {n} {b}")
                        if b == 0:
                            dve.wait_ge(pool_done, at("pool", sum_before))
                        y = T8[:, 2 * b:2 * b + 2, :]
                        nc.vector.tensor_tensor(y, y, gates[:, 2 * b:2 * b + 2, :], ALU.add).then_inc(dve_done, done("dve", f"y {b}"))
                if last:
                    for b in range(4):
                        dve.wait_ge(act_done, at("act", f"yh {b}"))
                        nc.vector.tensor_tensor(NL[:, 2 * b:2 * b + 2, :], T8[:, 2 * b:2 * b + 2, :], NH[:, 2 * b:2 * b + 2, :].bitcast(F32),
                                                ALU.subtract).then_inc(dve_done, done("dve", f"yl {b}"))

            m.section = "setup"
            nc.vector.memset(zero[:, :], 0.0).then_inc(lo_ready, 3)
            nc.vector.memset(tick[:, 1:2], 0.0).then_inc(ada_sum[0], 1)
            nc.vector.memset(tick[:, 2:3], 0.0).then_inc(ada_sum[1], 1)
            nc.vector.memset(tick[:, 3:4], 0.0).then_inc(ada_out, 1)
            mean_square("next")
            dve.wait_ge(act_done, at("act", "TB"))
            for block in (1, 2):
                m.section = f"block{block}"
                with dve.Fori(0, DEPTH) as l:
                    m.layer = l
                    dve.wait_ge(act_done, at("act", "vec"))
                    if block == 1:
                        for row in (V1_POST1, V1_POST2):
                            ins = nc.vector.tensor_scalar(vec[:, row:row + 8], vec[:, row:row + 8], 0.5, None, ALU.mult)
                        ins.then_inc(dve_done, done("dve", "gains"))
                        mine("gains")
                        pres = [vec[:, r:r + 8] for r in (V1_PRE1, V1_PREM, V1_PRE2)]
                        posts = [vec[:, r:r + 8] for r in (V1_POST1, V1_POSTM, V1_POST2)]
                        shifts = (None, None, None)
                    else:
                        nc.vector.tensor_tensor(modl, mods.rearrange("p a b -> p (a b)")[:, bass.ds(72 * l, 72)], vec[:, V2_B:V2_PE], ALU.add)\
                            .then_inc(dve_done, done("dve", "modl"))
                        mine("modl")
                        for k in range(3):
                            nc.vector.scalar_tensor_tensor(out=gains[:, 8 * k:8 * k + 8], in0=modl[:, 24 * k + 8:24 * k + 16], scalar=1.0,
                                                           in1=vec[:, V2_G + 8 * k:V2_G + 8 * k + 8], op0=ALU.add, op1=ALU.mult)
                            ins = nc.vector.tensor_scalar(gains[:, 24 + 8 * k:32 + 8 * k], modl[:, 24 * k + 16:24 * k + 24],
                                                          1.0 if k == 1 else 0.5, None, ALU.mult)
                        ins.then_inc(dve_done, done("dve", "gains"))
                        mine("gains")
                        pres = [gains[:, 8 * k:8 * k + 8] for k in range(3)]
                        posts = [gains[:, 24 + 8 * k:32 + 8 * k] for k in range(3)]
                        shifts = (0, 24, 48)
                    F = ((block - 1) * DEPTH + l) * 2
                    split_lo(block, l, 0, 0)
                    pre("pre1", pres[0], shifts[0])
                    split_lo(block, l, 0, 1)
                    ffn(block, l, 0, F, False, 0)
                    if block == 1:
                        post("post1", posts[0], "x1")
                    else:
                        gated_add(posts[0], "x1")
                    mean_square("prem")
                    pre("prem", pres[1], shifts[1])
                    for u in range(UNITS):
                        p = u + 2
                        split_lo(block, l, 11 + p // 3, p % 3, UNITS + p)
                        for work in (SIDE1 if block == 1 else SIDE2).get(u, ()):
                            if work[:3] not in ("top", "tap"):
                                settle()
                            (side1 if block == 1 else side2)(l, work)
                        if block == 1 and BR1 <= u < OUT1:
                            k = u - BR1
                            gated(G[:, 8 * k:8 * k + 8, :], k, k == 3, "sum 2")
                        if block == 2 and BR2 <= u < OUT2:
                            k = u - BR2
                            if k != 1:
                                if k == 2:
                                    gated(G2[:, 16:24, :], 1, False, None)
                                    gated(G2[:, 8:16, :], 2, True, "sum 1")
                                else:
                                    gated(G2[:, 0:8, :], 0, False, None)
                    if block == 1:
                        post("postm", posts[1], "xm")
                    else:
                        dve.wait_ge(unit_used, unit_number(block, l, 3 * 21 + 2) + 4)
                        gated_add(posts[1], "xm")
                    mean_square("pre2")
                    pre("pre2", pres[2], shifts[2])
                    ffn(block, l, 22, F + 1, True, 1)
                    if block == 1:
                        post("post2", posts[2], "x2")
                    else:
                        gated_add(posts[2], "x2")
                    mean_square("next")
            m.section = "end"
            for c in range(C):
                ins = nc.vector.scalar_tensor_tensor(out=T8[:, c, :], in0=XT[:, c, :], scalar=vec0[:, 8 + c:9 + c], in1=rms[:, 1, :],
                                                     op0=ALU.mult, op1=ALU.mult)
            ins.then_inc(dve_done, done("dve", "final n"))

        @block_.tensor
        def _(pe):
            def take_wait():
                nc.tensor.matmul(ps[:, 3, 0:1], zero[:, 0:P], zero[:, 0:1], start=True, stop=True)

            def ready(block, l, q, s):
                pe.wait_ge(lo_ready, unit_number(block, l, 3 * q + s) + 4)

            def three(dst, wh, wl, xh, xl, start, stop, weights_still=True, skip=False):
                pairs = ((wh, xh), (wh, xl), (wl, xh)) if weights_still else ((xh, wh), (xh, wl), (xl, wh))
                for k, (a, b) in enumerate(pairs):
                    last = nc.tensor.matmul(dst, a, b, start=start and k == 0, stop=stop and k == 2, skip_group_check=skip)
                return last

            def channels(dst, s, n, a, xh=NH, xl=NL):
                for c in range(C):
                    wh, wl = (v[:, s, n * c + a:n * c + a + P] for v in (hi, lo))
                    last = three(dst, wh, wl, xh[:, c, :], xl[:, c, :], c == 0, c == C - 1)
                return last

            def tokens(dst, s, n, a, w, t):
                for c in range(C):
                    wh, wl = (v[:, s, n * c + a:n * c + a + w] for v in (hi, lo))
                    x = slice(P * t, P * t + P)
                    last = three(dst, wh, wl, NH[:, c, x], NL[:, c, x], c == 0, c == C - 1, False)
                return last

            def stat(name, sources):
                for c in range(C):
                    if c in sources:
                        pe.wait_ge(*sources[c])
                    last = nc.tensor.matmul(ps[:, 3, 0:T], mean_d, T8[:, c, :], start=c == 0, stop=c == C - 1)
                last.then_inc(pe_done, done("pe", name + " stat"))

            def pre(name):
                stat(name, {2 * b: (act_done, at("act", f"{name} sq{b}")) for b in range(4)})

            def first_channels(name, dst, s):
                for c in range(C):
                    pe.wait_ge(dve_done, at("dve", f"{name} l{c}"))
                    for h in range(2):
                        wh, wl = (v[:, s, T * c + P * h:T * c + P * h + P] for v in (hi, lo))
                        last = three(dst[:, T * h:T * h + T], wh, wl, NH[:, c, :], NL[:, c, :], c == 0 and h == 0, c == C - 1, skip=True)
                return last

            def ffn(block, l, b, F, name, half):
                for k in range(4):
                    nc.tensor.matmul(ps[:, 4 + k, :], zero[:, 0:P], zero[:, P:640], start=True, stop=False, skip_group_check=True)

                def gate_up(q, s, bank, f):
                    ready(block, l, q, s)
                    if not isinstance(f, int) or f >= 2:
                        pe.wait_ge(hidden_ready, NF * F + f - 1)
                    if isinstance(f, int) and f == 0:
                        first_channels(name, ps[:, bank, :], s).then_inc(unit_used, 1)
                        return
                    channels(ps[:, bank, 0:T], s, T, 0)
                    channels(ps[:, bank, T:2 * T], s, T, P).then_inc(unit_used, 1)

                def down(q, s, i, final):
                    ready(block, l, q, s)
                    pe.wait_ge(hidden_lo, NF * F + 2 * i + 2)
                    for j in range(2):
                        for k in range(C):
                            o = 1024 * j + P * k
                            last = three(ps[:, 4 + k // 2, T * (k % 2):T * (k % 2) + T], hi[:, s, o:o + P], lo[:, s, o:o + P],
                                         BH[:, j, :], BL[:, j, :], False, final and j == 1, skip=True)
                    last.then_inc(unit_used, 1)

                def body(i, ada):
                    if ada:
                        a = 18 * l + 9 * half + i - 2
                        pe.wait_ge(ada_sum[0], a + 2)
                        pe.wait_ge(ada_sum[1], a + 2)
                        for k in range(4):
                            last = nc.tensor.matmul(ps[:, 1, k:k + 1], acc_ada[:, P * k:P * k + P], tri[:, P:P + 1],
                                                    start=True, stop=True)
                        last.then_inc(ada_out, 1)
                    gate_up(b + i - 1, 2, 2, 2 * i)
                    gate_up(b + i, 0, 0, 2 * i + 1)
                    down(b + i, 1, i - 1, False)

                gate_up(b, 0, 0, 0)
                gate_up(b, 1, 1, 1)
                body(1, False)
                with pe.Fori(2, NF // 2 - 1) as i:
                    body(i, block == 1)
                body(NF // 2 - 1, block == 1)
                down(b + 10, 2, 10, True)

            def scores(g, q, k, free):
                if free is not None:
                    pe.wait_ge(*free)
                for e in range(2):
                    rows = slice(64 * e, 64 * e + 64)
                    for t, (o, w) in enumerate(SPAN):
                        last = nc.tensor.matmul(ps[:, 3 + e, o:o + w], q[rows, P * t:P * t + P], k[rows, 0:w], start=True, stop=True)
                last.then_inc(pe_done, done("pe", f"qk {g}"))

            def turned(p_tile, g, slot, free):
                pe.wait_ge(pool_done, at("pool", f"p {g}"))
                if free is not None:
                    pe.wait_ge(*free)
                for e in range(2):
                    for k in range(3):
                        last = nc.tensor.transpose(ps[:, 5 + e, P * k:P * k + P], p_tile[:, 2 * slot + e, P * k:P * k + P], ident)
                last.then_inc(pe_done, done("pe", f"tr {g}"))

            def values(g, v, first, last_one, free):
                pe.wait_ge(act_done, at("act", f"pt {g}"))
                if free is not None:
                    pe.wait_ge(*free)
                for e in range(2):
                    rows = slice(64 * e, 64 * e + 64)
                    nc.tensor.matmul(ps[rows, 7, 0:T], v(0, e), PT[:, e, 0:T], start=first, stop=False, skip_group_check=True)
                    last = nc.tensor.matmul(ps[rows, 7, P:T], v(1, e), PT[:, e, T:CAUSAL], start=False, stop=last_one, skip_group_check=True)
                last.then_inc(pe_done, done("pe", f"pv {g}"))

            def unit1(l, u):
                q, s = 11 + u // 3, u % 3
                ready(1, l, q, s)
                bank = ps[:, u % 3, :]
                if 3 <= u < BR1:
                    pe.wait_ge(act_done, at("act", f"ev {u - 3}"))
                if u in (V_GATE, V_U):
                    for t in range(2):
                        last = tokens(bank[:, T * t:T * t + T], s, T, 0, T, t)
                elif u == IDX_U:
                    channels(bank[:, 0:T], s, 260, 0)
                    channels(bank[:, T:2 * T], s, 260, P)
                    for t in range(2):
                        last = tokens(ps[:, 7, 4 * t:4 * t + 4], s, 260, T, 4, t)
                elif u == 0:
                    last = first_channels("prem", bank, s)
                elif u < BR1:
                    channels(bank[:, 0:T], s, T, 0)
                    last = channels(bank[:, T:2 * T], s, T, P)
                elif u < OUT1:
                    if u == BR1:
                        pe.wait_ge(dve_done, at("dve", "bl 5"))
                    branch_unit(s, u - BR1, u - BR1, [(0, 2 * (u - BR1)), (1024, 2 * (u - BR1) + 1)], True, True).then_inc(unit_used, 1)
                    return
                else:
                    out_unit(s, u - OUT1).then_inc(unit_used, 1)
                    return
                last.then_inc(unit_used, 1)

            def branch_unit(s, n, waits, chunks, first, final):
                for k in range(C):
                    if k % 2 == 0 and first and waits:
                        w = waits - 1
                        pe.wait_ge(dve_done, at("dve", f"gated {w}" if k == 6 else f"gated {w} {k // 2}"))
                    for j, (o, chunk) in enumerate(chunks):
                        last = three(ps[:, 4 + k // 2, T * (k % 2):T * (k % 2) + T], hi[:, s, o + P * k:o + P * k + P],
                                     lo[:, s, o + P * k:o + P * k + P], BH[:, chunk, :], BL[:, chunk, :],
                                     first and j == 0 and k % 2 == 0, final and j == len(chunks) - 1, skip=True)
                    if k % 2 and final:
                        last.then_inc(pe_done, done("pe", f"br {n} {k // 2}"))
                if final:
                    last = nc.tensor.matmul(ps[0:1, 3, 0:1], zero[:, 0:1], zero[:, 0:1], start=True, stop=True)
                return last

            def out_unit(s, j):
                if j == 0:
                    for b in range(4):
                        pe.wait_ge(dve_done, at("dve", f"yl {b}"))
                channels(ps[:, 4 + j, 0:T], s, T, 0)
                return channels(ps[:, 4 + j, T:2 * T], s, T, P)

            def side1(l, work):
                what, _, g = work.partition(" ")
                if work == "gm0":
                    for k in range(4):
                        last = nc.tensor.transpose(ps[:, 3, P * k:P * k + P], WS[:, k, :], ident)
                    last.then_inc(pe_done, done("pe", "wsT"))
                elif work == "gm1":
                    pe.wait_ge(dve_done, at("dve", "VN"))
                    for k in range(4):
                        for t in range(2):
                            o = T * (k // 2) + P * t
                            last = nc.tensor.matmul(ps[64 * (k % 2):64 * (k % 2) + 64, 3, o:o + P], VG[:, t, 64 * k:64 * k + 64], WST[:, k, :],
                                                    start=True, stop=True)
                    last.then_inc(pe_done, done("pe", "mixed"))
                elif work == "pool1":
                    pe.wait_ge(dve_done, at("dve", "pd"))
                    take_wait()
                    for k in range(4):
                        rows = slice(64 * (k % 2), 64 * (k % 2) + 64)
                        last = nc.tensor.matmul(ps[rows, 3, T * (k // 2):T * (k // 2) + T], PW[rows, k // 2, :], PD[rows, k // 2, :],
                                                start=True, stop=True)
                    last.then_inc(pe_done, done("pe", "pw"))
                elif what == "idx":
                    t = int(g)
                    o, w = SPAN[t]
                    pe.wait_ge(act_done, at("act", f"ev {IDX_U}" if t == 0 else "rel 0 3"))
                    for h in range(4):
                        rows = slice(32 * h, 32 * h + 32)
                        last = nc.tensor.matmul(ps[:, 3 + h, 0:w], QKI[rows, 0, P * t:P * t + P], QKI[rows, 1, 0:w], start=True, stop=True,
                                                tile_position=(32 * h, 0))
                    last.then_inc(pe_done, done("pe", work))
                elif work == "ln1":
                    pe.wait_ge(dve_done, at("dve", "tap 30"))
                    for c in range(2):
                        last = nc.tensor.matmul(ps[:, 5, 0:T], mean_w, ACC[:, c, :], start=c == 0, stop=c == 1)
                    last.then_inc(pe_done, done("pe", "lnmean"))
                elif work == "ln2":
                    pe.wait_ge(act_done, at("act", "xcsq"))
                    for c in range(2):
                        last = nc.tensor.matmul(ps[:, 6, 0:T], mean_w, BT[:, c, :], start=c == 0, stop=c == 1)
                    last.then_inc(pe_done, done("pe", "ln stat"))
                elif what == "qk":
                    k = int(g)
                    scores(k, QT[:, k, :], KT[:, k, :], (dve_done, at("dve", f"nm {k - 1}")) if k else (act_done, at("act", "rel 1 3")))
                elif what == "tr":
                    k = int(g)
                    turned(P1, k, k, (act_done, at("act", f"pt {k - 1}")) if k else (dve_done, at("dve", "lnx")))
                elif what == "pv":
                    k = int(g)
                    values(k, lambda t, e: VT[:, t, 64 * (2 * k + e):64 * (2 * k + e) + 64], True, True,
                           (dve_done, at("dve", "bl 4")) if k else None)

            def unit2(l, u):
                q, s = 11 + u // 3, u % 3
                ready(2, l, q, s)
                bank = ps[:, u % 3, :]
                if 3 <= u < BR2:
                    before = u - 2 if u == W1_U else u - 3
                    pe.wait_ge(act_done, at("act", "hid" if before in (W1_U, W1_U + 1) else f"ev {before}"))
                if u == VG_U:
                    for t in range(2):
                        last = tokens(bank[:, 140 * t:140 * t + 140], s, 140, 0, 140, t)
                elif u in (DV_U, FV_U):
                    for t in range(2):
                        last = tokens(bank[:, T * t:T * t + T], s, T, 0, T, t)
                elif u == DVF_U:
                    tokens(bank[:, 0:262], s, 262, 0, 262, 0)
                    last = tokens(ps[:, 6, 0:262], s, 262, 0, 262, 1)
                elif u in (W1_U, W1_U + 1):
                    if u == W1_U:
                        pe.wait_ge(dve_done, at("dve", "kel"))
                    keys = [v[:, 6:8, :].rearrange("p a t -> p (a t)") for v in (BH, BL)]
                    for j in range(16):
                        for kv in range(2):
                            rows = slice(64 * kv, 64 * kv + 64)
                            o = 16 * (16 * (u - W1_U) + j)
                            last = three(ps[:, kv, 0:16], hi[rows, s, P * j:P * j + P], lo[rows, s, P * j:P * j + P],
                                         keys[0][rows, o:o + 16], keys[1][rows, o:o + 16],
                                         u == W1_U and j == 0, u == W1_U + 1 and j == 15, skip=True)
                elif u == 0:
                    last = first_channels("prem", bank, s)
                elif u < BR2:
                    channels(bank[:, 0:T], s, T, 0)
                    last = channels(bank[:, T:2 * T], s, T, P)
                elif u == BR2:
                    pe.wait_ge(dve_done, at("dve", "bl 5"))
                    last = branch_unit(s, 0, 0, [(0, 0), (1024, 1)], True, True)
                elif u == BR2 + 1:
                    last = branch_unit(s, 1, 1, [(0, 3), (1024, 4)], True, False)
                elif u == BR2 + 2:
                    branch_unit(s, 1, 0, [(0, 5)], False, True)
                    last = branch_unit(s, 2, 2, [(1024, 2)], True, True)
                else:
                    last = out_unit(s, u - OUT2)
                last.then_inc(unit_used, 1)

            def side2(l, work):
                what, _, g = work.partition(" ")
                if work[:4] == "rope":
                    u = int(work[4:])
                    pe.wait_ge(act_done, at("act", f"ev {u}"))
                    if u:
                        pe.wait_ge(dve_done, at("dve", f"rope {ROPED[ROPED.index(u) - 1]}"))
                    for k in range(2):
                        last = nc.tensor.matmul(ps[:, 4, T * k:T * k + T], SWAP, Z[:, u % 2, k, :], start=True, stop=True)
                    last.then_inc(pe_done, done("pe", f"swap {u}"))
                elif work == "dup":
                    pe.wait_ge(dve_done, at("dve", "rope 1"))
                    for k in range(2):
                        last = nc.tensor.matmul(ps[:, 3, T * k:T * k + T], DUP[:, k, :], KSW, start=True, stop=True)
                    last.then_inc(pe_done, done("pe", "dup"))
                elif work == "fox":
                    pe.wait_ge(dve_done, at("dve", "lfb"))
                    pe.wait_ge(act_done, at("act", "exp 2"))
                    ones, up = tri[:, P:T], tri[:, 0:P]
                    nc.tensor.matmul(ps[:, 7, 0:6], up, LF[:, 0, 0:6], start=True, stop=True)
                    nc.tensor.matmul(ps[:, 7, 8:14], ones, LF[:, 0, 0:6], start=True, stop=False)
                    nc.tensor.matmul(ps[:, 7, 8:14], up, LF[:, 1, 0:6], start=False, stop=True)
                    for h in range(6):
                        b, o = ((3, 0), (3, T), (4, 0), (4, T), (5, 0), (6, 0))[h]
                        nc.tensor.matmul(ps[:, b, o:o + T], LFB[:, h, 0, :], tri, start=True, stop=False)
                        last = nc.tensor.matmul(ps[:, b, o + P:o + T], LFB[:, h, 1, :], up, start=False, stop=True)
                    last.then_inc(pe_done, done("pe", "fox"))
                elif work == "w2":
                    pe.wait_ge(act_done, at("act", "hid"))
                    nc.tensor.matmul(ps[:, 3, 384:400], W2[:, 0:P], HID[:, 0, :], start=True, stop=True)
                    nc.tensor.matmul(ps[0:16, 4, 384:448], HID[:, 1, :], W2[:, P:192], start=True, stop=True).then_inc(pe_done, done("pe", "w2"))
                elif work == "cqk":
                    pe.wait_ge(act_done, at("act", "w2"))
                    for e in range(2):
                        rows = slice(64 * e, 64 * e + 64)
                        for j in range(2):
                            for t in range(2):
                                o = 384 + 16 * (2 * j + t)
                                last = nc.tensor.matmul(ps[:, 3 + e, o:o + 16], NQ[rows, j, P * t:P * t + P], KC2[rows, :], start=True, stop=True)
                    last.then_inc(pe_done, done("pe", "cqk"))
                elif work == "ctr":
                    pe.wait_ge(dve_done, at("dve", "pc"))
                    pe.wait_ge(act_done, at("act", "pt 2"))
                    for e in range(2):
                        for j in range(2):
                            for t in range(2):
                                o = T * j + P * t
                                last = nc.tensor.matmul(ps[0:16, 5 + e, o:o + P], PC[:, 4 * e + 2 * j + t, :], ident, start=True, stop=True)
                    last.then_inc(pe_done, done("pe", "ctr"))
                elif what == "cpv":
                    j = int(g)
                    pe.wait_ge(act_done, at("act", "ptc"))
                    pe.wait_ge(dve_done, at("dve", "bl 2" if j == 0 else "bl 0"))
                    for e in range(2):
                        nc.tensor.matmul(ps[64 * e:64 * e + 64, 7, 0:T], VC2[0:16, :], PTC[0:16, 2 * e + j, :], start=True, stop=False,
                                         skip_group_check=True)
                elif what == "qk":
                    k, j = GROUPS2.index(g), int(g[1])
                    qk = {"d": lambda: (DQK[:, j, :], DQK[:, 3 + j, :]), "s": lambda: (NQ[:, j, :], KSD[:, 0, :]),
                          "w": lambda: (NQ[:, j, :], KSD[:, 1, :]), "f": lambda: (FQK[:, j, :], FQK[:, 3 + j, :])}[g[0]]()
                    free = {"d0": (dve_done, at("dve", "rope 5")), "s0": (dve_done, at("dve", "pc"))}.get(g)
                    scores(k, *qk, free or (dve_done, at("dve", f"nm {k - 1}")))
                elif what == "tr":
                    k = GROUPS2.index(g)
                    free = {"d0": (act_done, at("act", "cs")), "s0": (act_done, at("act", "ptc"))}.get(g)
                    turned(P2, k, k % 3, free or (act_done, at("act", f"pt {k - 1}")))
                elif what == "pv":
                    k, j = GROUPS2.index(g), int(g[1])
                    v = {"d": lambda t, e: DV[:, t, P * j + 64 * e:P * j + 64 * e + 64], "s": lambda t, e: VSW[:, t, 0:64],
                         "w": lambda t, e: VSW[:, t, 64:128], "f": lambda t, e: FV[:, t, P * j + 64 * e:P * j + 64 * e + 64]}[g[0]]
                    before = {"d0": (act_done, at("act", "cs")), "f0": (dve_done, at("dve", "bl 1")), "f1": (dve_done, at("dve", "bl 3")),
                              "f2": (dve_done, at("dve", "bl 4"))}.get(g)
                    values(k, v, g in ("d0", "f0", "f1", "f2"), g in CHUNK2, before)

            m.section = "setup"
            pe.wait_ge(const_in, 16 * 10)
            nc.tensor.transpose(ps[:, 0, 0:16], vrow[0:16, :], ident[0:16, 0:16]).then_inc(pe_done, done("pe", "vec0"))
            nc.tensor.matmul(ps[0:4, 1, :], WI.rearrange("p a b -> p (a b)")[0:32, 0:4], onehot.rearrange("p a b -> p (a b)")[0:32],
                             start=True, stop=True).then_inc(pe_done, done("pe", "bias rows"))
            x_in = T8[:, :, :].rearrange("p (a b) t -> p a (b t)", a=2)
            for c in range(C):
                for t in range(2):
                    o = T * (c % 2) + P * t
                    last = nc.tensor.transpose(ps[:, 4 + c // 2, o:o + P], x_in[:, t, P * c:P * c + P], ident)
            last.then_inc(pe_done, done("pe", "xT"))
            pe.wait_ge(pool_done, at("pool", "mean_w"))
            pre("next")
            pe.wait_ge(const_in, 16 * 13)
            pe.wait_ge(dve_done, at("dve", "next rstd"))
            for h in range(4):
                for t, (o, w) in enumerate(SPAN):
                    last = nc.tensor.matmul(ps[:, h, o:o + w], flip, brev[:, 2 * h + t, 0:w], start=True, stop=True)
            last.then_inc(pe_done, done("pe", "TB"))
            pe.wait_ge(pool_done, at("pool", "mean_w"))
            pe.wait_ge(act_done, at("act", "TB"))
            pe.wait_ge(lo_ready, 3)
            nc.tensor.matmul(ps[0:1, 0, 0:1], zero[:, 0:1], zero[:, 0:1], start=True, stop=True).then_inc(unit_used, 3)
            for block in (1, 2):
                m.section = f"block{block}"
                with pe.Fori(0, DEPTH) as l:
                    m.layer = l
                    pe.wait_ge(rows_in, rows_target(block, l))
                    n = V1_N if block == 1 else V2_N
                    nc.tensor.transpose(ps[:, 1, 0:n], vrow[0:n, :], ident[0:n, 0:n]).then_inc(pe_done, done("pe", "vec"))
                    pe.wait_ge(act_done, at("act", "vec"))
                    F = ((block - 1) * DEPTH + l) * 2
                    ffn(block, l, 0, F, "pre1", 0)
                    if block == 1:
                        pre("post1")
                    pe.wait_ge(small_in, small_target(block, l))
                    pre("prem")
                    for u in range(UNITS):
                        (unit1 if block == 1 else unit2)(l, u)
                        for work in (SIDE1 if block == 1 else SIDE2).get(u, ()):
                            (side1 if block == 1 else side2)(l, work)
                    if block == 1:
                        pre("postm")
                    pre("pre2")
                    ffn(block, l, 22, F + 1, "pre2", 1)
                    if block == 1:
                        pre("post2")
                    pre("next")
            m.section = "end"
            pe.wait_ge(dve_done, at("dve", "final n"))
            for t in range(2):
                for c in range(C):
                    b, o = 4 * t + c // 2, P * (c % 2)
                    last = nc.tensor.transpose(ps[:, b, o:o + P], T8[:, c, P * t:P * t + P], ident)
            last.then_inc(pe_done, done("pe", "out"))

    return m


def constants():
    f = np.float32
    k = np.arange(P)
    t = np.arange(T)
    c = {"ident": np.eye(P, dtype=f), "flip": np.eye(P, dtype=f)[::-1].copy()}
    c["tri"] = np.concatenate([(k[:, None] <= k[None]).astype(f), np.ones((P, P), f)], 1)

    def causal_tiles(seen):
        return np.concatenate([np.where(seen(P * i + k[:, None], np.arange(w)[None]), 0, NEG).astype(f) for i, (_, w) in enumerate(SPAN)], 1)

    c["causal"] = causal_tiles(lambda t, s: s <= t)
    c["dilated"] = np.concatenate([causal_tiles(lambda t, s, w=w, d=d: (s <= t) & ((t - s) % d == 0) & (t - s <= w))
                                   for w, d in ((128, 1), (512, 4), (2048, 16))], 1)
    windows = np.array([2, 4, 8, 16]).reshape(2, 2)
    c["rcount"] = np.concatenate([1 / np.minimum(t[None] + 1, windows[h][k // 64][:, None]) for h in range(2)], 1).astype(f)
    n = np.arange(T)
    large = 16 + (np.log(np.maximum(n, 1).astype(f) / f(16)) / f(np.log(128 / 16)) * f(16)).astype(np.int32)
    bucket = np.where(n < 16, n, np.minimum(large, 31))
    onehot = np.zeros((32, 512), f)
    onehot[bucket, T - 1 - n] = 1
    c["onehot"] = onehot
    inv = f(500000.0) ** (-np.arange(0, 16, 2, dtype=f) / f(16))
    ang = (t.astype(f)[:, None] * inv[None]).T
    cos, sin = np.ones((P, T), f), np.zeros((P, T), f)
    swap = np.zeros((P, P), f)
    for base in (0, 64):
        for r in range(8):
            cos[base + r] = cos[base + 8 + r] = np.cos(ang[r])
            sin[base + r] = sin[base + 8 + r] = np.sin(ang[r])
            swap[base + 8 + r, base + r] = -1
            swap[base + r, base + 8 + r] = 1
    c["rope"], c["swap"] = np.concatenate([cos, sin], 1), swap
    half = np.eye(64, dtype=f)
    z = np.zeros((64, P), f)
    both = np.concatenate([half, half], 1)
    c["dup"] = np.concatenate([np.concatenate([both, z]), np.concatenate([z, both])], 1)
    end = 16 * np.arange(16) + 31
    keep = np.concatenate([(end[None] <= P * i + k[:, None]) & (np.arange(16)[None] < 15) for i in range(2)], 1)
    c["cmp_keep"], c["cmp_add"] = keep.astype(f), np.where(keep, 0, NEG).astype(f)
    return c


_INS = ['x', 'ffn1_pre_g', 'ffn1_post_g', 'ffn1_w_gu', 'ffn1_w_down', 'mix_pre_g', 'mix_post_g', 'w_in', 'gm_v_g', 'gm_ws', 'gm_b',
        'pool_w', 'pool_scale', 'conv_dw', 'conv_b', 'conv_ln_g', 'conv_ln_b', 'w_branch', 'w_out', 'ffn2_pre_g', 'ffn2_post_g',
        'ffn2_w_gu', 'ffn2_w_down', 'rel_bias', 'c_2', 'ada_w_2', 'ada_b_2', 'norm_g_2', 'final_norm_g_2', 'ffn_w_in_2', 'ffn_w_out_2',
        'mix_w_in_2', 'nsa_cmp_pe_2', 'nsa_cmp_w1_2', 'nsa_cmp_w2_2', 'fox_f_bias_2', 'br_w_nsa_2', 'br_w_dil_2', 'br_w_fox_2',
        'mix_w_out_2']


def build(nc, shapes, known):
    ins = {n: nc.dram_tensor(f"in_{n}", s, mybir.dt.float32, kind="ExternalInput").ap() for n, s in shapes.items()}
    out = nc.dram_tensor("out", (1, T, D), mybir.dt.float32, kind="ExternalOutput").ap()
    return program(nc, known, ins, out)


def kernel(**inputs):
    import concourse.bacc as _bacc
    from concourse.bass_utils import run_bass_kernel_spmd as _run

    arrays = {n: np.ascontiguousarray(inputs[n]) for n in _INS}
    arrays.update(constants())
    shapes = {n: a.shape for n, a in arrays.items()}
    counts = build(_bacc.Bacc("TRN2", target_bir_lowering=False, num_devices=1), shapes, None).order
    nc = _bacc.Bacc("TRN2", target_bir_lowering=False, num_devices=1)
    build(nc, shapes, counts)
    r = _run(nc, [{f"in_{n}": a for n, a in arrays.items()}], core_ids=[0])
    return r.results[0]["out"]
```

```python
from contextlib import ExitStack

import numpy as np
import concourse.bass as bass
from concourse import mybir

F32 = mybir.dt.float32
F32R = mybir.dt.float32r
ALU = mybir.AluOpType
ACT = mybir.ActivationFunctionType
AX = mybir.AxisListType

P = 128
D = 1024
C = D // P
T = 256
FF = 2816
NF = FF // P
DEPTH = 2
RING = 3
UNITS = 33
LAYER_UNITS = 3 * UNITS
SLOT = 2096
EPS = 1e-6
NEG = -1e30
TAKEN = -3e38
WARM_POST, WARM_PRE = 24, 16
UPDATES = {1: (0, 1, 3, 2), 2: (0, 1, 2, 3)}
POOL_TAPS = 13
ADA_V = 336
CAUSAL = P + T
SPAN = ((0, P), (P, T))

U_GATE, V_GATE, POOL_U, Q_U, K_U, V_U, IDX_U, CONV_A, CONV_G, GATES1, BR1, OUT1 = 0, 1, 2, 3, 4, 5, 6, 7, 8, 9, 25, 29
COLS1 = [(0, 256), (256, 256), (512, 256), (768, 256), (1024, 256), (1280, 256), (1536, 164), (1700, 256), (1956, 256)]
COLS1 += [(2212 + 256 * i, 256) for i in range(16)]
NQ_U, KV_U, VG_U, DQK_U, FQK_U, DVF_U, DV_U, FV_U, W1_U, GATES2, BR2, OUT2 = 0, 1, 2, 3, 6, 9, 10, 11, 12, 14, 26, 29
COLS2 = [[(0, 256)], [(256, 192), (512, 64)], [(448, 64), (576, 76)]]
COLS2 += [[(652 + 256 * i, 256)] for i in range(3)] + [[(1804 + 256 * i, 256)] for i in range(3)]
COLS2 += [[(1420 + 256, 128), (2572 + 256, 134)], [(1420, 256)], [(2572, 256)], None, None]
COLS2 += [[(2962 + 256 * i, 256)] for i in range(12)]
V1_PRE1, V1_POST1, V1_PREM, V1_POSTM, V1_PRE2, V1_POST2, V1_PS, V1_CB, V1_LG, V1_LB, V1_DW, V1_N = 0, 8, 16, 24, 32, 40, 48, 50, 52, 54, 56, 118
V2_G, V2_B, V2_PE, V2_N = 0, 24, 96, 128
GROUPS2 = ["d0", "d1", "d2", "s0", "w0", "s1", "w1", "f0", "f1", "f2"]
SIDE2 = {1: ["rope0"], 2: ["rope1"], 3: ["dup"], 4: ["rope3"], 5: ["rope4"], 6: ["rope5"],
         7: ["qk d0"], 8: ["qk d1", "ke"], 9: ["qk d2"], 10: ["lf"], 12: ["fox"], 13: ["tr d0", "hid"],
         14: ["pv d0", "tr d1", "hidt"], 15: ["w2", "pv d1", "tr d2", "cqk"], 16: ["pv d2", "ctr", "qk s0"], 17: ["qk w0"],
         18: ["tr s0", "qk s1"], 19: ["cpv 0", "pv s0", "tr w0", "qk w1"], 20: ["pv w0", "tr s1", "qk f0"],
         21: ["cpv 1", "pv s1", "tr w1", "qk f1"], 22: ["pv w1", "tr f0", "qk f2"], 23: ["pv f0", "tr f1"],
         24: ["pv f1", "tr f2"], 25: ["pv f2"]}
ROPED = [0, 1, 3, 4, 5]
CHUNK2 = {"w0": 0, "w1": 1, "d2": 2, "f0": 3, "f1": 4, "f2": 5}
SIDE1 = {2: ["gm0"], 3: ["gm1"], 4: ["pool0"], 5: ["pool1"], 7: ["idx 0"], 8: ["idx 1"], 9: ["convh"],
         **{10 + j: [f"top {j}", f"tap {j}"] for j in range(8)},
         18: ["qk 0"], 19: ["ln1"], 20: ["tr 0", "qk 1"], 21: ["ln2"], 22: ["pv 0", "tr 1"], 23: ["pv 1", "ln3"]}


class Counts:

    def __init__(self, known=None):
        self.known, self.order, self.section, self.layer, self.newest = known, {}, "setup", 0, {}

    def done(self, who, what):
        names = self.order.setdefault((who, self.section), {})
        assert what not in names, what
        names[what] = len(names) + 1
        self.newest[who] = what
        return 1

    def at(self, who, what, section=None):
        if self.known is None:
            return 1
        section = section or self.section
        value = self.known[(who, section)][what]
        for s, times in (("setup", 1), ("block1", DEPTH), ("block2", DEPTH), ("end", 1)):
            if s == section:
                break
            value += times * len(self.known.get((who, s), {}))
        if section == self.section and section.startswith("block"):
            return value + self.layer * len(self.known[(who, section)])
        return value + ((DEPTH - 1) * len(self.known[(who, section)]) if section.startswith("block") else 0)


def spread(ap, at, n):
    dims = [list(d) for d in ap.ap]
    dims.insert(at, [0, n])
    return bass.AP(ap.tensor, ap.offset, dims)


def window(ap, dims):
    return bass.AP(ap.tensor, ap.offset, [list(ap.ap[0])] + [list(d) for d in dims])


def program(nc, known, i, out):
    m = Counts(known)
    at, done = m.at, m.done
    with ExitStack() as ctx:
        def sb(name, shape, dt=F32):
            return ctx.enter_context(nc.sbuf_tensor(name, shape, dt))

        def sem(name):
            return ctx.enter_context(nc.semaphore(name))

        raw = sb("raw", [P, RING, SLOT])
        OUT = raw[:, 0, 0:2048].rearrange("p (b t) -> p b t", t=T)
        hi = sb("hi", [P, RING, SLOT], F32R)
        lo = sb("lo", [P, RING, SLOT], F32R)
        XT = sb("XT", [P, C, T])
        NH = sb("NH", [P, C, T], F32R)
        NL = sb("NL", [P, C, T], F32R)
        T8 = sb("T8", [P, C, T])
        BH = sb("BH", [P, 8, T], F32R)
        BL = sb("BL", [P, 8, T], F32R)
        arena = sb("arena", [P, 21700])
        used = {"shared": 0, "block1": 0, "block2": 0}

        def place(where, *shape):
            size = int(np.prod(shape))
            a = used[where] + (used["shared"] if where != "shared" else 0)
            used[where] += size
            assert used["shared"] + max(used["block1"], used["block2"]) <= 21700
            v = arena[:, a:a + size]
            if len(shape) == 2:
                v = v.rearrange("p (a b) -> p a b", b=shape[1])
            if len(shape) == 3:
                v = v.rearrange("p (a b c) -> p a b c", b=shape[1], c=shape[2])
            return v

        ident = place("shared", P)
        tri = place("shared", T)
        causal = place("shared", CAUSAL)
        mean_d = place("shared", P)
        mean_w = place("shared", P)
        eps = place("shared", 1)
        rms = place("shared", 3, T)
        vrow = place("shared", P)
        vec = place("shared", P)
        vec0 = place("shared", 16)
        cond = place("shared", C)
        mods = place("shared", DEPTH, 72)
        modl = place("shared", 72)
        gains = place("shared", 48)
        acc_ada = place("shared", 2 * T)
        PT = place("shared", 2, CAUSAL)
        NM = place("shared", 10, 4)
        DEN = place("shared", 10, 4)
        FAC = place("shared", 10, 4)
        G = place("block1", 32, T)
        SA, HF = G[:, 0:2, :], G[:, 2:4, :]
        P1 = place("block1", 4, CAUSAL)
        CA = P1[:, 0:2, 0:T]
        SG = P1[:, 2:4, 0:T]
        TB = place("block1", 4, CAUSAL)
        UT = place("block1", 2, T)
        PZ = place("block1", 2, 16 + T)
        SC = place("block1", 2, 16 + T)
        WK = place("block1", 2, 16 + T)
        PD = place("block1", 2, T)
        WI = place("block1", 2, 4)
        M8 = place("block1", 2, 8)
        REL = UT
        CH = place("block1", 2, 30 + T)
        ACC = PD
        SM = place("block1", CAUSAL)
        WS = place("block1", 4, P)
        QKI = WS.rearrange("p g t -> p (g t)").rearrange("p (a t) -> p a t", a=2)
        WST = place("block1", 4, P)
        PW = place("block1", 2, 64)
        RC = place("block1", 2, T)
        GB = place("block1", 2, P)
        BG = place("block1", T)
        ms = place("block1", 8)
        BT = place("block1", 2, T)
        SCf, WKf = (v.rearrange("p a b -> p (a b)") for v in (SC, WK))
        QT, KT, VT, VG = (T8[:, 2 * k:2 * k + 2, :] for k in range(4))
        ADA = ((0, ADA_V), (ADA_V, 2 * T - ADA_V))
        ADW = [G[:, 8:24, :].rearrange("p c t -> p (c t)")[:, C * o:C * (o + w)].rearrange("p (c n) -> p c n", n=w) for o, w in ADA]
        HG = G[:, 24:32, :]
        onehot = G[:, 0:2, :]
        brev = G[:, 2:10, :]
        flip = G[:, 10, 0:P]
        bias_rows = G[:, 12:14, :]
        G2 = place("block2", 24, T)
        P2 = place("block2", 6, CAUSAL)
        DM = place("block2", 3, CAUSAL)
        NQ = place("block2", 2, T)
        KVC = place("block2", 16 + T)
        KSW = G2[:, 8, :]
        KSD = place("block2", 2, T)
        VSW = place("block2", 2, 140)
        DQK = place("block2", 6, T)
        FQK = place("block2", 6, T)
        DV = place("block2", 2, 3 * P)
        FV = place("block2", 2, 3 * P)
        FL = place("block2", 2, 8)
        LF = place("block2", 2, 8)
        LE = place("block2", 2, 8)
        CT = place("block2", 2, 8)
        CS = DQK
        PTC = T8[:, 0:4, :]
        FM = T8[:, 4:7, :].rearrange("p a t -> p (a t)").rearrange("p (e k) -> p e k", e=2)
        LFB = G2[:, 0:6, :].rearrange("p h (t k) -> p h t k", t=2)
        ROPE = place("block2", 2, T)
        SWAP = place("block2", P)
        DUP = place("block2", 2, P)
        KE = G2[:, 6:8, :]
        W2 = place("block2", 192)
        HT = place("block2", P)
        HID = place("block2", 2, 16)
        KC2 = place("block2", 16)
        VC2 = place("block2", 64)
        PC = place("block2", 8, 16)
        CMK = place("block2", 2, 16)
        CMB = place("block2", 2, 16)
        CN = place("block2", 3, 8)
        GT = place("block2", 2, 12)
        FB = place("block2", 8)
        DE = place("block2", 3, 12)
        D4 = place("block2", 3, 4)
        KEH, KEL = (v[:, 4:8, :].rearrange("p a t -> p (a t)").rearrange("p (j n) -> p j n", n=32) for v in (BH, BL))
        Z = T8[:, 0:4, :].rearrange("p (r a) t -> p r a t", r=2)
        RT = T8[:, 4:8, :].rearrange("p (r a) t -> p r a t", r=2)

        zero = sb("zero", [P, 640], mybir.dt.bfloat16)
        tick = sb("tick", [P, 4])
        pool_tick = sb("pool_tick", [P, 2])

        ps = ctx.enter_context(nc.psum_tensor("ps", [P, 8, 512], F32))
        g_dram = nc.dram_tensor("bias_by_distance", [4, 512], F32, kind="Internal").ap()

        raw_ready = [sem(f"raw_ready{k}") for k in range(RING)]
        hi_ready = sem("hi_ready")
        lo_ready = sem("lo_ready")
        unit_used = sem("unit_used")
        silu_ready = sem("silu_ready")
        hidden_ready = sem("hidden_ready")
        hidden_hi = sem("hidden_hi")
        hidden_lo = sem("hidden_lo")
        const_in = sem("const_in")
        ada_in = [sem(f"ada_in{k}") for k in range(2)]
        ada_sum = [sem(f"ada_sum{k}") for k in range(2)]
        ada_out = sem("ada_out")
        ada_step = sem("ada_step")
        ada_fold = sem("ada_fold")
        ada_kept = sem("ada_kept")
        small_in = sem("small_in")
        rows_in = sem("rows_in")
        stored = sem("stored")
        pe_done, act_done, dve_done, pool_done = sem("pe_done"), sem("act_done"), sem("dve_done"), sem("pool_done")

        SMALL1, SMALL2, CONSTS2 = 6, 4, 6
        ROWS1, ROWS2 = 11, 3

        def small_target(block, l):
            return 16 * SMALL1 * (l + 1) if block == 1 else 16 * (SMALL1 * DEPTH + CONSTS2 + SMALL2 * (l + 1))

        def rows_target(block, l):
            return 16 * ROWS1 * (l + 1) if block == 1 else 16 * (ROWS1 * (DEPTH + 1) + ROWS2 * (l + 1))

        def unit_number(block, l, pos):
            return (block - 1) * DEPTH * LAYER_UNITS + l * LAYER_UNITS + pos

        block_ = ctx.enter_context(nc.Block())

        @block_.sync
        def _(sp):
            def load(block, l, q, s, pieces):
                sp.wait_ge(lo_ready, unit_number(block, l, 3 * q + s) + 1)
                assert len(pieces) == 2
                for dst, src in pieces:
                    sp.dma_start(dst(s), src).then_inc(raw_ready[s], 16)

            def cols(slot, a, b, n):
                return raw[:, slot, 0:8 * n].rearrange("p (c n) -> p c n", n=n)[:, :, a:b]

            def gate_up(w, f):
                view = w.rearrange("(c p) n -> p c n", p=P)
                return [(lambda s: cols(s, 0, P, T), view[:, :, bass.ds(P * f, P)]),
                        (lambda s: cols(s, P, T, T), view[:, :, bass.ds(P * f + FF, P)])]

            def down(w, i):
                view = w.rearrange("(k p) n -> p k n", p=P)
                return [(lambda s: raw[:, s, 0:1024], view[:, 2 * i, :]),
                        (lambda s: raw[:, s, 1024:2048], view[:, 2 * i + 1, :])]

            def halves(w, a, n):
                view = w.rearrange("(c p) n -> p c n", p=P)
                return [(lambda s, h=h: raw[:, s, 0:8 * n].rearrange("p (c n) -> p c n", n=n)[:, 4 * h:4 * h + 4, :],
                         view[:, 4 * h:4 * h + 4, a:a + n]) for h in range(2)]

            def rows(w, k):
                view = w.rearrange("(k p) n -> p k n", p=P)
                return [(lambda s, j=j: raw[:, s, 1024 * j:1024 * j + 1024], view[:, k + j, :]) for j in range(2)]

            def ffn(block, l, b, gu, dn):
                load(block, l, b, 0, gate_up(gu, 0))
                load(block, l, b, 1, gate_up(gu, 1))
                with sp.Fori(1, NF // 2) as i:
                    load(block, l, b + i - 1, 2, gate_up(gu, 2 * i))
                    load(block, l, b + i, 0, gate_up(gu, 2 * i + 1))
                    load(block, l, b + i, 1, down(dn, i - 1))
                load(block, l, b + 10, 2, down(dn, NF // 2 - 1))

            sp.dma_start(T8[:, :, :].rearrange("p (a b) t -> p a (b t)", a=2),
                         i["x"][0].rearrange("(a p) d -> p a d", p=P)).then_inc(const_in, 16)
            for n, (dst, src) in enumerate([
                (ident, i["ident"]), (tri, i["tri"]), (causal, i["causal"]), (RC.rearrange("p a b -> p (a b)"), i["rcount"]),
                (onehot.rearrange("p a b -> p (a b)")[0:32], i["onehot"]), (flip, i["flip"]),
                (WI.rearrange("p a b -> p (a b)")[0:32, 0:4], i["rel_bias"]),
                (vrow[0:8], i["c_2"].rearrange("a (c p) -> (a c) p", p=P)),
                (vrow[8:16], i["final_norm_g_2"].rearrange("(c p) -> c p", p=P)),
            ]):
                sp.dma_start(dst, src).then_inc(const_in, 16)
            sp.wait_ge(act_done, at("act", "bias rows", "setup"))
            sp.dma_start(g_dram, bias_rows.rearrange("p a b -> p (a b)")[0:4]).then_inc(const_in, 16)
            sp.wait_ge(const_in, 16 * 11)
            for t in range(2):
                sp.dma_start(brev.rearrange("p (h t) w -> p h t w", t=2)[:, :, t, :],
                             bass.AP(g_dram.tensor, P * (1 - t), [[1, P], [512, 4], [1, T]])).then_inc(const_in, 16)
            for block in (1, 2):
                m.section = f"block{block}"
                with sp.Fori(0, DEPTH) as l:
                    m.layer = l
                    if block == 1:
                        gu1, dn1, gu2, dn2 = i["ffn1_w_gu"][l], i["ffn1_w_down"][l], i["ffn2_w_gu"][l], i["ffn2_w_down"][l]
                    else:
                        gu1, dn1 = i["ffn_w_in_2"][l, 0], i["ffn_w_out_2"][l, 0]
                        gu2, dn2 = i["ffn_w_in_2"][l, 1], i["ffn_w_out_2"][l, 1]
                    ffn(block, l, 0, gu1, dn1)
                    for u in range(UNITS):
                        if block == 1:
                            if u < BR1:
                                pieces = halves(i["w_in"][l], *COLS1[u])
                            elif u < OUT1:
                                pieces = rows(i["w_branch"][l, u - BR1], 0)
                            else:
                                pieces = halves(i["w_out"][l], 256 * (u - OUT1), 256)
                        else:
                            if u in (W1_U, W1_U + 1):
                                pieces = [(lambda s, kv=kv: raw[64 * kv:64 * kv + 64, s, 0:2048].rearrange("p (j n) -> p j n", n=P),
                                           i["nsa_cmp_w1_2"][l, kv, 1024 * (u - W1_U):1024 * (u - W1_U) + 1024, :]
                                           .rearrange("(j d) n -> d j n", d=64)) for kv in range(2)]
                            elif u < BR2:
                                parts = COLS2[u]
                                if len(parts) == 1:
                                    pieces = halves(i["mix_w_in_2"][l], *parts[0])
                                else:
                                    n = parts[0][1] + parts[1][1]
                                    view = i["mix_w_in_2"][l].rearrange("(c p) n -> p c n", p=P)
                                    pieces = []
                                    for k, (a, w) in enumerate(parts):
                                        o = 0 if k == 0 else parts[0][1]
                                        pieces.append((lambda s, o=o, w=w, n=n: cols(s, o, o + w, n), view[:, :, a:a + w]))
                            elif u == BR2:
                                pieces = rows(i["br_w_nsa_2"][l], 0)
                            elif u == BR2 + 1:
                                pieces = rows(i["br_w_fox_2"][l], 0)
                            elif u == BR2 + 2:
                                pieces = [(lambda s: raw[:, s, 0:1024], i["br_w_fox_2"][l, 256:384, :]),
                                          (lambda s: raw[:, s, 1024:2048], i["br_w_dil_2"][l])]
                            else:
                                pieces = halves(i["mix_w_out_2"][l], 256 * (u - OUT2), 256)
                        load(block, l, 11 + u // 3, u % 3, pieces)
                    ffn(block, l, 22, gu2, dn2)
            sp.wait_ge(act_done, at("act", "out", "end"))
            sp.dma_start(out[0].rearrange("(a p) d -> p a d", p=P),
                         OUT.rearrange("p (a b) t -> p a (b t)", a=2)).then_inc(stored, 16)
            sp.wait_ge(stored, 16)


        @block_.gpsimd
        def _(pool):
            m.section = "setup"
            nc.gpsimd.memset(eps, EPS).then_inc(pool_done, done("pool", "eps"))
            nc.gpsimd.memset(mean_d, 1.0 / D).then_inc(pool_done, done("pool", "mean_d"))
            nc.gpsimd.memset(mean_w, 1.0 / 256).then_inc(pool_done, done("pool", "mean_w"))

            def small(dst, src):
                pool.dma_start(dst, src).then_inc(small_in, 16)

            def take_wait(k):
                nc.gpsimd.tensor_tensor(pool_tick[:, k:k + 1], eps, eps, ALU.mult)

            def load_rows(block, l):
                def rows(dst, src):
                    pool.dma_start(dst, src).then_inc(rows_in, 16)

                if block == 1:
                    for name, row, n in (("ffn1_pre_g", V1_PRE1, 8), ("ffn1_post_g", V1_POST1, 8), ("mix_pre_g", V1_PREM, 8),
                                         ("mix_post_g", V1_POSTM, 8), ("ffn2_pre_g", V1_PRE2, 8), ("ffn2_post_g", V1_POST2, 8),
                                         ("pool_scale", V1_PS, 2), ("conv_b", V1_CB, 2), ("conv_ln_g", V1_LG, 2), ("conv_ln_b", V1_LB, 2)):
                        rows(vrow[row:row + n], i[name][l].rearrange("(c p) -> c p", p=P))
                    rows(vrow[V1_DW:V1_N], i["conv_dw"][l].rearrange("j (c p) -> (j c) p", p=P))
                else:
                    rows(vrow[V2_G:V2_B], i["norm_g_2"][l].rearrange("k (c p) -> (k c) p", p=P))
                    rows(vrow[V2_B:V2_PE], i["ada_b_2"][l].rearrange("(k p) -> k p", p=P))
                    rows(vrow[V2_PE:V2_N].rearrange("p (v d) -> p v d", v=2), i["nsa_cmp_pe_2"][l].rearrange("v j d -> j v d"))

            def ada(l, s):
                w = i["ada_w_2"][l].rearrange("(c p) n -> p c n", p=P)
                with pool.Fori(0, 9) as k:
                    a = 18 * l + 9 * s + k
                    for h, (o, n) in reversed(list(enumerate(ADA))):
                        pool.wait_ge(ada_sum[h], a + 1)
                        pool.dma_start(ADW[h], w[:, :, bass.ds(512 * (9 * s + k) + o, n)]).then_inc(ada_in[h], 16)
                    pool.wait_ge(ada_in[1], 16 * (a + 1))
                    nc.gpsimd.tensor_tensor(ADW[1], ADW[1], spread(cond, 2, ADA[1][1]), ALU.mult).then_inc(ada_fold, 1)
                    for n, half in enumerate((4, 2)):
                        pool.wait_ge(ada_fold, 3 * a + n + 1)
                        nc.gpsimd.tensor_tensor(ADW[1][:, 0:half], ADW[1][:, 0:half], ADW[1][:, half:2 * half], ALU.add).then_inc(ada_fold, 1)
                    pool.wait_ge(ada_fold, 3 * a + 3)
                    pool.wait_ge(ada_out, a + 1)
                    nc.gpsimd.tensor_tensor(acc_ada[:, ADA_V:], ADW[1][:, 0], ADW[1][:, 1], ALU.add).then_inc(ada_sum[1], 1)

            def update(name, x):
                h, pair = HG[:, 6:8, :], XT[:, 6:8, :]
                pool.wait_ge(act_done, at("act", f"{name} hg3"))
                pool.wait_ge(dve_done, at("dve", f"{name} rstd"))
                nc.gpsimd.tensor_tensor(h, h, spread(rms[:, 1, :], 1, 2), ALU.mult).then_inc(pool_done, done("pool", f"{name} n3"))
                pool.wait_ge(pool_done, at("pool", f"{name} n3"))
                nc.gpsimd.tensor_tensor(pair, pair, h, ALU.add).then_inc(pool_done, done("pool", f"{x} 3"))

            def scale_group(p_tile, g, slot):
                pool.wait_ge(dve_done, at("dve", f"factor {g}"))
                for e in range(2):
                    for t, (o, w) in enumerate(SPAN):
                        v = p_tile[:, 2 * slot + e, o:o + w]
                        last = nc.gpsimd.tensor_tensor(v, v, window(FAC[:, g, 2 * e + t:2 * e + t + 1], [[0, w]]), ALU.mult)
                last.then_inc(pool_done, done("pool", f"p {g}"))

            pool.wait_ge(pe_done, at("pe", "vec0"))
            load_rows(1, 0)
            pool.wait_ge(act_done, at("act", "TB"))
            for block in (1, 2):
                if block == 2:
                    m.section = "between"
                    pool.wait_ge(rows_in, 16 * ROWS1 * (DEPTH + 1))
                    load_rows(2, 0)
                    pool.wait_ge(dve_done, at("dve", "x2 2", "block1"))
                    for dst, src in ((DM.rearrange("p a b -> p (a b)"), i["dilated"]), (ROPE.rearrange("p a b -> p (a b)"), i["rope"]),
                                     (SWAP, i["swap"]), (DUP.rearrange("p a b -> p (a b)"), i["dup"]),
                                     (CMK.rearrange("p a b -> p (a b)"), i["cmp_add"]), (CMB.rearrange("p a b -> p (a b)"), i["cmp_keep"])):
                        small(dst, src)
                m.section = f"block{block}"
                with pool.Fori(0, DEPTH) as l:
                    m.layer = l
                    pool.wait_ge(dve_done, at("dve", "gains"))
                    take_wait(0)
                    if block == 1:
                        small(WS, i["gm_ws"][l].rearrange("g t s -> t g s"))
                        for k in range(2):
                            small(GB[64 * k:64 * k + 64], i["gm_b"][l].rearrange("(h k) t -> k h t", k=2)[k].partition_broadcast(64))
                            small(PW[64 * k:64 * k + 64], i["pool_w"][l].rearrange("(h k) c d -> k c h d", k=2)[k])
                        small(BG, i["gm_v_g"][l].partition_broadcast(P))
                        nc.gpsimd.memset(PZ[:, :, 0:16], 0.0)
                        nc.gpsimd.memset(CH[:, :, 0:30], 0.0).then_inc(pool_done, done("pool", "pads"))
                    else:
                        for k in range(2):
                            small(W2[:, 64 * k:64 * k + 64], i["nsa_cmp_w2_2"][l, 0])
                        small(W2[:, 128:192], i["nsa_cmp_w2_2"][l, 1])
                        small(FB[:, 0:6], i["fox_f_bias_2"][l].partition_broadcast(P))
                        for part in (KEH, KEL):
                            nc.gpsimd.tensor_copy(part, window(zero[:, 0:1], [[0, 32], [0, 32]]))
                        nc.gpsimd.memset(KVC[:, T:T + 16], 0.0).then_inc(pool_done, done("pool", "pads"))
                    if block == 1:
                        ada(l, 0)
                        update("post1", "x1")
                    load_rows(block, DEPTH - 1)
                    for u in range(UNITS):
                        for work in (SIDE1 if block == 1 else SIDE2).get(u, ()):
                            if block == 1 and work == "convh":
                                pool.wait_ge(dve_done, at("dve", "convh"))
                                for tap in range(31 - POOL_TAPS, 31):
                                    first = tap == 31 - POOL_TAPS
                                    w = spread(vec[:, V1_DW + 2 * tap:V1_DW + 2 * tap + 2], 2, T)
                                    if tap > 32 - POOL_TAPS:
                                        pool.wait_ge(pool_done, at("pool", f"tap {tap - 1}"))
                                    nc.gpsimd.tensor_tensor(BT if first else REL, CH[:, :, tap:tap + T], w, ALU.mult)\
                                        .then_inc(pool_done, done("pool", f"tap {tap}" if first else f"part {tap}"))
                                    if not first:
                                        pool.wait_ge(pool_done, at("pool", f"part {tap}"))
                                        nc.gpsimd.tensor_tensor(BT, BT, REL, ALU.add).then_inc(pool_done, done("pool", f"tap {tap}"))
                            elif block == 1 and work[:2] == "qk":
                                scale_group(P1, int(work[3:]), int(work[3:]))
                            elif work == "qk d2":
                                for g in range(3):
                                    scale_group(P2, g, g)
                            elif work[:2] == "qk" and work[3] != "d":
                                g = GROUPS2.index(work[3:])
                                scale_group(P2, g, g % 3)
                        if block == 1 and u in (BR1 + 1, BR1 + 2):
                            k = u - BR1
                            for b in range(4):
                                pair = slice(2 * b, 2 * b + 2)
                                pool.wait_ge(dve_done, at("dve", f"gated {k}" if b == 3 else f"gated {k} {b}"))
                                if k == 2:
                                    pool.wait_ge(pool_done, at("pool", f"sum 1 {b}"))
                                nc.gpsimd.tensor_tensor(T8[:, pair, :], (G if k == 1 else T8)[:, pair, :], G[:, 8 * k + 2 * b:8 * k + 2 * b + 2, :],
                                                        ALU.add).then_inc(pool_done, done("pool", f"sum {k} {b}"))
                        if block == 2 and u == BR2 + 2:
                            for b in range(4):
                                pair = slice(2 * b, 2 * b + 2)
                                pool.wait_ge(dve_done, at("dve", "gated 1" if b == 3 else f"gated 1 {b}"))
                                nc.gpsimd.tensor_tensor(T8[:, pair, :], G2[:, pair, :], G2[:, 16 + 2 * b:18 + 2 * b, :],
                                                        ALU.add).then_inc(pool_done, done("pool", f"sum 1 {b}"))
                    if block == 1:
                        update("postm", "xm")
                    if block == 1:
                        pool.wait_ge(dve_done, at("dve", "xm 2"))
                        take_wait(1)
                        ada(l, 1)
                        update("post2", "x2")

        def split_pieces(block, pos, s, dst):
            u = pos - UNITS
            if block == 1 and u == IDX_U:
                a, b = dst[:, s, 0:8 * 260].rearrange("p (c n) -> p c n", n=260), raw[:, s, 0:8 * 164].rearrange("p (c n) -> p c n", n=164)
                return [(a[:, :, 0:128], b[:, :, 0:128]),
                        (a[:, :, 128:256].rearrange("p c (k n) -> p c k n", k=4), spread(b[:, :, 128:160], 2, 4)),
                        (a[:, :, 256:260], b[:, :, 160:164])]
            n = 2048
            if block == 2 and u == VG_U:
                n = 8 * 140
            if block == 2 and u == DVF_U:
                n = 8 * 262
            return [(dst[:, s, 0:n], raw[:, s, 0:n])]

        @block_.scalar
        def _(act):
            def split_hi(block, l, q, s, pos=0):
                n = unit_number(block, l, 3 * q + s)
                act.wait_ge(raw_ready[s], 32 * ((block - 1) * DEPTH * UNITS + l * UNITS + q + 1))
                act.wait_ge(unit_used, n + 1)
                for dst, src in split_pieces(block, pos, s, hi):
                    last = nc.scalar.activation(dst, src, ACT.Copy)
                last.then_inc(hi_ready, 1)

            def settle():
                act.wait_ge(act_done, at("act", m.newest["act"]))

            def unit_out(block, l, q, s):
                act.wait_ge(unit_used, unit_number(block, l, 3 * q + s) + 4)

            def root(name, bank, o=0):
                act.wait_ge(pe_done, at("pe", name + " stat"))
                nc.scalar.activation(rms[:, 0, :], ps[:, bank, o:o + T], ACT.Sqrt, bias=eps).then_inc(act_done, done("act", name + " root"))

            def squares(name, x, block):
                for b in UPDATES[block]:
                    if x and block == 1 and b == 3:
                        act.wait_ge(pool_done, at("pool", f"{x} 3"))
                    elif x:
                        act.wait_ge(dve_done, at("dve", f"{x} {b}"))
                    nc.scalar.activation(T8[:, 2 * b:2 * b + 2, :], XT[:, 2 * b:2 * b + 2, :], ACT.Square)\
                        .then_inc(act_done, done("act", f"{name} sq{b}"))
                root(name, 3)

            def pre(name, shift):
                for c in range(C):
                    act.wait_ge(dve_done, at("dve", f"{name} n{c}"))
                    if shift is None:
                        ins = nc.scalar.activation(NH[:, c, :], T8[:, c, :], ACT.Copy)
                    else:
                        ins = nc.scalar.activation(NH[:, c, :], T8[:, c, :], ACT.Identity, bias=modl[:, shift + c:shift + c + 1])
                    ins.then_inc(act_done, done("act", f"{name} h{c}"))

            def down_out(block, l, name, q, b):
                if name == "prem":
                    unit_out(block, l, 20 + (2 + b) // 3, (2 + b) % 3)
                elif b < 3:
                    act.wait_ge(pe_done, at("pe", f"{name} down {b}"))
                else:
                    unit_out(block, l, q, 2)

            def post(name, block, l, before, q, gain):
                nc.scalar.activation(rms[:, 0, 0:1], eps, ACT.Sqrt)
                for b in range(4):
                    down_out(block, l, before, q, b)
                    nc.scalar.activation(T8[:, 2 * b:2 * b + 2, :].rearrange("p a t -> p (a t)"), ps[:, 4 + b, :],
                                         ACT.Square).then_inc(act_done, done("act", f"{name} sq{b}"))
                for b in UPDATES[1]:
                    for c in (2 * b, 2 * b + 1):
                        ins = nc.scalar.activation(HG[:, c, :], ps[:, 4 + b, T * (c % 2):T * (c % 2) + T], ACT.Copy, scale=gain[:, c:c + 1])
                    ins.then_inc(act_done, done("act", f"{name} hg{b}"))
                root(name, 3)

            def silu(block, l, F, f, q, s, bank, par):
                unit_out(block, l, q, s)
                nc.scalar.activation(SA[:, par, :], ps[:, bank, 0:T], ACT.Silu).then_inc(silu_ready, 1)

            def hidden_parts(F, f, place=0):
                for k in range(2):
                    act.wait_ge(hidden_ready, NF * F + f + k + 1)
                    nc.scalar.activation(BH[:, place + k, :], HF[:, k, :], ACT.Copy).then_inc(hidden_hi, 1)

            def ffn(block, l, b, F, last_of_layer):
                split_hi(block, l, b, 2)
                silu(block, l, F, 0, b, 0, 0, 0)
                split_hi(block, l, b + 1, 0)
                silu(block, l, F, 1, b, 1, 1, 1)
                hidden_parts(F, 0)

                def body(i, more):
                    split_hi(block, l, b + i, 1)
                    silu(block, l, F, 2 * i, b + i - 1, 2, 2, 0)
                    if more is not None:
                        split_hi(block, l, b + i, 2, more)
                    silu(block, l, F, 2 * i + 1, b + i, 0, 0, 1)
                    if more is not None and not (last_of_layer and more == -1):
                        split_hi(block, l, b + i + 1, 0, 0 if more != -1 else b * 3 + UNITS)
                    if more == -1:
                        hidden_parts(F, 2 * i, 2)
                        return
                    unit_out(block, l, b + i, 1)
                    hidden_parts(F, 2 * i)

                with act.Fori(1, NF // 2 - 1) as i:
                    body(i, 0)
                body(NF // 2 - 1, -1)
                if not last_of_layer:
                    split_hi(block, l, b + 11, 1, b * 3 + UNITS + 1)

            def softmax_exp(p_tile, g, slot):
                act.wait_ge(dve_done, at("dve", f"nm {g}"))
                for e in range(2):
                    for t, (o, w) in enumerate(SPAN):
                        v = p_tile[:, 2 * slot + e, o:o + w]
                        k = 2 * e + t
                        last = nc.scalar.activation(v, v, ACT.Exp, bias=NM[:, g, k:k + 1], scale=-1.0, accum_out=DEN[:, g, k:k + 1])
                last.then_inc(act_done, done("act", f"exp {g}"))

            def turned_out(g):
                act.wait_ge(pe_done, at("pe", f"tr {g}"))
                for e in range(2):
                    last = nc.scalar.activation(PT[:, e, :], ps[:, 5 + e, 0:CAUSAL], ACT.Copy)
                last.then_inc(act_done, done("act", f"pt {g}"))

            def heads_out(name, chunk):
                act.wait_ge(pe_done, at("pe", f"pv {name}"))
                nc.scalar.activation(BH[:, chunk, :], ps[:, 7, 0:T], ACT.Copy).then_inc(act_done, done("act", f"bh {chunk}"))

            def evac1(l, u):
                if u < BR1:
                    unit_out(1, l, 11 + u // 3, u % 3)
                bank = ps[:, u % 3, :]
                if u in (U_GATE, V_GATE):
                    ins = nc.scalar.activation((UT if u == U_GATE else VG)[:, :, :], bank.rearrange("p (a t) -> p a t", a=2), ACT.Gelu_apprx_tanh)
                elif u == POOL_U:
                    act.wait_ge(pool_done, at("pool", "pads"))
                    ins = nc.scalar.activation(PZ[:, :, 16:16 + T], bank.rearrange("p (a t) -> p a t", a=2), ACT.Copy)
                elif u in (Q_U, K_U, V_U, IDX_U, CONV_A):
                    dst = {Q_U: QT, K_U: KT, V_U: VT, IDX_U: QKI, CONV_A: CA}[u]
                    ins = nc.scalar.activation(dst, bank.rearrange("p (a t) -> p a t", a=2), ACT.Copy)
                    if u == IDX_U:
                        ins = nc.scalar.activation(WI.rearrange("p a b -> p (a b)"), ps[:, 7, 0:8], ACT.Copy, scale=0.5)
                elif u == CONV_G:
                    ins = nc.scalar.activation(SG, bank.rearrange("p (a t) -> p a t", a=2), ACT.Sigmoid)
                elif u < BR1:
                    k = 2 * (u - GATES1)
                    ins = nc.scalar.activation(G[:, k:k + 2, :], bank.rearrange("p (a t) -> p a t", a=2), ACT.Sigmoid)
                else:
                    return
                ins.then_inc(act_done, done("act", f"ev {u}"))

            def side1(l, work):
                if work == "gm1":
                    act.wait_ge(dve_done, at("dve", "b0"))
                    nc.scalar.activation(BH[:, 0:2, :], BT, ACT.Copy).then_inc(act_done, done("act", "bh b0"))
                elif work == "pool1":
                    act.wait_ge(pe_done, at("pe", "pw"))
                    act.wait_ge(dve_done, at("dve", "bl b0"))
                    for c in range(2):
                        ins = nc.scalar.activation(BT[:, c, :], ps[:, 3, T * c:T * c + T], ACT.Copy, scale=vec[:, V1_PS + c:V1_PS + c + 1])
                    ins.then_inc(act_done, done("act", "b1"))
                    act.wait_ge(act_done, at("act", "b1"))
                    nc.scalar.activation(BH[:, 2:4, :], BT, ACT.Copy).then_inc(act_done, done("act", "bh b1"))
                elif work[:3] == "idx":
                    t = int(work[4:])
                    o, w = SPAN[t]
                    act.wait_ge(pe_done, at("pe", work))
                    for h in range(4):
                        if h >= 2 or t:
                            act.wait_ge(dve_done, at("dve", f"score {t} {h - 2}" if h >= 2 else f"score 0 {h + 2}"))
                        nc.scalar.activation(REL[:, h % 2, 0:w], ps[:, 3 + h, 0:w], ACT.Relu, scale=32 ** -0.5)\
                            .then_inc(act_done, done("act", f"rel {t} {h}"))
                elif work == "ln1":
                    act.wait_ge(dve_done, at("dve", "xc"))
                    act.wait_ge(dve_done, at("dve", "bl b1"))
                    nc.scalar.activation(BT, ACC, ACT.Square).then_inc(act_done, done("act", "xcsq"))
                elif work == "gm0":
                    act.wait_ge(dve_done, at("dve", "gm ms"))
                    nc.scalar.activation(ms[:, 2:4], ms[:, 0:2], ACT.Sqrt).then_inc(act_done, done("act", "gm root"))
                elif work == "ln2":
                    root("ln", 7, T)
                elif work == "ln3":
                    act.wait_ge(dve_done, at("dve", "lnx"))
                    for c in range(2):
                        ins = nc.scalar.activation(BT[:, c, :], ACC[:, c, :], ACT.Silu, bias=vec[:, V1_LB + c:V1_LB + c + 1],
                                                   scale=vec[:, V1_LG + c:V1_LG + c + 1])
                    ins.then_inc(act_done, done("act", "b3"))
                    act.wait_ge(act_done, at("act", "b3"))
                    nc.scalar.activation(BH[:, 6:8, :], BT, ACT.Copy).then_inc(act_done, done("act", "bh b3"))
                elif work[:2] == "tr":
                    turned_out(int(work[3:]))
                elif work[:2] == "pv":
                    heads_out(work[3:], 4 + int(work[3:]))

            def evac2(l, u):
                if u < BR2 and u not in (W1_U, W1_U + 1):
                    unit_out(2, l, 11 + u // 3, u % 3)
                bank = ps[:, u % 3, :]
                pair = bank.rearrange("p (a t) -> p a t", a=2)
                if u in ROPED:
                    if u in ROPED[2:]:
                        act.wait_ge(dve_done, at("dve", f"rope {({3: 1, 4: 0, 5: 3})[u]}"))
                    ins = nc.scalar.activation(Z[:, u % 2], pair, ACT.Copy)
                elif u == VG_U:
                    v = bank[:, 0:280].rearrange("p (a t) -> p a t", a=2)
                    nc.scalar.activation(VSW, v, ACT.Copy)
                    ins = nc.scalar.activation(GT, v[:, :, 128:140], ACT.Sigmoid)
                elif u in (FQK_U, FQK_U + 1, FQK_U + 2):
                    ins = nc.scalar.activation(FQK[:, 2 * (u - FQK_U):2 * (u - FQK_U) + 2, :], pair, ACT.Copy)
                elif u == DV_U or u == FV_U:
                    ins = nc.scalar.activation((DV if u == DV_U else FV)[:, :, 0:T], pair, ACT.Copy)
                elif u == DVF_U:
                    for t in range(2):
                        src = (bank, ps[:, 6, :])[t]
                        nc.scalar.activation(DV[:, t, T:T + P], src[:, 0:P], ACT.Copy)
                        nc.scalar.activation(FV[:, t, T:T + P], src[:, P:T], ACT.Copy)
                        ins = nc.scalar.activation(FL[:, t, 0:6], src[:, T:T + 6], ACT.Copy)
                elif GATES2 <= u < BR2:
                    k = 2 * (u - GATES2)
                    ins = nc.scalar.activation(G2[:, k:k + 2, :], pair, ACT.Sigmoid)
                else:
                    return
                ins.then_inc(act_done, done("act", f"ev {u}"))

            def side2(l, work):
                what, _, g = work.partition(" ")
                if work == "dup":
                    act.wait_ge(pe_done, at("pe", "dup"))
                    nc.scalar.activation(KSD, ps[:, 3, :].rearrange("p (a t) -> p a t", a=2), ACT.Copy).then_inc(act_done, done("act", "ksd"))
                elif work == "ke":
                    act.wait_ge(dve_done, at("dve", "ke"))
                    act.wait_ge(pool_done, at("pool", "pads"))
                    for kv in range(2):
                        rows = slice(64 * kv, 64 * kv + 64)
                        ins = nc.scalar.activation(KEH[rows, :, 16 * kv:16 * kv + 16], KE[rows].rearrange("p a t -> p (a t)")
                                                   .rearrange("p (j n) -> p j n", n=16), ACT.Copy)
                    ins.then_inc(act_done, done("act", "keh"))
                elif work == "lf":
                    act.wait_ge(dve_done, at("dve", "fx"))
                    nc.scalar.activation(LE[:, :, 0:6], LF[:, :, 0:6], ACT.Abs).then_inc(act_done, done("act", "fabs"))
                    act.wait_ge(act_done, at("act", "fabs"))
                    nc.scalar.activation(LE[:, :, 0:6], LE[:, :, 0:6], ACT.Exp, scale=-1.0).then_inc(act_done, done("act", "fexp"))
                    act.wait_ge(dve_done, at("dve", "fexp1"))
                    nc.scalar.activation(LE[:, :, 0:6], LE[:, :, 0:6], ACT.Ln).then_inc(act_done, done("act", "fln"))
                elif work == "fox":
                    act.wait_ge(pe_done, at("pe", "fox"))
                    nc.scalar.activation(CT, ps[:, 7, 0:16].rearrange("p (a b) -> p a b", a=2), ACT.Copy)
                    for k, b in enumerate((3, 4)):
                        nc.scalar.activation(CS[:, 2 * k:2 * k + 2, :], ps[:, b, :].rearrange("p (a t) -> p a t", a=2), ACT.Copy)
                    for k in range(2):
                        ins = nc.scalar.activation(CS[:, 4 + k, :], ps[:, 5 + k, 0:T], ACT.Copy)
                    ins.then_inc(act_done, done("act", "cs"))
                elif work == "hid":
                    unit_out(2, l, 11 + (W1_U + 1) // 3, (W1_U + 1) % 3)
                    nc.scalar.activation(HT[0:32], ps[0:32, 0, 0:P], ACT.Silu).then_inc(act_done, done("act", "hid"))
                elif work == "hidt":
                    act.wait_ge(pe_done, at("pe", "hidt"))
                    nc.scalar.activation(HID.rearrange("p a b -> p (a b)"), ps[:, 3, 448:480], ACT.Copy).then_inc(act_done, done("act", "hidt"))
                elif work == "w2":
                    act.wait_ge(pe_done, at("pe", "w2"))
                    nc.scalar.activation(KC2, ps[:, 3, 384:400], ACT.Copy)
                    nc.scalar.activation(VC2[0:16], ps[0:16, 4, 384:448], ACT.Copy).then_inc(act_done, done("act", "w2"))
                elif work == "cqk":
                    act.wait_ge(dve_done, at("dve", "cnm"))
                    nc.scalar.activation(PC, PC, ACT.Exp, scale=0.125).then_inc(act_done, done("act", "cexp"))
                elif work == "ctr":
                    act.wait_ge(pe_done, at("pe", "ctr"))
                    for e in range(2):
                        ins = nc.scalar.activation(PTC[0:16, 2 * e:2 * e + 2, :], ps[0:16, 5 + e, :].rearrange("p (a t) -> p a t", a=2), ACT.Copy)
                    ins.then_inc(act_done, done("act", "ptc"))
                elif what == "tr":
                    turned_out(GROUPS2.index(g))
                elif what == "pv" and g in CHUNK2:
                    heads_out(GROUPS2.index(g), CHUNK2[g])

            def exps(block, works):
                for work in works:
                    if work[:2] != "qk":
                        continue
                    settle()
                    if block == 1:
                        softmax_exp(P1, int(work[3:]), int(work[3:]))
                    else:
                        k = GROUPS2.index(work[3:])
                        softmax_exp(P2, k, k % 3)
                        if work == "qk d2":
                            act.wait_ge(dve_done, at("dve", "dmax"))
                            nc.scalar.activation(DE[:, 0, :], DE[:, 0, :], ACT.Exp).then_inc(act_done, done("act", "dexp"))

            def gated_parts():
                for b in range(4):
                    act.wait_ge(dve_done, at("dve", f"y {b}"))
                    nc.scalar.activation(NH[:, 2 * b:2 * b + 2, :], T8[:, 2 * b:2 * b + 2, :], ACT.Copy).then_inc(act_done, done("act", f"yh {b}"))

            m.section = "setup"
            act.wait_ge(pe_done, at("pe", "vec0"))
            nc.scalar.activation(vec0, ps[:, 0, 0:16], ACT.Copy).then_inc(act_done, done("act", "vec0"))
            act.wait_ge(act_done, at("act", "vec0"))
            nc.scalar.activation(cond, vec0[:, 0:8], ACT.Silu)
            act.wait_ge(pe_done, at("pe", "bias rows"))
            nc.scalar.activation(bias_rows.rearrange("p a b -> p (a b)")[0:4], ps[0:4, 1, :], ACT.Copy).then_inc(act_done, done("act", "bias rows"))
            act.wait_ge(pe_done, at("pe", "xT"))
            for b in range(4):
                ins = nc.scalar.activation(XT[:, 2 * b:2 * b + 2, :].rearrange("p a t -> p (a t)"), ps[:, 4 + b, :], ACT.Copy)
            ins.then_inc(act_done, done("act", "XT"))
            act.wait_ge(act_done, at("act", "XT"))
            act.wait_ge(pool_done, at("pool", "eps"))
            squares("next", None, 2)
            act.wait_ge(pe_done, at("pe", "TB"))
            for h in range(4):
                ins = nc.scalar.activation(TB[:, h, :], ps[:, h, 0:CAUSAL], ACT.Copy, scale=8.0)
            ins.then_inc(act_done, done("act", "TB"))

            for block in (1, 2):
                m.section = f"block{block}"
                with act.Fori(0, DEPTH) as l:
                    m.layer = l
                    split_hi(block, l, 0, 0)
                    act.wait_ge(pe_done, at("pe", "vec"))
                    n = V1_N if block == 1 else V2_N
                    nc.scalar.activation(vec[:, 0:n], ps[:, 1, 0:n], ACT.Copy).then_inc(act_done, done("act", "vec"))
                    if block == 2:
                        act.wait_ge(dve_done, at("dve", "gains"))
                    F = ((block - 1) * DEPTH + l) * 2
                    shifts = (None, None, None) if block == 1 else (0, 24, 48)
                    pre("pre1", shifts[0])
                    split_hi(block, l, 0, 1)
                    ffn(block, l, 0, F, False)
                    if block == 1:
                        post("post1", block, l, "pre1", 10, vec[:, V1_POST1:V1_POST1 + 8])
                    squares("prem", "x1", block)
                    pre("prem", shifts[1])
                    for u in range(UNITS):
                        p = u + 2
                        split_hi(block, l, 11 + p // 3, p % 3, UNITS + p)
                        exps(block, (SIDE1 if block == 1 else SIDE2).get(u - 1, ()))
                        (evac1 if block == 1 else evac2)(l, u)
                        for work in (SIDE1 if block == 1 else SIDE2).get(u, ()):
                            settle()
                            (side1 if block == 1 else side2)(l, work)
                        if u == (BR1 + 3 if block == 1 else BR2 + 2):
                            gated_parts()
                    if block == 1:
                        post("postm", block, l, "prem", 21, vec[:, V1_POSTM:V1_POSTM + 8])
                    squares("pre2", "xm", block)
                    pre("pre2", shifts[2])
                    ffn(block, l, 22, F + 1, True)
                    if block == 1:
                        post("post2", block, l, "pre2", 32, vec[:, V1_POST2:V1_POST2 + 8])
                    squares("next", "x2", block)
            m.section = "end"
            for j in range(4):
                act.wait_ge(pe_done, at("pe", f"out {j}"))
                for b in (j, 4 + j):
                    ins = nc.scalar.activation(OUT[:, b, :], ps[:, b, 0:T], ACT.Copy)
            ins.then_inc(act_done, done("act", "out"))

        @block_.vector
        def _(dve):
            def mine(what):
                dve.wait_ge(dve_done, at("dve", what))

            def settle():
                mine(m.newest["dve"])

            def take_wait():
                nc.vector.memset(tick[:, 0:1], 0.0)

            def split_lo(block, l, q, s, pos=0):
                dve.wait_ge(hi_ready, unit_number(block, l, 3 * q + s) + 1)
                for (dst, src), (part, _) in zip(split_pieces(block, pos, s, lo), split_pieces(block, pos, s, hi)):
                    last = nc.vector.tensor_tensor(dst, src, part.bitcast(F32), ALU.subtract)
                last.then_inc(lo_ready, 1)

            def inverse_root(name, v, plus, r, root, step):
                dve.wait_ge(act_done, at("act", name + " root"))
                nc.vector.reciprocal(r, root).then_inc(dve_done, done("dve", name + " recip"))
                mine(name + " recip")
                nc.vector.scalar_tensor_tensor(out=step, in0=v, scalar=plus, in1=r, op0=ALU.add, op1=ALU.mult).then_inc(dve_done, done("dve", name + " vr"))
                mine(name + " vr")
                nc.vector.scalar_tensor_tensor(out=step, in0=step, scalar=-0.5, in1=r, op0=ALU.mult, op1=ALU.mult)\
                    .then_inc(dve_done, done("dve", name + " vrr"))
                mine(name + " vrr")
                nc.vector.scalar_tensor_tensor(out=r, in0=step, scalar=1.5, in1=r, op0=ALU.add, op1=ALU.mult)\
                    .then_inc(dve_done, done("dve", name + " rstd"))
                mine(name + " rstd")

            def mean_square(name, bank=3, o=0):
                inverse_root(name, ps[:, bank, o:o + T], EPS, rms[:, 1, :], rms[:, 0, :], rms[:, 2, :])

            def pre(name, gain, shift):

                def scaled(c):
                    nc.vector.scalar_tensor_tensor(out=T8[:, c, :], in0=XT[:, c, :], scalar=gain[:, c:c + 1], in1=rms[:, 1, :],
                                                   op0=ALU.mult, op1=ALU.mult).then_inc(dve_done, done("dve", f"{name} n{c}"))

                scaled(0)
                for c in range(C):
                    if c + 1 < C:
                        scaled(c + 1)
                    dve.wait_ge(act_done, at("act", f"{name} h{c}"))
                    part = NH[:, c, :].bitcast(F32)
                    if shift is None:
                        ins = nc.vector.tensor_tensor(NL[:, c, :], T8[:, c, :], part, ALU.subtract)
                    else:
                        ins = nc.vector.scalar_tensor_tensor(out=NL[:, c, :], in0=T8[:, c, :], scalar=modl[:, shift + c:shift + c + 1],
                                                             in1=part, op0=ALU.add, op1=ALU.subtract)
                    ins.then_inc(dve_done, done("dve", f"{name} l{c}"))

            def post(name, x):
                mean_square(name)

                def scaled(b):
                    dve.wait_ge(act_done, at("act", f"{name} hg{b}"))
                    h = HG[:, 2 * b:2 * b + 2, :]
                    nc.vector.tensor_tensor(h, h, spread(rms[:, 1, :], 1, 2), ALU.mult).then_inc(dve_done, done("dve", f"{name} n{b}"))

                scaled(0)
                for b in range(3):
                    if b < 2:
                        scaled(b + 1)
                    mine(f"{name} n{b}")
                    pair = XT[:, 2 * b:2 * b + 2, :]
                    nc.vector.tensor_tensor(pair, pair, HG[:, 2 * b:2 * b + 2, :], ALU.add).then_inc(dve_done, done("dve", f"{x} {b}"))
                mine(x + " 2")

            def gated_add(gate, x, l, before, q):
                for c in range(C):
                    b = c // 2
                    if c % 2 == 0:
                        if before == "prem":
                            dve.wait_ge(unit_used, unit_number(2, l, 62 + b) + 4)
                        elif b < 3:
                            dve.wait_ge(pe_done, at("pe", f"{before} down {b}"))
                        else:
                            dve.wait_ge(unit_used, unit_number(2, l, 3 * q + 2) + 4)
                    ins = nc.vector.scalar_tensor_tensor(out=XT[:, c, :], in0=ps[:, 4 + c // 2, T * (c % 2):T * (c % 2) + T],
                                                         scalar=gate[:, c:c + 1], in1=XT[:, c, :], op0=ALU.mult, op1=ALU.add)
                    if c % 2:
                        ins.then_inc(dve_done, done("dve", f"{x} {c // 2}"))
                mine(x + " 3")

            def gate_times_up(F, f, bank, par):
                dve.wait_ge(silu_ready, NF * F + f + 1)
                if not isinstance(f, int) or f >= 2:
                    dve.wait_ge(hidden_lo, NF * F + f - 1)
                nc.vector.tensor_tensor(HF[:, par, :], SA[:, par, :], ps[:, bank, T:2 * T], ALU.mult).then_inc(hidden_ready, 1)

            def hidden_parts(F, f, place=0):
                for k in range(2):
                    dve.wait_ge(hidden_hi, NF * F + f + k + 1)
                    nc.vector.tensor_tensor(BL[:, place + k, :], HF[:, k, :], BH[:, place + k, :].bitcast(F32), ALU.subtract).then_inc(hidden_lo, 1)

            def ada_column(a):
                dve.wait_ge(ada_in[0], 16 * (a + 1))
                for c in range(C):
                    if c == 0:
                        ins = nc.vector.tensor_scalar(acc_ada[:, 0:ADA_V], ADW[0][:, c, :], cond[:, 0:1], None, ALU.mult)
                    else:
                        dve.wait_ge(ada_step, 7 * a + c)
                        ins = nc.vector.scalar_tensor_tensor(out=acc_ada[:, 0:ADA_V], in0=ADW[0][:, c, :], scalar=cond[:, c:c + 1],
                                                             in1=acc_ada[:, 0:ADA_V], op0=ALU.mult, op1=ALU.add)
                    ins.then_inc(ada_step if c < C - 1 else ada_sum[0], 1)

            def ffn(block, l, b, F, last_of_layer, half):
                split_lo(block, l, b, 2)
                gate_times_up(F, 0, 0, 0)
                split_lo(block, l, b + 1, 0)
                gate_times_up(F, 1, 1, 1)
                hidden_parts(F, 0)

                def body(i, more):
                    a = 18 * l + 9 * half + i - 1
                    split_lo(block, l, b + i, 1)
                    gate_times_up(F, 2 * i, 2, 0)
                    if block == 1 and not (isinstance(i, int) and i == 1):
                        dve.wait_ge(ada_out, a + 1)
                        nc.vector.tensor_copy(mods.rearrange("p a b -> p (a b)")[:, bass.ds(4 * a - 4, 4)], ps[:, 1, 0:4]).then_inc(ada_kept, 1)
                    if more != -1 and block == 1:
                        ada_column(a)
                    split_lo(block, l, b + i, 2)
                    gate_times_up(F, 2 * i + 1, 0, 1)
                    if not (last_of_layer and more == -1):
                        split_lo(block, l, b + i + 1, 0)
                    hidden_parts(F, 2 * i, 2 if more == -1 else 0)

                body(1, 0)
                with dve.Fori(2, NF // 2 - 1) as i:
                    body(i, 0)
                body(NF // 2 - 1, -1)
                if not last_of_layer:
                    split_lo(block, l, b + 11, 1, b * 3 + UNITS + 1)

            def negated_logits(p_tile, g, slot, masks, by_head=None):
                dve.wait_ge(pe_done, at("pe", f"qk {g}"))
                if by_head is None:
                    take_wait()
                else:
                    for e in range(2):
                        last = nc.vector.tensor_tensor(p_tile[:, 2 * slot + e, :], ps[:, 3 + e, 0:CAUSAL], by_head(e), ALU.add)
                    last.then_inc(dve_done, done("dve", f"biased {g}"))
                    mine(f"biased {g}")
                    take_wait()
                for e in range(2):
                    for t, (o, w) in enumerate(SPAN):
                        v = p_tile[:, 2 * slot + e, o:o + w]
                        scores = ps[:, 3 + e, o:o + w] if by_head is None else v
                        k = 2 * e + t
                        last = nc.vector.tensor_tensor_reduce(v, scores, masks(e)[:, o:o + w], -0.125, 3e38, ALU.add, ALU.min, NM[:, g, k:k + 1])
                last.then_inc(dve_done, done("dve", f"nm {g}"))

            def factor(g, gate=None):
                dve.wait_ge(act_done, at("act", f"exp {g}"))
                if gate is None:
                    nc.vector.reciprocal(FAC[:, g, :], DEN[:, g, :]).then_inc(dve_done, done("dve", f"factor {g}"))
                else:
                    nc.vector.reciprocal(FAC[:, g, :], DEN[:, g, :]).then_inc(dve_done, done("dve", f"recip {g}"))
                    mine(f"recip {g}")
                    nc.vector.tensor_tensor(window(FAC[:, g, :], [[2, 2], [1, 2]]), window(FAC[:, g, :], [[2, 2], [1, 2]]), gate, ALU.mult)\
                        .then_inc(dve_done, done("dve", f"factor {g}"))

            def heads_rest(chunk):
                dve.wait_ge(act_done, at("act", f"bh {chunk}"))
                nc.vector.tensor_tensor(BL[:, chunk, :], ps[:, 7, 0:T], BH[:, chunk, :].bitcast(F32), ALU.subtract)\
                    .then_inc(dve_done, done("dve", f"bl {chunk}"))

            def branch_rest(k):
                dve.wait_ge(act_done, at("act", f"bh b{k}"))
                nc.vector.tensor_tensor(BL[:, 2 * k:2 * k + 2, :], BT, BH[:, 2 * k:2 * k + 2, :].bitcast(F32), ALU.subtract)\
                    .then_inc(dve_done, done("dve", f"bl b{k}"))

            def side1(l, work):
                what, _, g = work.partition(" ")
                if work == "gm0":
                    dve.wait_ge(act_done, at("act", f"ev {V_GATE}"))
                    take_wait()
                    for t in range(2):
                        last = nc.vector.tensor_tensor_reduce(PD[:, t, :], VG[:, t, :], VG[:, t, :], 1.0, 0.0, ALU.mult, ALU.add, ms[:, t:t + 1])
                    last.then_inc(dve_done, done("dve", "gm sum"))
                    mine("gm sum")
                    nc.vector.tensor_scalar(ms[:, 0:2], ms[:, 0:2], 1.0 / 256, EPS, ALU.mult, ALU.add).then_inc(dve_done, done("dve", "gm ms"))
                    dve.wait_ge(pe_done, at("pe", "wsT"))
                    nc.vector.tensor_tensor(WST, ps[:, 3, :].rearrange("p (g t) -> p g t", g=4), spread(tri[:, 0:P], 1, 4), ALU.mult)\
                        .then_inc(dve_done, done("dve", "WST"))
                    inverse_root("gm", ms[:, 0:2], 0.0, ms[:, 4:6], ms[:, 2:4], ms[:, 6:8])
                    for t in range(2):
                        last = nc.vector.scalar_tensor_tensor(out=VG[:, t, :], in0=VG[:, t, :], scalar=ms[:, 4 + t:5 + t], in1=BG,
                                                              op0=ALU.mult, op1=ALU.mult)
                    last.then_inc(dve_done, done("dve", "VN"))
                elif work == "gm1":
                    dve.wait_ge(pe_done, at("pe", "mixed"))
                    for c in range(2):
                        last = nc.vector.tensor_tensor(BT[:, c, :].rearrange("p (a t) -> p a t", a=2), ps[:, 3, T * c:T * c + T].rearrange("p (a t) -> p a t", a=2),
                                                       spread(GB[:, c, :], 1, 2), ALU.add)
                    last.then_inc(dve_done, done("dve", "mixed"))
                    mine("mixed")
                    nc.vector.tensor_tensor(BT, BT, UT, ALU.mult).then_inc(dve_done, done("dve", "b0"))
                    branch_rest(0)
                elif work == "pool0":
                    dve.wait_ge(act_done, at("act", f"ev {POOL_U}"))
                    A, B, n = SC, WK, 16 + T
                    for k, (dst, src, w, c) in enumerate(((A, PZ, 1, 0), (B, A, 2, 0), (A, B, 4, 1), (B, A, 8, 1))):
                        lo_x = 2 * w - 1
                        nc.vector.tensor_tensor(dst[:, c:2, lo_x:n], src[:, c:2, lo_x:n], src[:, c:2, lo_x - w:n - w], ALU.add)\
                            .then_inc(dve_done, done("dve", f"window {k}"))
                        mine(f"window {k}")
                    for k, W in enumerate((A, B)):
                        rows = slice(64 * k, 64 * k + 64)
                        last = nc.vector.tensor_tensor(PD[rows], W[rows, :, 16:n], RC[rows], ALU.mult)
                    last.then_inc(dve_done, done("dve", "means"))
                    mine("means")
                    nc.vector.tensor_tensor(PD, PD, PZ[:, :, 16:n], ALU.subtract).then_inc(dve_done, done("dve", "pd"))
                elif work == "pool1":
                    branch_rest(1)
                elif what == "idx":
                    t = int(g)
                    o, w = SPAN[t]
                    for h in range(4):
                        dve.wait_ge(act_done, at("act", f"rel {t} {h}"))
                        if h == 0:
                            if t == 0:
                                mine("pd")
                            ins = nc.vector.tensor_scalar(SCf[:, o:o + w], REL[:, 0, 0:w], WI[:, t, 0:1], None, ALU.mult)
                        else:
                            mine(f"score {t} {h - 1}")
                            ins = nc.vector.scalar_tensor_tensor(out=SCf[:, o:o + w], in0=REL[:, h % 2, 0:w], scalar=WI[:, t, h:h + 1],
                                                                 in1=SCf[:, o:o + w], op0=ALU.mult, op1=ALU.add)
                        ins.then_inc(dve_done, done("dve", f"score {t} {h}"))
                    mine(f"score {t} 3")
                    nc.vector.tensor_tensor(WKf[:, o:o + w], SCf[:, o:o + w], causal[:, o:o + w], ALU.add).then_inc(dve_done, done("dve", f"scores {t}"))
                elif work == "convh":
                    dve.wait_ge(act_done, at("act", f"ev {CONV_G}"))
                    dve.wait_ge(pool_done, at("pool", "pads"))
                    nc.vector.tensor_tensor(CH[:, :, 30:30 + T], CA, SG, ALU.mult).then_inc(dve_done, done("dve", "convh"))
                elif what == "top":
                    j = int(g)
                    mine(f"taken {j - 1}" if j else "scores 1")
                    take_wait()
                    for t, (o, w) in enumerate(SPAN):
                        last = nc.vector.max(M8[:, t, :], WKf[:, o:o + w])
                    last.then_inc(dve_done, done("dve", f"best {j}"))
                    mine(f"best {j}")
                    take_wait()
                    for t, (o, w) in enumerate(SPAN):
                        last = nc.vector.match_replace(WKf[:, o:o + w], M8[:, t, :], WKf[:, o:o + w], TAKEN)
                    last.then_inc(dve_done, done("dve", f"taken {j}"))
                    if j == 7:
                        mine("taken 7")
                        nc.vector.tensor_scalar(SM, WKf[:, 0:CAUSAL], -2e38, NEG, ALU.is_ge, ALU.mult).then_inc(dve_done, done("dve", "not taken"))
                        mine("not taken")
                        nc.vector.tensor_tensor(SM, SM, causal, ALU.add).then_inc(dve_done, done("dve", "SM"))
                        mine("SM")
                elif what == "tap":
                    j = int(g)
                    n = 31 - POOL_TAPS
                    for tap in range(n * j // 8, n * (j + 1) // 8):
                        mine(f"tap {tap - 1}" if tap else "convh")
                        for c in range(2):
                            w = vec[:, V1_DW + 2 * tap + c:V1_DW + 2 * tap + c + 1]
                            if tap == 0:
                                last = nc.vector.tensor_scalar(ACC[:, c, :], CH[:, c, 0:T], w, vec[:, V1_CB + c:V1_CB + c + 1], ALU.mult, ALU.add)
                            else:
                                last = nc.vector.scalar_tensor_tensor(out=ACC[:, c, :], in0=CH[:, c, tap:tap + T], scalar=w,
                                                                      in1=ACC[:, c, :], op0=ALU.mult, op1=ALU.add)
                        last.then_inc(dve_done, done("dve", f"tap {tap}"))
                    if j == 7:
                        mine(f"tap {n - 1}")
                        dve.wait_ge(pool_done, at("pool", "tap 30"))
                        nc.vector.tensor_tensor(ACC, ACC, BT, ALU.add).then_inc(dve_done, done("dve", "conv"))
                elif work == "ln1":
                    dve.wait_ge(pe_done, at("pe", "lnmean"))
                    nc.vector.tensor_tensor(ACC, ACC, spread(ps[:, 7, 0:T], 1, 2), ALU.subtract).then_inc(dve_done, done("dve", "xc"))
                elif work == "ln2":
                    mean_square("ln", 7, T)
                    nc.vector.tensor_tensor(ACC, ACC, spread(rms[:, 1, :], 1, 2), ALU.mult).then_inc(dve_done, done("dve", "lnx"))
                elif work == "ln3":
                    branch_rest(3)
                elif what == "qk":
                    k = int(g)
                    negated_logits(P1, k, k, lambda e: SM, lambda e: TB[:, 2 * k + e, :])
                elif what == "pv":
                    heads_rest(4 + int(g))

            def side2(l, work):
                what, _, g = work.partition(" ")
                if work[:4] == "rope":
                    u = int(work[4:])
                    dve.wait_ge(pe_done, at("pe", f"swap {u}"))
                    nc.vector.tensor_tensor(RT[:, 0], Z[:, u % 2], spread(ROPE[:, 0, :], 1, 2), ALU.mult)
                    nc.vector.tensor_tensor(RT[:, 1], ps[:, 4, :].rearrange("p (a t) -> p a t", a=2), spread(ROPE[:, 1, :], 1, 2), ALU.mult)\
                        .then_inc(dve_done, done("dve", f"parts {u}"))
                    mine(f"parts {u}")
                    if u == KV_U:
                        nc.vector.tensor_tensor(KVC[0:64, 0:T], RT[0:64, 0, 0, :], RT[0:64, 1, 0, :], ALU.add)
                        nc.vector.tensor_copy(KVC[64:128, 0:T], Z[64:128, u % 2, 0, :])
                        ins = nc.vector.tensor_tensor(KSW, RT[:, 0, 1, :], RT[:, 1, 1, :], ALU.add)
                    else:
                        dst = NQ if u == NQ_U else DQK[:, 2 * (u - DQK_U):2 * (u - DQK_U) + 2, :]
                        ins = nc.vector.tensor_tensor(dst, RT[:, 0], RT[:, 1], ALU.add)
                    ins.then_inc(dve_done, done("dve", f"rope {u}"))
                    mine(f"rope {u}")
                elif work == "ke":
                    dve.wait_ge(pool_done, at("pool", "pads"))
                    nc.vector.tensor_tensor(window(KE, [[16, 32], [1, 16]]), window(KVC, [[1, 32], [16, 16]]), window(vec[:, V2_PE:V2_N], [[1, 32], [0, 16]]), ALU.add)\
                        .then_inc(dve_done, done("dve", "ke"))
                    dve.wait_ge(act_done, at("act", "keh"))
                    for kv in range(2):
                        rows, cols_ = slice(64 * kv, 64 * kv + 64), slice(16 * kv, 16 * kv + 16)
                        last = nc.vector.tensor_tensor(KEL[rows, :, cols_], KE[rows].rearrange("p a t -> p (a t)").rearrange("p (j n) -> p j n", n=16),
                                                       KEH[rows, :, cols_].bitcast(F32), ALU.subtract)
                    last.then_inc(dve_done, done("dve", "kel"))
                elif work == "lf":
                    dve.wait_ge(act_done, at("act", f"ev {DVF_U}"))
                    nc.vector.tensor_tensor(LF[:, :, 0:6], FL[:, :, 0:6], spread(FB[:, 0:6], 1, 2), ALU.add).then_inc(dve_done, done("dve", "fx"))
                    dve.wait_ge(act_done, at("act", "fexp"))
                    nc.vector.tensor_scalar(LE[:, :, 0:6], LE[:, :, 0:6], 1.0, None, ALU.add).then_inc(dve_done, done("dve", "fexp1"))
                    nc.vector.tensor_scalar(FL[:, :, 0:6], LF[:, :, 0:6], 0.0, -8.0, ALU.min, ALU.mult).then_inc(dve_done, done("dve", "fmin"))
                    mine("fmin")
                    dve.wait_ge(act_done, at("act", "fln"))
                    nc.vector.scalar_tensor_tensor(out=LF[:, :, 0:6], in0=LE[:, :, 0:6], scalar=8.0, in1=FL[:, :, 0:6], op0=ALU.mult, op1=ALU.add)\
                        .then_inc(dve_done, done("dve", "lf"))
                    mine("lf")
                    for h in range(6):
                        last = nc.vector.tensor_copy(LFB[:, h], spread(LF[:, :, h], 2, P))
                    last.then_inc(dve_done, done("dve", "lfb"))
                elif work == "cqk":
                    dve.wait_ge(pe_done, at("pe", "cqk"))
                    for e in range(2):
                        last = nc.vector.tensor_tensor(window(PC[:, 4 * e, :], [[32, 2], [16, 2], [1, 16]]), window(ps[:, 3 + e, 384:448], [[32, 2], [16, 2], [1, 16]]),
                                                       window(CMK[:, 0, :], [[0, 2], [16, 2], [1, 16]]), ALU.add)
                    last.then_inc(dve_done, done("dve", "cadd"))
                    mine("cadd")
                    nc.vector.tensor_reduce(CN[:, 0, :], PC, AX.X, ALU.max).then_inc(dve_done, done("dve", "cmax"))
                    mine("cmax")
                    nc.vector.tensor_tensor(PC, PC, spread(CN[:, 0, :], 2, 16), ALU.subtract).then_inc(dve_done, done("dve", "cnm"))
                    dve.wait_ge(act_done, at("act", "cexp"))
                    for e in range(2):
                        last = nc.vector.tensor_tensor(window(PC[:, 4 * e, :], [[32, 2], [16, 2], [1, 16]]), window(PC[:, 4 * e, :], [[32, 2], [16, 2], [1, 16]]),
                                                       window(CMB[:, 0, :], [[0, 2], [16, 2], [1, 16]]), ALU.mult)
                    last.then_inc(dve_done, done("dve", "ckeep"))
                    mine("ckeep")
                    nc.vector.tensor_reduce(CN[:, 1, :], PC, AX.X, ALU.add).then_inc(dve_done, done("dve", "csum"))
                    mine("csum")
                    nc.vector.tensor_scalar(CN[:, 1, :], CN[:, 1, :], 1.0, None, ALU.max).then_inc(dve_done, done("dve", "cden"))
                    mine("cden")
                    nc.vector.reciprocal(CN[:, 2, :], CN[:, 1, :]).then_inc(dve_done, done("dve", "crec"))
                    mine("crec")
                    nc.vector.tensor_tensor(window(CN[:, 2, :], [[4, 2], [2, 2], [1, 2]]), window(CN[:, 2, :], [[4, 2], [2, 2], [1, 2]]),
                                            window(GT[:, 0, :], [[3, 2], [6, 2], [12, 2]]), ALU.mult).then_inc(dve_done, done("dve", "cfac"))
                    mine("cfac")
                    nc.vector.tensor_tensor(PC, PC, spread(CN[:, 2, :], 2, 16), ALU.mult).then_inc(dve_done, done("dve", "pc"))
                elif what == "qk":
                    k = GROUPS2.index(g)
                    j = int(g[1])
                    if g[0] == "f":
                        if j == 0:
                            dve.wait_ge(act_done, at("act", "cs"))
                        for e in range(2):
                            for t, (o, w) in enumerate(SPAN):
                                h = 2 * j + e
                                last = nc.vector.scalar_tensor_tensor(out=FM[:, e, o:o + w], in0=CS[:, h, 0:w], scalar=CT[:, t, h:h + 1],
                                                                      in1=causal[:, o:o + w], op0=ALU.subtract, op1=ALU.add)
                        last.then_inc(dve_done, done("dve", f"decay {g}"))
                        mine(f"decay {g}")
                    masks = {"d": lambda e: DM[:, j, :], "s": lambda e: causal, "w": lambda e: causal, "f": lambda e: FM[:, e, :]}[g[0]]
                    negated_logits(P2, k, k % 3, masks)
                elif what == "pv" and g in CHUNK2:
                    heads_rest(CHUNK2[g])

            def factors(block, works):
                for work in works:
                    if work[:2] != "qk":
                        continue
                    settle()
                    if block == 1:
                        factor(int(work[3:]))
                        continue
                    g = work[3:]
                    k, j = GROUPS2.index(g), int(g[1])
                    if g[0] in "sw":
                        factor(k, window(GT[:, 0, 6 * j + "sw".index(g[0]) + 1:], [[3, 2], [12, 2]]))
                    elif g[0] == "f":
                        factor(k)
                    elif g == "d2":
                        nm, den = NM[:, 0:3, :], DEN[:, 0:3, :]
                        mine("nm 2")
                        nc.vector.tensor_tensor(D4[:, 0, :], NM[:, 0, :], NM[:, 1, :], ALU.min).then_inc(dve_done, done("dve", "dmin0"))
                        mine("dmin0")
                        nc.vector.tensor_tensor(D4[:, 0, :], D4[:, 0, :], NM[:, 2, :], ALU.min).then_inc(dve_done, done("dve", "dmin"))
                        mine("dmin")
                        de = window(DE[:, 0, :], [[4, 3], [1, 4]])
                        nc.vector.tensor_tensor(de, spread(D4[:, 0, :], 1, 3), nm, ALU.subtract).then_inc(dve_done, done("dve", "dmax"))
                        dve.wait_ge(act_done, at("act", "dexp"))
                        nc.vector.tensor_tensor(window(DE[:, 1, :], [[4, 3], [1, 4]]), de, den, ALU.mult).then_inc(dve_done, done("dve", "dprod"))
                        mine("dprod")
                        nc.vector.tensor_tensor(D4[:, 1, :], DE[:, 1, 0:4], DE[:, 1, 4:8], ALU.add).then_inc(dve_done, done("dve", "dsum0"))
                        mine("dsum0")
                        nc.vector.tensor_tensor(D4[:, 1, :], D4[:, 1, :], DE[:, 1, 8:12], ALU.add).then_inc(dve_done, done("dve", "dsum"))
                        mine("dsum")
                        nc.vector.reciprocal(D4[:, 2, :], D4[:, 1, :]).then_inc(dve_done, done("dve", "drec"))
                        mine("drec")
                        for n in range(3):
                            nc.vector.tensor_tensor(FAC[:, n, :], DE[:, 0, 4 * n:4 * n + 4], D4[:, 2, :], ALU.mult)\
                                .then_inc(dve_done, done("dve", f"factor {n}"))

            def gated(gates, n, last, sum_before):
                def rest(b):
                    dve.wait_ge(act_done, at("act", f"yh {b}"))
                    nc.vector.tensor_tensor(NL[:, 2 * b:2 * b + 2, :], T8[:, 2 * b:2 * b + 2, :], NH[:, 2 * b:2 * b + 2, :].bitcast(F32),
                                            ALU.subtract).then_inc(dve_done, done("dve", f"yl {b}"))

                for b in range(4):
                    dve.wait_ge(pe_done, at("pe", f"br {n} {b}"))
                    v = gates[:, 2 * b:2 * b + 2, :].rearrange("p a t -> p (a t)")
                    nc.vector.tensor_tensor(v, v, ps[:, 4 * (1 - n % 2) + b, :], ALU.mult).then_inc(dve_done, done("dve", f"gated {n}" if b == 3 else f"gated {n} {b}"))
                    if last:
                        mine(f"gated {n}" if b == 3 else f"gated {n} {b}")
                        dve.wait_ge(pool_done, at("pool", f"{sum_before} {b}"))
                        y = T8[:, 2 * b:2 * b + 2, :]
                        nc.vector.tensor_tensor(y, y, gates[:, 2 * b:2 * b + 2, :], ALU.add).then_inc(dve_done, done("dve", f"y {b}"))
                        if b:
                            rest(b - 1)
                        if b == 3:
                            rest(3)


            m.section = "setup"
            nc.vector.memset(zero[:, :], 0.0).then_inc(lo_ready, 3)
            nc.vector.memset(tick[:, 1:2], 0.0).then_inc(ada_sum[0], 1)
            nc.vector.memset(tick[:, 2:3], 0.0).then_inc(ada_sum[1], 1)
            nc.vector.memset(tick[:, 3:4], 0.0).then_inc(ada_out, 1)
            mean_square("next")
            dve.wait_ge(act_done, at("act", "TB"))
            for block in (1, 2):
                m.section = f"block{block}"
                with dve.Fori(0, DEPTH) as l:
                    m.layer = l
                    split_lo(block, l, 0, 0)
                    dve.wait_ge(act_done, at("act", "vec"))
                    if block == 1:
                        for row in (V1_POST1, V1_POST2):
                            ins = nc.vector.tensor_scalar(vec[:, row:row + 8], vec[:, row:row + 8], 0.5, None, ALU.mult)
                        ins.then_inc(dve_done, done("dve", "gains"))
                        mine("gains")
                        pres = [vec[:, r:r + 8] for r in (V1_PRE1, V1_PREM, V1_PRE2)]
                        posts = [vec[:, r:r + 8] for r in (V1_POST1, V1_POSTM, V1_POST2)]
                        shifts = (None, None, None)
                    else:
                        nc.vector.tensor_tensor(modl, mods.rearrange("p a b -> p (a b)")[:, bass.ds(72 * l, 72)], vec[:, V2_B:V2_PE], ALU.add)\
                            .then_inc(dve_done, done("dve", "modl"))
                        mine("modl")
                        for k in range(3):
                            nc.vector.scalar_tensor_tensor(out=gains[:, 8 * k:8 * k + 8], in0=modl[:, 24 * k + 8:24 * k + 16], scalar=1.0,
                                                           in1=vec[:, V2_G + 8 * k:V2_G + 8 * k + 8], op0=ALU.add, op1=ALU.mult)
                            ins = nc.vector.tensor_scalar(gains[:, 24 + 8 * k:32 + 8 * k], modl[:, 24 * k + 16:24 * k + 24],
                                                          1.0 if k == 1 else 0.5, None, ALU.mult)
                        ins.then_inc(dve_done, done("dve", "gains"))
                        mine("gains")
                        pres = [gains[:, 8 * k:8 * k + 8] for k in range(3)]
                        posts = [gains[:, 24 + 8 * k:32 + 8 * k] for k in range(3)]
                        shifts = (0, 24, 48)
                    F = ((block - 1) * DEPTH + l) * 2
                    pre("pre1", pres[0], shifts[0])
                    split_lo(block, l, 0, 1)
                    ffn(block, l, 0, F, False, 0)
                    if block == 1:
                        post("post1", "x1")
                    else:
                        gated_add(posts[0], "x1", l, "pre1", 10)
                    mean_square("prem")
                    pre("prem", pres[1], shifts[1])
                    for u in range(UNITS):
                        p = u + 2
                        if block == 2 and u == BR2 + 2:
                            gated(G2[:, 16:24, :], 1, False, None)
                        split_lo(block, l, 11 + p // 3, p % 3, UNITS + p)
                        factors(block, (SIDE1 if block == 1 else SIDE2).get(u - 1, ()))
                        for work in (SIDE1 if block == 1 else SIDE2).get(u, ()):
                            if work[:3] not in ("top", "tap"):
                                settle()
                            (side1 if block == 1 else side2)(l, work)
                        if block == 1 and BR1 <= u < OUT1:
                            k = u - BR1
                            gated(G[:, 8 * k:8 * k + 8, :], k, k == 3, "sum 2")
                        if block == 2 and BR2 <= u < OUT2:
                            k = u - BR2
                            if k != 1:
                                if k == 2:
                                    gated(G2[:, 8:16, :], 2, True, "sum 1")
                                else:
                                    gated(G2[:, 0:8, :], 0, False, None)
                    if block == 1:
                        post("postm", "xm")
                    else:
                        gated_add(posts[1], "xm", l, "prem", 21)
                    mean_square("pre2")
                    pre("pre2", pres[2], shifts[2])
                    ffn(block, l, 22, F + 1, True, 1)
                    if block == 1:
                        post("post2", "x2")
                    else:
                        gated_add(posts[2], "x2", l, "pre2", 32)
                    mean_square("next")
            m.section = "end"
            for c in range(C):
                ins = nc.vector.scalar_tensor_tensor(out=T8[:, c, :], in0=XT[:, c, :], scalar=vec0[:, 8 + c:9 + c], in1=rms[:, 1, :],
                                                     op0=ALU.mult, op1=ALU.mult)
                if c % 2:
                    ins.then_inc(dve_done, done("dve", f"final n{c // 2}"))

        @block_.tensor
        def _(pe):
            def take_wait():
                nc.tensor.matmul(ps[:, 3, 0:1], zero[:, 0:P], zero[:, 0:1], start=True, stop=True)

            def ready(block, l, q, s):
                pe.wait_ge(lo_ready, unit_number(block, l, 3 * q + s) + 4)

            def three(dst, wh, wl, xh, xl, start, stop, weights_still=True, skip=False):
                pairs = ((wh, xh), (wh, xl), (wl, xh)) if weights_still else ((xh, wh), (xh, wl), (xl, wh))
                for k, (a, b) in enumerate(pairs):
                    last = nc.tensor.matmul(dst, a, b, start=start and k == 0, stop=stop and k == 2, skip_group_check=skip)
                return last

            def channels(dst, s, n, a, xh=NH, xl=NL):
                for c in range(C):
                    wh, wl = (v[:, s, n * c + a:n * c + a + P] for v in (hi, lo))
                    last = three(dst, wh, wl, xh[:, c, :], xl[:, c, :], c == 0, c == C - 1)
                return last

            def tokens(dst, s, n, a, w, t):
                for c in range(C):
                    wh, wl = (v[:, s, n * c + a:n * c + a + w] for v in (hi, lo))
                    x = slice(P * t, P * t + P)
                    last = three(dst, wh, wl, NH[:, c, x], NL[:, c, x], c == 0, c == C - 1, False)
                return last

            def pre(name, order=(0, 1, 2, 3)):
                for n, b in enumerate(order):
                    pe.wait_ge(act_done, at("act", f"{name} sq{b}"))
                    for c in (2 * b, 2 * b + 1):
                        last = nc.tensor.matmul(ps[:, 3, 0:T], mean_d, T8[:, c, :], start=n == 0 and c % 2 == 0, stop=n == 3 and c % 2 == 1)
                last.then_inc(pe_done, done("pe", name + " stat"))
                if name != "next":
                    stay_warm(WARM_PRE if name[:3] == "pre" else WARM_POST)

            def stay_warm(n):
                for _ in range(n):
                    nc.tensor.matmul(ps[:, 2, :], zero[:, 0:P], zero[:, P:640], start=True, stop=True)

            def first_channels(name, dst, s):
                for c in range(C):
                    if name != "y":
                        pe.wait_ge(dve_done, at("dve", f"{name} l{c}"))
                    elif c % 2 == 0:
                        pe.wait_ge(dve_done, at("dve", f"yl {c // 2}"))
                    for h in range(2):
                        wh, wl = (v[:, s, T * c + P * h:T * c + P * h + P] for v in (hi, lo))
                        last = three(dst[:, T * h:T * h + T], wh, wl, NH[:, c, :], NL[:, c, :], c == 0 and h == 0, c == C - 1, skip=True)
                return last

            def ffn(block, l, b, F, name, half):
                for k in range(4):
                    nc.tensor.matmul(ps[:, 4 + k, :], zero[:, 0:P], zero[:, P:640], start=True, stop=False, skip_group_check=True)

                def gate_up(q, s, bank, f):
                    ready(block, l, q, s)
                    if not isinstance(f, int) or f >= 2:
                        pe.wait_ge(hidden_ready, NF * F + f - 1)
                    if isinstance(f, int) and f == 0:
                        first_channels(name, ps[:, bank, :], s).then_inc(unit_used, 1)
                        return
                    channels(ps[:, bank, 0:T], s, T, 0)
                    channels(ps[:, bank, T:2 * T], s, T, P).then_inc(unit_used, 1)

                def down(q, s, i, final):
                    ready(block, l, q, s)
                    pe.wait_ge(hidden_lo, NF * F + 2 * i + 2)
                    for n in range(2 * C):
                        k, j = (n // 2, n % 2) if final else (n % C, n // C)
                        o = 1024 * j + P * k
                        last = three(ps[:, 4 + k // 2, T * (k % 2):T * (k % 2) + T], hi[:, s, o:o + P], lo[:, s, o:o + P],
                                     BH[:, j + 2 * final, :], BL[:, j + 2 * final, :], False, final and j == 1, skip=True)
                        if final and n % 4 == 3 and n < 15:
                            last.then_inc(pe_done, done("pe", f"{name} down {n // 4}"))
                    last.then_inc(unit_used, 1)

                def body(i, ada):
                    if ada:
                        a = 18 * l + 9 * half + i - 2
                        pe.wait_ge(ada_sum[0], a + 2)
                        pe.wait_ge(ada_sum[1], a + 2)
                        for k in range(4):
                            last = nc.tensor.matmul(ps[:, 1, k:k + 1], acc_ada[:, P * k:P * k + P], tri[:, P:P + 1],
                                                    start=True, stop=True)
                        last.then_inc(ada_out, 1)
                    gate_up(b + i - 1, 2, 2, 2 * i)
                    gate_up(b + i, 0, 0, 2 * i + 1)
                    down(b + i, 1, i - 1, False)

                gate_up(b, 0, 0, 0)
                gate_up(b, 1, 1, 1)
                body(1, False)
                with pe.Fori(2, NF // 2 - 1) as i:
                    body(i, block == 1)
                body(NF // 2 - 1, block == 1)
                down(b + 10, 2, 10, True)

            def scores(g, q, k, free):
                if free is not None:
                    pe.wait_ge(*free)
                for e in range(2):
                    rows = slice(64 * e, 64 * e + 64)
                    for t, (o, w) in enumerate(SPAN):
                        last = nc.tensor.matmul(ps[:, 3 + e, o:o + w], q[rows, P * t:P * t + P], k[rows, 0:w], start=True, stop=True)
                last.then_inc(pe_done, done("pe", f"qk {g}"))

            def turned(p_tile, g, slot, free):
                pe.wait_ge(pool_done, at("pool", f"p {g}"))
                if free is not None:
                    pe.wait_ge(*free)
                for e in range(2):
                    for k in range(3):
                        last = nc.tensor.transpose(ps[:, 5 + e, P * k:P * k + P], p_tile[:, 2 * slot + e, P * k:P * k + P], ident)
                last.then_inc(pe_done, done("pe", f"tr {g}"))

            def values(g, v, first, last_one, free):
                pe.wait_ge(act_done, at("act", f"pt {g}"))
                if free is not None:
                    pe.wait_ge(*free)
                for e in range(2):
                    rows = slice(64 * e, 64 * e + 64)
                    nc.tensor.matmul(ps[rows, 7, 0:T], v(0, e), PT[:, e, 0:T], start=first, stop=False, skip_group_check=True)
                    last = nc.tensor.matmul(ps[rows, 7, P:T], v(1, e), PT[:, e, T:CAUSAL], start=False, stop=last_one, skip_group_check=True)
                last.then_inc(pe_done, done("pe", f"pv {g}"))

            def unit1(l, u):
                q, s = 11 + u // 3, u % 3
                ready(1, l, q, s)
                bank = ps[:, u % 3, :]
                if 3 <= u < BR1:
                    pe.wait_ge(act_done, at("act", f"ev {u - 3}"))
                if u in (V_GATE, V_U):
                    for t in range(2):
                        last = tokens(bank[:, T * t:T * t + T], s, T, 0, T, t)
                elif u == IDX_U:
                    channels(bank[:, 0:T], s, 260, 0)
                    channels(bank[:, T:2 * T], s, 260, P)
                    for t in range(2):
                        last = tokens(ps[:, 7, 4 * t:4 * t + 4], s, 260, T, 4, t)
                elif u == 0:
                    last = first_channels("prem", bank, s)
                elif u < BR1:
                    channels(bank[:, 0:T], s, T, 0)
                    last = channels(bank[:, T:2 * T], s, T, P)
                elif u < OUT1:
                    if u == BR1:
                        pe.wait_ge(dve_done, at("dve", "bl 5"))
                    if u == BR1 + 1:
                        pe.wait_ge(act_done, at("act", f"ev {BR1 - 1}"))
                    branch_unit(s, u - BR1, [(0, 2 * (u - BR1)), (1024, 2 * (u - BR1) + 1)], True, True).then_inc(unit_used, 1)
                    return
                else:
                    out_unit(s, u - OUT1).then_inc(unit_used, 1)
                    return
                last.then_inc(unit_used, 1)

            def branch_unit(s, n, chunks, first, final):
                base = 4 * (1 - n % 2)
                for k in range(C):
                    if k % 2 == 0 and first and n >= 2:
                        pe.wait_ge(dve_done, at("dve", f"gated {n - 2}" if k == 6 else f"gated {n - 2} {k // 2}"))
                    for j, (o, chunk) in enumerate(chunks):
                        last = three(ps[:, base + k // 2, T * (k % 2):T * (k % 2) + T], hi[:, s, o + P * k:o + P * k + P],
                                     lo[:, s, o + P * k:o + P * k + P], BH[:, chunk, :], BL[:, chunk, :],
                                     first and j == 0 and k % 2 == 0, final and j == len(chunks) - 1, skip=True)
                    if k % 2 and final:
                        done_one = last
                        if k == C - 1:
                            done_one = nc.tensor.matmul(ps[0:1, base + 3, 0:1], zero[:, 0:1], zero[:, 0:1], start=False, stop=True,
                                                        skip_group_check=True)
                        done_one.then_inc(pe_done, done("pe", f"br {n} {k // 2}"))
                return last

            def out_unit(s, j):
                if j == 0:
                    return first_channels("y", ps[:, 4, :], s)
                channels(ps[:, 4 + j, 0:T], s, T, 0)
                return channels(ps[:, 4 + j, T:2 * T], s, T, P)

            def side1(l, work):
                what, _, g = work.partition(" ")
                if work == "gm0":
                    for k in range(4):
                        last = nc.tensor.transpose(ps[:, 3, P * k:P * k + P], WS[:, k, :], ident)
                    last.then_inc(pe_done, done("pe", "wsT"))
                elif work == "gm1":
                    pe.wait_ge(dve_done, at("dve", "VN"))
                    for k in range(4):
                        for t in range(2):
                            o = T * (k // 2) + P * t
                            last = nc.tensor.matmul(ps[64 * (k % 2):64 * (k % 2) + 64, 3, o:o + P], VG[:, t, 64 * k:64 * k + 64], WST[:, k, :],
                                                    start=True, stop=True)
                    last.then_inc(pe_done, done("pe", "mixed"))
                elif work == "pool1":
                    pe.wait_ge(dve_done, at("dve", "pd"))
                    take_wait()
                    for k in range(4):
                        rows = slice(64 * (k % 2), 64 * (k % 2) + 64)
                        last = nc.tensor.matmul(ps[rows, 3, T * (k // 2):T * (k // 2) + T], PW[rows, k // 2, :], PD[rows, k // 2, :],
                                                start=True, stop=True)
                    last.then_inc(pe_done, done("pe", "pw"))
                elif what == "idx":
                    t = int(g)
                    o, w = SPAN[t]
                    pe.wait_ge(act_done, at("act", f"ev {IDX_U}" if t == 0 else "rel 0 3"))
                    for h in range(4):
                        rows = slice(32 * h, 32 * h + 32)
                        last = nc.tensor.matmul(ps[:, 3 + h, 0:w], QKI[rows, 0, P * t:P * t + P], QKI[rows, 1, 0:w], start=True, stop=True,
                                                tile_position=(32 * h, 0))
                    last.then_inc(pe_done, done("pe", work))
                elif work == "ln1":
                    pe.wait_ge(dve_done, at("dve", "conv"))
                    for c in range(2):
                        last = nc.tensor.matmul(ps[:, 7, 0:T], mean_w, ACC[:, c, :], start=c == 0, stop=c == 1)
                    last.then_inc(pe_done, done("pe", "lnmean"))
                elif work == "ln2":
                    pe.wait_ge(act_done, at("act", "xcsq"))
                    for c in range(2):
                        last = nc.tensor.matmul(ps[:, 7, T:2 * T], mean_w, BT[:, c, :], start=c == 0, stop=c == 1)
                    last.then_inc(pe_done, done("pe", "ln stat"))
                elif what == "qk":
                    k = int(g)
                    scores(k, QT[:, k, :], KT[:, k, :], (dve_done, at("dve", f"nm {k - 1}")) if k else (act_done, at("act", "rel 1 3")))
                elif what == "tr":
                    k = int(g)
                    turned(P1, k, k, (act_done, at("act", f"pt {k - 1}")) if k else None)
                elif what == "pv":
                    k = int(g)
                    values(k, lambda t, e: VT[:, t, 64 * (2 * k + e):64 * (2 * k + e) + 64], True, True,
                           (dve_done, at("dve", "bl 4" if k else "lnx")))

            def unit2(l, u):
                q, s = 11 + u // 3, u % 3
                ready(2, l, q, s)
                bank = ps[:, u % 3, :]
                if 3 <= u < BR2:
                    before = u - 2 if u == W1_U else u - 3
                    pe.wait_ge(act_done, at("act", "hid" if before in (W1_U, W1_U + 1) else f"ev {before}"))
                if u == VG_U:
                    for t in range(2):
                        last = tokens(bank[:, 140 * t:140 * t + 140], s, 140, 0, 140, t)
                elif u in (DV_U, FV_U):
                    for t in range(2):
                        last = tokens(bank[:, T * t:T * t + T], s, T, 0, T, t)
                elif u == DVF_U:
                    tokens(bank[:, 0:262], s, 262, 0, 262, 0)
                    last = tokens(ps[:, 6, 0:262], s, 262, 0, 262, 1)
                elif u in (W1_U, W1_U + 1):
                    if u == W1_U:
                        pe.wait_ge(dve_done, at("dve", "kel"))
                    for j in range(16):
                        k = 16 * (u - W1_U) + j
                        last = three(ps[0:32, 0, 0:P], hi[:, s, P * j:P * j + P], lo[:, s, P * j:P * j + P], KEH[:, k, :], KEL[:, k, :],
                                     k == 0, k == 31, False, skip=True)
                elif u == 0:
                    last = first_channels("prem", bank, s)
                elif u < BR2:
                    channels(bank[:, 0:T], s, T, 0)
                    last = channels(bank[:, T:2 * T], s, T, P)
                elif u == BR2:
                    pe.wait_ge(dve_done, at("dve", "bl 5"))
                    last = branch_unit(s, 0, [(0, 0), (1024, 1)], True, True)
                elif u == BR2 + 1:
                    pe.wait_ge(act_done, at("act", f"ev {BR2 - 1}"))
                    last = branch_unit(s, 1, [(0, 3), (1024, 4)], True, False)
                elif u == BR2 + 2:
                    branch_unit(s, 1, [(0, 5)], False, True)
                    last = branch_unit(s, 2, [(1024, 2)], True, True)
                else:
                    last = out_unit(s, u - OUT2)
                last.then_inc(unit_used, 1)

            def side2(l, work):
                what, _, g = work.partition(" ")
                if work[:4] == "rope":
                    u = int(work[4:])
                    pe.wait_ge(act_done, at("act", f"ev {u}"))
                    if u:
                        pe.wait_ge(dve_done, at("dve", f"rope {ROPED[ROPED.index(u) - 1]}"))
                    for k in range(2):
                        last = nc.tensor.matmul(ps[:, 4, T * k:T * k + T], SWAP, Z[:, u % 2, k, :], start=True, stop=True)
                    last.then_inc(pe_done, done("pe", f"swap {u}"))
                elif work == "dup":
                    pe.wait_ge(dve_done, at("dve", "rope 1"))
                    for k in range(2):
                        last = nc.tensor.matmul(ps[:, 3, T * k:T * k + T], DUP[:, k, :], KSW, start=True, stop=True)
                    last.then_inc(pe_done, done("pe", "dup"))
                elif work == "fox":
                    pe.wait_ge(dve_done, at("dve", "lfb"))
                    pe.wait_ge(act_done, at("act", "exp 2"))
                    ones, up = tri[:, P:T], tri[:, 0:P]
                    nc.tensor.matmul(ps[:, 7, 0:6], up, LF[:, 0, 0:6], start=True, stop=True)
                    nc.tensor.matmul(ps[:, 7, 8:14], ones, LF[:, 0, 0:6], start=True, stop=False)
                    nc.tensor.matmul(ps[:, 7, 8:14], up, LF[:, 1, 0:6], start=False, stop=True)
                    for h in range(6):
                        b, o = ((3, 0), (3, T), (4, 0), (4, T), (5, 0), (6, 0))[h]
                        nc.tensor.matmul(ps[:, b, o:o + T], LFB[:, h, 0, :], tri, start=True, stop=False)
                        last = nc.tensor.matmul(ps[:, b, o + P:o + T], LFB[:, h, 1, :], up, start=False, stop=True)
                    last.then_inc(pe_done, done("pe", "fox"))
                elif work == "hidt":
                    pe.wait_ge(act_done, at("act", "hid"))
                    take_wait()
                    nc.tensor.transpose(ps[:, 3, 448:480], HT[0:32, :], ident[0:32, 0:32]).then_inc(pe_done, done("pe", "hidt"))
                elif work == "w2":
                    pe.wait_ge(act_done, at("act", "hidt"))
                    nc.tensor.matmul(ps[:, 3, 384:400], W2[:, 0:P], HID[:, 0, :], start=True, stop=True)
                    nc.tensor.matmul(ps[0:16, 4, 384:448], HID[:, 1, :], W2[:, P:192], start=True, stop=True).then_inc(pe_done, done("pe", "w2"))
                elif work == "cqk":
                    pe.wait_ge(act_done, at("act", "w2"))
                    for e in range(2):
                        rows = slice(64 * e, 64 * e + 64)
                        for j in range(2):
                            for t in range(2):
                                o = 384 + 16 * (2 * j + t)
                                last = nc.tensor.matmul(ps[:, 3 + e, o:o + 16], NQ[rows, j, P * t:P * t + P], KC2[rows, :], start=True, stop=True)
                    last.then_inc(pe_done, done("pe", "cqk"))
                elif work == "ctr":
                    pe.wait_ge(dve_done, at("dve", "pc"))
                    pe.wait_ge(act_done, at("act", "pt 2"))
                    for e in range(2):
                        for j in range(2):
                            for t in range(2):
                                o = T * j + P * t
                                last = nc.tensor.matmul(ps[0:16, 5 + e, o:o + P], PC[:, 4 * e + 2 * j + t, :], ident, start=True, stop=True)
                    last.then_inc(pe_done, done("pe", "ctr"))
                elif what == "cpv":
                    j = int(g)
                    pe.wait_ge(act_done, at("act", "ptc"))
                    pe.wait_ge(dve_done, at("dve", "bl 2" if j == 0 else "bl 0"))
                    for e in range(2):
                        nc.tensor.matmul(ps[64 * e:64 * e + 64, 7, 0:T], VC2[0:16, :], PTC[0:16, 2 * e + j, :], start=True, stop=False,
                                         skip_group_check=True)
                elif what == "qk":
                    k, j = GROUPS2.index(g), int(g[1])
                    qk = {"d": lambda: (DQK[:, j, :], DQK[:, 3 + j, :]), "s": lambda: (NQ[:, j, :], KSD[:, 0, :]),
                          "w": lambda: (NQ[:, j, :], KSD[:, 1, :]), "f": lambda: (FQK[:, j, :], FQK[:, 3 + j, :])}[g[0]]()
                    free = {"d0": (dve_done, at("dve", "rope 5")), "s0": (dve_done, at("dve", "pc"))}.get(g)
                    scores(k, *qk, free or (dve_done, at("dve", f"nm {k - 1}")))
                elif what == "tr":
                    k = GROUPS2.index(g)
                    free = {"d0": (act_done, at("act", "cs")), "s0": (act_done, at("act", "ptc"))}.get(g)
                    turned(P2, k, k % 3, free or (act_done, at("act", f"pt {k - 1}")))
                elif what == "pv":
                    k, j = GROUPS2.index(g), int(g[1])
                    v = {"d": lambda t, e: DV[:, t, P * j + 64 * e:P * j + 64 * e + 64], "s": lambda t, e: VSW[:, t, 0:64],
                         "w": lambda t, e: VSW[:, t, 64:128], "f": lambda t, e: FV[:, t, P * j + 64 * e:P * j + 64 * e + 64]}[g[0]]
                    before = {"d0": (act_done, at("act", "cs")), "f0": (dve_done, at("dve", "bl 1")), "f1": (dve_done, at("dve", "bl 3")),
                              "f2": (dve_done, at("dve", "bl 4"))}.get(g)
                    values(k, v, g in ("d0", "f0", "f1", "f2"), g in CHUNK2, before)

            m.section = "setup"
            pe.wait_ge(const_in, 16 * 10)
            nc.tensor.transpose(ps[:, 0, 0:16], vrow[0:16, :], ident[0:16, 0:16]).then_inc(pe_done, done("pe", "vec0"))
            nc.tensor.matmul(ps[0:4, 1, :], WI.rearrange("p a b -> p (a b)")[0:32, 0:4], onehot.rearrange("p a b -> p (a b)")[0:32],
                             start=True, stop=True).then_inc(pe_done, done("pe", "bias rows"))
            x_in = T8[:, :, :].rearrange("p (a b) t -> p a (b t)", a=2)
            for c in range(C):
                for t in range(2):
                    o = T * (c % 2) + P * t
                    last = nc.tensor.transpose(ps[:, 4 + c // 2, o:o + P], x_in[:, t, P * c:P * c + P], ident)
            last.then_inc(pe_done, done("pe", "xT"))
            pe.wait_ge(pool_done, at("pool", "mean_w"))
            pe.wait_ge(lo_ready, 3)
            pre("next")
            pe.wait_ge(const_in, 16 * 13)
            pe.wait_ge(dve_done, at("dve", "next rstd"))
            for h in range(4):
                for t, (o, w) in enumerate(SPAN):
                    last = nc.tensor.matmul(ps[:, h, o:o + w], flip, brev[:, 2 * h + t, 0:w], start=True, stop=True)
            last.then_inc(pe_done, done("pe", "TB"))
            pe.wait_ge(pool_done, at("pool", "mean_w"))
            pe.wait_ge(act_done, at("act", "TB"))
            nc.tensor.matmul(ps[0:1, 0, 0:1], zero[:, 0:1], zero[:, 0:1], start=True, stop=True).then_inc(unit_used, 3)
            for block in (1, 2):
                m.section = f"block{block}"
                with pe.Fori(0, DEPTH) as l:
                    m.layer = l
                    pe.wait_ge(rows_in, rows_target(block, l))
                    n = V1_N if block == 1 else V2_N
                    nc.tensor.transpose(ps[:, 1, 0:n], vrow[0:n, :], ident[0:n, 0:n]).then_inc(pe_done, done("pe", "vec"))
                    stay_warm(WARM_PRE)
                    pe.wait_ge(act_done, at("act", "vec"))
                    F = ((block - 1) * DEPTH + l) * 2
                    ffn(block, l, 0, F, "pre1", 0)
                    if block == 1:
                        pre("post1")
                    pe.wait_ge(small_in, small_target(block, l))
                    pre("prem", UPDATES[block])
                    for u in range(UNITS):
                        (unit1 if block == 1 else unit2)(l, u)
                        for work in (SIDE1 if block == 1 else SIDE2).get(u, ()):
                            (side1 if block == 1 else side2)(l, work)
                    if block == 1:
                        pre("postm")
                    pre("pre2", UPDATES[block])
                    ffn(block, l, 22, F + 1, "pre2", 1)
                    if block == 1:
                        pre("post2")
                    pre("next", UPDATES[block])
            m.section = "end"
            for j in range(4):
                pe.wait_ge(dve_done, at("dve", f"final n{j}"))
                for c in (2 * j, 2 * j + 1):
                    for t in range(2):
                        o = P * (c % 2)
                        last = nc.tensor.transpose(ps[:, 4 * t + j, o:o + P], T8[:, c, P * t:P * t + P], ident)
                last.then_inc(pe_done, done("pe", f"out {j}"))

    return m


def constants():
    f = np.float32
    k = np.arange(P)
    t = np.arange(T)
    c = {"ident": np.eye(P, dtype=f), "flip": np.eye(P, dtype=f)[::-1].copy()}
    c["tri"] = np.concatenate([(k[:, None] <= k[None]).astype(f), np.ones((P, P), f)], 1)

    def causal_tiles(seen):
        return np.concatenate([np.where(seen(P * i + k[:, None], np.arange(w)[None]), 0, NEG).astype(f) for i, (_, w) in enumerate(SPAN)], 1)

    c["causal"] = causal_tiles(lambda t, s: s <= t)
    c["dilated"] = np.concatenate([causal_tiles(lambda t, s, w=w, d=d: (s <= t) & ((t - s) % d == 0) & (t - s <= w))
                                   for w, d in ((128, 1), (512, 4), (2048, 16))], 1)
    windows = np.array([2, 4, 8, 16]).reshape(2, 2)
    c["rcount"] = np.concatenate([1 / np.minimum(t[None] + 1, windows[h][k // 64][:, None]) for h in range(2)], 1).astype(f)
    n = np.arange(T)
    large = 16 + (np.log(np.maximum(n, 1).astype(f) / f(16)) / f(np.log(128 / 16)) * f(16)).astype(np.int32)
    bucket = np.where(n < 16, n, np.minimum(large, 31))
    onehot = np.zeros((32, 512), f)
    onehot[bucket, T - 1 - n] = 1
    c["onehot"] = onehot
    inv = f(500000.0) ** (-np.arange(0, 16, 2, dtype=f) / f(16))
    ang = (t.astype(f)[:, None] * inv[None]).T
    cos, sin = np.ones((P, T), f), np.zeros((P, T), f)
    swap = np.zeros((P, P), f)
    for base in (0, 64):
        for r in range(8):
            cos[base + r] = cos[base + 8 + r] = np.cos(ang[r])
            sin[base + r] = sin[base + 8 + r] = np.sin(ang[r])
            swap[base + 8 + r, base + r] = -1
            swap[base + r, base + 8 + r] = 1
    c["rope"], c["swap"] = np.concatenate([cos, sin], 1), swap
    half = np.eye(64, dtype=f)
    z = np.zeros((64, P), f)
    both = np.concatenate([half, half], 1)
    c["dup"] = np.concatenate([np.concatenate([both, z]), np.concatenate([z, both])], 1)
    end = 16 * np.arange(16) + 31
    keep = np.concatenate([(end[None] <= P * i + k[:, None]) & (np.arange(16)[None] < 15) for i in range(2)], 1)
    c["cmp_keep"], c["cmp_add"] = keep.astype(f), np.where(keep, 0, NEG).astype(f)
    return c


_INS = ['x', 'ffn1_pre_g', 'ffn1_post_g', 'ffn1_w_gu', 'ffn1_w_down', 'mix_pre_g', 'mix_post_g', 'w_in', 'gm_v_g', 'gm_ws', 'gm_b',
        'pool_w', 'pool_scale', 'conv_dw', 'conv_b', 'conv_ln_g', 'conv_ln_b', 'w_branch', 'w_out', 'ffn2_pre_g', 'ffn2_post_g',
        'ffn2_w_gu', 'ffn2_w_down', 'rel_bias', 'c_2', 'ada_w_2', 'ada_b_2', 'norm_g_2', 'final_norm_g_2', 'ffn_w_in_2', 'ffn_w_out_2',
        'mix_w_in_2', 'nsa_cmp_pe_2', 'nsa_cmp_w1_2', 'nsa_cmp_w2_2', 'fox_f_bias_2', 'br_w_nsa_2', 'br_w_dil_2', 'br_w_fox_2',
        'mix_w_out_2']


def build(nc, shapes, known):
    ins = {n: nc.dram_tensor(f"in_{n}", s, mybir.dt.float32, kind="ExternalInput").ap() for n, s in shapes.items()}
    out = nc.dram_tensor("out", (1, T, D), mybir.dt.float32, kind="ExternalOutput").ap()
    return program(nc, known, ins, out)


def kernel(**inputs):
    import concourse.bacc as _bacc
    from concourse.bass_utils import run_bass_kernel_spmd as _run

    arrays = {n: np.ascontiguousarray(inputs[n]) for n in _INS}
    arrays.update(constants())
    shapes = {n: a.shape for n, a in arrays.items()}
    counts = build(_bacc.Bacc("TRN2", target_bir_lowering=False, num_devices=1), shapes, None).order
    nc = _bacc.Bacc("TRN2", target_bir_lowering=False, num_devices=1)
    build(nc, shapes, counts)
    r = _run(nc, [{f"in_{n}": a for n, a in arrays.items()}], core_ids=[0])
    return r.results[0]["out"]
```
